# Optimizing a Trainium2 kernel written in Bass

```python
import math
import jax, jax.numpy as jnp
from jax import lax
import numpy as np

D_MODEL = 1024
BATCH = 1
SEQ = 1024
DEPTH = 1

CHUNK = 64
N_META = 16

N_HEADS = 8
HEAD_DIM = 64
V_HEAD_DIM = 2 * HEAD_DIM
QK_COLS = N_HEADS * 2 * HEAD_DIM
ATTN_WIDTH = N_HEADS * V_HEAD_DIM
ROPE_DIMS = HEAD_DIM // 4
ROPE_THETA = 500000.0
Q_BLOCK = 128
NEG_INF = -1e30

CONV_WIDTH = D_MODEL
CONV_K = 31

SPLIT_IDX = [QK_COLS, 2 * QK_COLS, 2 * QK_COLS + ATTN_WIDTH,
             2 * QK_COLS + ATTN_WIDTH + 2 * CONV_WIDTH]
IN_COLS = 2 * QK_COLS + ATTN_WIDTH + 2 * CONV_WIDTH + 2 * D_MODEL

PEER_HEADS = 8
PEER_KEYS = 128
PEER_N = PEER_KEYS * PEER_KEYS
PEER_DKEY = 256
PEER_TOPK = 16
PEER_TOKEN_BLOCK = 128

LN_EPS = 1e-5
DEEPNORM_ALPHA = (2 * DEPTH) ** 0.25
DEEPNORM_BETA = (8 * DEPTH) ** -0.25

kernel_name = "hybrid_diffattn_conformer_peer_block"

def layer_norm(x, g, b):
    xf = x.astype(jnp.float32)
    mu = jnp.mean(xf, axis=-1, keepdims=True)
    var = jnp.mean(jnp.square(xf - mu), axis=-1, keepdims=True)
    y = (xf - mu) * lax.rsqrt(var + LN_EPS)
    return (y * g.astype(jnp.float32) + b.astype(jnp.float32)).astype(x.dtype)

def chunk_ids(L):
    pos = np.arange(L)
    return np.where(pos < N_META, 0, (pos - N_META) // CHUNK + 1)

def chunk_end(p, L):
    if p < N_META:
        return N_META
    c = (p - N_META) // CHUNK + 1
    return min(L, N_META + CHUNK * c)

def rope_tables(L, dtype):
    pos = jnp.arange(L, dtype=jnp.float32)
    inv = ROPE_THETA ** (-jnp.arange(0, ROPE_DIMS, 2, dtype=jnp.float32) / ROPE_DIMS)
    ang = (pos[:, None] * inv[None, :])[None, :, None, None, :]
    return jnp.cos(ang).astype(dtype), jnp.sin(ang).astype(dtype)

def apply_partial_rope(t, cos, sin):
    rot, rest = t[..., :ROPE_DIMS], t[..., ROPE_DIMS:]
    r1, r2 = rot[..., :ROPE_DIMS // 2], rot[..., ROPE_DIMS // 2:]
    rot = jnp.concatenate([r1 * cos - r2 * sin, r2 * cos + r1 * sin], axis=-1)
    return jnp.concatenate([rot, rest], axis=-1)

def diff_attention(q, k, v, lam):
    L = q.shape[1]
    cid = chunk_ids(L)
    scale = HEAD_DIM ** -0.5
    outs = []
    for qs in range(0, L, Q_BLOCK):
        qe = min(qs + Q_BLOCK, L)
        kend = chunk_end(qe - 1, L)
        s = jnp.einsum('bqhmd,bkhmd->bhmqk', q[:, qs:qe], k[:, :kend]).astype(jnp.float32) * scale
        mask = jnp.asarray(cid[None, :kend] <= cid[qs:qe, None])
        p = jax.nn.softmax(jnp.where(mask, s, NEG_INF), axis=-1)
        w = p[:, :, 0] - lam * p[:, :, 1]
        outs.append(jnp.einsum('bhqk,bkhe->bqhe', w.astype(v.dtype), v[:, :kend]))
    return jnp.concatenate(outs, axis=1)

def conformer_conv(c, dw_kernel, dw_bias, ln_g, ln_b, w_proj, b_proj):
    a, gt = jnp.split(c, 2, axis=-1)
    u = a * jax.nn.sigmoid(gt)
    u = lax.conv_general_dilated(
        u, dw_kernel[:, None, :].astype(u.dtype), window_strides=(1,),
        padding=((CONV_K - 1, 0),), dimension_numbers=('NWC', 'WIO', 'NWC'),
        feature_group_count=CONV_WIDTH) + dw_bias
    u = jax.nn.silu(layer_norm(u, ln_g, ln_b))
    return u @ w_proj + b_proj

def peer_ffn(h, wq, subkeys, u_tab, v_tab):
    Bb, L, D = h.shape
    t = h.reshape(-1, D)
    n = t.shape[0]
    pad = (-n) % PEER_TOKEN_BLOCK
    blocks = jnp.pad(t, ((0, pad), (0, 0))).reshape(-1, PEER_TOKEN_BLOCK, D)
    K = PEER_TOPK

    def one_block(tb):
        q = (tb @ wq).reshape(PEER_TOKEN_BLOCK, PEER_HEADS, 2, PEER_DKEY // 2)
        s = jnp.einsum('thpc,hpnc->thpn', q, subkeys).astype(jnp.float32)
        sv, si = lax.top_k(s, K)
        cand = sv[:, :, 0, :, None] + sv[:, :, 1, None, :]
        cv, ci = lax.top_k(cand.reshape(PEER_TOKEN_BLOCK, PEER_HEADS, K * K), K)
        i1 = jnp.take_along_axis(si[:, :, 0], ci // K, axis=-1)
        i2 = jnp.take_along_axis(si[:, :, 1], ci % K, axis=-1)
        e = i1 * PEER_KEYS + i2
        gate = jax.nn.softmax(cv, axis=-1)
        act = jax.nn.gelu(jnp.einsum('td,thkd->thk', tb, u_tab[e]), approximate=False)
        coef = (gate * act.astype(jnp.float32)).astype(tb.dtype)
        return jnp.einsum('thk,thkd->td', coef, v_tab[e])

    out = lax.map(one_block, blocks).reshape(-1, D)[:n]
    return out.reshape(Bb, L, D)

def setup_inputs(seed: int = 0) -> dict:
    key = jax.random.key(seed)
    ks = jax.random.split(key, 28)

    def nrm(k, shape, scale):
        return jax.random.normal(k, shape, jnp.float32) * scale

    def gain(k, shape):
        return 1.0 + nrm(k, shape, 0.02)

    Dp = DEPTH
    col_scale = jnp.concatenate([
        jnp.ones((2 * QK_COLS,), jnp.float32),
        jnp.full((ATTN_WIDTH,), DEEPNORM_BETA, jnp.float32),
        jnp.ones((2 * CONV_WIDTH + 2 * D_MODEL,), jnp.float32)])
    return {
        "x": nrm(ks[0], (BATCH, SEQ, D_MODEL), 1.0),
        "meta": nrm(ks[1], (N_META, D_MODEL), 1.0),
        "ln_in_g": gain(ks[2], (D_MODEL,)),
        "ln_in_b": nrm(ks[3], (D_MODEL,), 0.02),
        "w_in": nrm(ks[4], (Dp, D_MODEL, IN_COLS), D_MODEL ** -0.5) * col_scale,
        "b_in": nrm(ks[5], (Dp, IN_COLS), 0.02),
        "lambda_q1": nrm(ks[6], (Dp, HEAD_DIM), 0.1),
        "lambda_k1": nrm(ks[7], (Dp, HEAD_DIM), 0.1),
        "lambda_q2": nrm(ks[8], (Dp, HEAD_DIM), 0.1),
        "lambda_k2": nrm(ks[9], (Dp, HEAD_DIM), 0.1),
        "subln_g": gain(ks[10], (Dp, V_HEAD_DIM)),
        "w_attn_proj": nrm(ks[11], (Dp, ATTN_WIDTH, D_MODEL), ATTN_WIDTH ** -0.5 * DEEPNORM_BETA),
        "dw_kernel": nrm(ks[12], (Dp, CONV_K, CONV_WIDTH), CONV_K ** -0.5),
        "dw_bias": nrm(ks[13], (Dp, CONV_WIDTH), 0.02),
        "conv_ln_g": gain(ks[14], (Dp, CONV_WIDTH)),
        "conv_ln_b": nrm(ks[15], (Dp, CONV_WIDTH), 0.02),
        "w_conv_proj": nrm(ks[16], (Dp, CONV_WIDTH, D_MODEL), CONV_WIDTH ** -0.5 * DEEPNORM_BETA),
        "b_conv_proj": nrm(ks[17], (Dp, D_MODEL), 0.02),
        "w_out": nrm(ks[18], (Dp, D_MODEL, D_MODEL), D_MODEL ** -0.5 * DEEPNORM_BETA),
        "b_out": nrm(ks[19], (Dp, D_MODEL), 0.02),
        "ln1_g": gain(ks[20], (Dp, D_MODEL)),
        "ln1_b": nrm(ks[21], (Dp, D_MODEL), 0.02),
        "peer_wq": nrm(ks[22], (Dp, D_MODEL, PEER_HEADS * PEER_DKEY), D_MODEL ** -0.5),
        "peer_subkeys": nrm(ks[23], (Dp, PEER_HEADS, 2, PEER_KEYS, PEER_DKEY // 2), (PEER_DKEY // 2) ** -0.5),
        "peer_u": nrm(ks[24], (Dp, PEER_N, D_MODEL), D_MODEL ** -0.5),
        "peer_v": nrm(ks[25], (Dp, PEER_N, D_MODEL), DEEPNORM_BETA * PEER_HEADS ** -0.5),
        "ln2_g": gain(ks[26], (Dp, D_MODEL)),
        "ln2_b": nrm(ks[27], (Dp, D_MODEL), 0.02),
    }

def reference(x, meta, ln_in_g, ln_in_b, w_in, b_in, lambda_q1, lambda_k1, lambda_q2,
              lambda_k2, subln_g, w_attn_proj, dw_kernel, dw_bias, conv_ln_g, conv_ln_b,
              w_conv_proj, b_conv_proj, w_out, b_out, ln1_g, ln1_b, peer_wq, peer_subkeys,
              peer_u, peer_v, ln2_g, ln2_b):
    B = x.shape[0]
    h = jnp.concatenate(
        [jnp.broadcast_to(meta[None].astype(x.dtype), (B, N_META, D_MODEL)), x], axis=1)
    h = layer_norm(h, ln_in_g, ln_in_b)
    L = h.shape[1]
    cos, sin = rope_tables(L, h.dtype)

    for l in range(DEPTH):
        lam_init = 0.8 - 0.6 * math.exp(-0.3 * l)
        proj = h @ w_in[l] + b_in[l]
        q, k, v, c, g = jnp.split(proj, SPLIT_IDX, axis=-1)
        q = apply_partial_rope(q.reshape(B, L, N_HEADS, 2, HEAD_DIM), cos, sin)
        k = apply_partial_rope(k.reshape(B, L, N_HEADS, 2, HEAD_DIM), cos, sin)
        v = v.reshape(B, L, N_HEADS, V_HEAD_DIM)
        lam = (jnp.exp(jnp.sum(lambda_q1[l].astype(jnp.float32) * lambda_k1[l].astype(jnp.float32)))
               - jnp.exp(jnp.sum(lambda_q2[l].astype(jnp.float32) * lambda_k2[l].astype(jnp.float32)))
               + lam_init)
        o = diff_attention(q, k, v, lam).astype(jnp.float32)
        o = (o * lax.rsqrt(jnp.mean(jnp.square(o), axis=-1, keepdims=True) + LN_EPS)
             * subln_g[l].astype(jnp.float32) * (1.0 - lam_init)).astype(h.dtype)
        attn_d = o.reshape(B, L, ATTN_WIDTH) @ w_attn_proj[l]
        conv_d = conformer_conv(c, dw_kernel[l], dw_bias[l], conv_ln_g[l], conv_ln_b[l],
                                w_conv_proj[l], b_conv_proj[l])
        g_attn, g_conv = jnp.split(jax.nn.sigmoid(g), 2, axis=-1)
        y = (g_attn * attn_d + g_conv * conv_d) @ w_out[l] + b_out[l]
        h = layer_norm(DEEPNORM_ALPHA * h + y, ln1_g[l], ln1_b[l])
        f = peer_ffn(h, peer_wq[l], peer_subkeys[l], peer_u[l], peer_v[l])
        h = layer_norm(DEEPNORM_ALPHA * h + f, ln2_g[l], ln2_b[l])

    return h[:, N_META:]


_drawn_inputs = setup_inputs


def setup_inputs(seed=0):
    import zlib

    import numpy as np

    out = dict(_drawn_inputs(seed))
    spreads = {}
    factors = {'lambda_q1': 64.0,
     'lambda_k1': 4.334,
     'lambda_q2': 3.339,
     'lambda_k2': 200.0,
     'subln_g': 74.648,
     'dw_bias': 8.0,
     'conv_ln_g': 99.026,
     'conv_ln_b': 99.148,
     'b_conv_proj': 34.105,
     'b_out': 11.775,
     'ln2_g': 22.536,
     'ln2_b': 24.783}
    for name, (base, spread) in spreads.items():
        noise = np.random.default_rng([zlib.crc32(name.encode()), seed]).standard_normal(out[name].shape)
        drawn = base * np.exp(spread * noise) if base else spread * noise
        out[name] = __import__('jax').numpy.asarray(drawn.astype(out[name].dtype))
    for name, factor in factors.items():
        out[name] = (out[name] * factor).astype(out[name].dtype)
    return out
```

```python
import math
from contextlib import ExitStack

import concourse.bass as bass
from concourse import mybir

F32 = mybir.dt.float32
F32R = mybir.dt.float32r
BF16 = mybir.dt.bfloat16
U32 = mybir.dt.uint32
ACT = mybir.ActivationFunctionType
ALU = mybir.AluOpType
AX = mybir.AxisListType
ds = bass.ds

P = 128
D = 1024
KD = D // P
T = 1024
TT = T // P
M = 16
L = T + M
CHUNK = 64
HEADS = 8
HD = 64
ROT = HD // 8
TAPS = 31
PAD = TAPS - 1
K = 16
KEYS = 128
E2 = 2
STEPS = KEYS // E2
GT = 64
GROUPS = T // GT
LN_EPS = 1e-5
ALPHA = 2.0 ** 0.25
LAM_INIT = 0.8 - 0.6 * math.exp(0.0)
BANK = 512
LOWEST = -3.0e38
O_LIMIT = 1.6e18


class Chain:

    def __init__(self, eng, sem, base=0):
        self.eng, self.sem, self.base, self.n = eng, sem, base, 0

    def mark(self, ins):
        ins.then_inc(self.sem, 1)
        self.n += 1
        return self.base + self.n

    def then(self, ins, apart=False):
        self.eng.wait_ge(self.sem, self.mark(ins))
        if apart:
            self.eng.nop(nofuse=True)



class Map:

    def __init__(self, nc, at=0):
        self.nc, self.at = nc, at

    def take(self, name, shape, dt=F32):
        n = 2 if dt == BF16 else 4
        for s in shape[1:]:
            n *= s
        h = self.nc.alloc_sbuf_tensor_at(name, shape, dt, offset=self.at)
        self.at += (n + 31) // 32 * 32
        return h


def row(ap, n=P):
    return ap.rearrange("(o d) -> o d", o=1).to_broadcast([n, ap.shape[0]])


def norm_in(nc, sem, A, hT, h_dram, identity, at):
    m = Map(nc, at)
    xin = m.take("xin", [P, 2, D])
    xn = m.take("xn", [P, 2, D])
    gamma = m.take("ni_gamma", [P, D])
    beta = m.take("ni_beta", [P, D])
    stats = m.take("ni_stats", [P, 2, 6])
    mv = m.take("ni_mv", [P, 2])
    std = m.take("ni_std", [P, 2])
    with nc.psum_tensor("ni_tp", [P, 4, BANK], F32) as tp:
        const_in = sem("ni_const_in")
        x_in = [sem("ni_x_in0"), sem("ni_x_in1")]
        x_used = sem("ni_x_used")
        chain = sem("ni_chain")
        var_ready = sem("ni_var")
        std_ready = sem("ni_std_s")
        xn_ready = sem("ni_xn")
        tr_done = sem("ni_tr")
        ht_done = sem("ni_ht")
        h_out = [sem("ni_h_out0"), sem("ni_h_out1")]
        x_t = A["x"].rearrange("b (t p) d -> (b t) p d", p=P)
        PER = 3

        with nc.Block() as block:
            @block.sync
            def _(sp):
                sp.dma_start(gamma[:, :], row(A["ln_in_g"])).then_inc(const_in, 16)
                sp.dma_start(beta[:, :], row(A["ln_in_b"])).then_inc(const_in, 16)
                sp.dma_start(identity[:, :], A["identity"]).then_inc(const_in, 16)
                with sp.Fori(0, TT // 2) as i:
                    for u in range(2):
                        sp.wait_ge(x_used, i * 2 + u)
                        sp.dma_start(xin[:, u, :], x_t[ds(i * 2 + u, 1)].rearrange("o p d -> (o p) d")
                                     ).then_inc(x_in[u], 16)
                sp.wait_ge(x_used, TT)
                sp.dma_start(xin[0:M, 0, :], A["meta"]).then_inc(x_in[0], 16)

            @block.gpsimd
            def _(pool):
                with pool.Fori(0, TT // 2) as i:
                    for u in range(2):
                        pool.wait_ge(xn_ready, i * 2 + u + 1)
                        pool.dma_start(h_dram[ds(i * 2 + u, 1)].rearrange("o p d -> (o p) d"), xn[:, u, :]
                                       ).then_inc(h_out[u], 16)
                for u in range(2):
                    pool.wait_ge(h_out[u], 16 * TT // 2)

            def normalise(dve, t, u, i, n):
                c = Chain(dve, chain, t * PER)
                dve.wait_ge(x_in[u], i * 16 + 16)
                nc.vector.bn_stats(stats[0:n, 0, :], xin[0:n, u, 0:BANK])
                c.then(nc.vector.bn_stats(stats[0:n, 1, :], xin[0:n, u, BANK:D]), apart=True)
                c.then(nc.vector.bn_aggr(mv[0:n, :], stats[0:n, :, :].rearrange("p a b -> p (a b)")))
                nc.vector.tensor_scalar(std[0:n, 0:1], mv[0:n, 1:2], LN_EPS, None, ALU.add).then_inc(var_ready, 1)
                dve.wait_ge(std_ready, t + 1)
                c.then(nc.vector.reciprocal(std[0:n, 1:2], std[0:n, 1:2]))
                dve.wait_ge(ht_done, t * 2 + 2)
                dve.wait_ge(h_out[u], i * 16)
                nc.vector.tensor_scalar(xn[0:n, u, :], xin[0:n, u, :], mv[0:n, 0:1], std[0:n, 1:2],
                                        ALU.subtract, ALU.mult).then_inc(x_used, 1)
                dve.wait_ge(x_used, t + 2)

            @block.vector
            def _(dve):
                nc.vector.memset(stats[:, :, :], 0.0).then_inc(x_used, 1)
                dve.wait_ge(x_used, 1)
                nc.vector.memset(mv[:, :], 0.0).then_inc(ht_done, 4)
                dve.wait_ge(ht_done, 4)
                dve.wait_ge(const_in, 48)
                gb = sem("ni_gamma_done")

                def scale_shift(t, u, n):
                    nc.vector.tensor_tensor(xn[0:n, u, :], xn[0:n, u, :], gamma[0:n, :], ALU.mult).then_inc(gb, 1)
                    dve.wait_ge(gb, t + 1)
                    nc.vector.tensor_tensor(xn[0:n, u, :], xn[0:n, u, :], beta[0:n, :], ALU.add).then_inc(xn_ready, 1)

                with dve.Fori(0, TT // 2) as i:
                    for u in range(2):
                        normalise(dve, i * 2 + u, u, i, P)
                        scale_shift(i * 2 + u, u, P)
                normalise(dve, TT, 0, TT // 2, M)
                scale_shift(TT, 0, M)

            @block.scalar
            def _(act):
                def root(t, n):
                    act.wait_ge(var_ready, t + 1)
                    nc.scalar.activation(std[0:n, 1:2], std[0:n, 0:1], ACT.Sqrt).then_inc(std_ready, 1)

                def store(t, u, n):
                    for f in range(2):
                        act.wait_ge(tr_done, t * 2 + f + 1)
                        act.nop(nofuse=True)
                        nc.scalar.activation(hT[:, 4 * f:4 * f + 4, ds(t * P, n)],
                                             tp[:, 2 * u + f, :].rearrange("p (k c) -> p k c", k=4)[:, :, 0:n],
                                             ACT.Copy).then_inc(ht_done, 1)

                root(0, P)
                with act.Fori(0, TT // 2 - 1) as i:
                    for u in range(2):
                        root(i * 2 + u + 1, P)
                        store(i * 2 + u, u, P)
                root(TT - 1, P)
                store(TT - 2, 0, P)
                root(TT, M)
                store(TT - 1, 1, P)
                store(TT, 0, M)

            @block.tensor
            def _(pe):
                def turn(t, u, n):
                    pe.wait_ge(xn_ready, t + 1)
                    for f in range(2):
                        pe.wait_ge(ht_done, t * 2 + f + 1)
                        for k in range(4):
                            ins = nc.tensor.transpose(tp[:, 2 * u + f, k * P:k * P + n],
                                                      xn[0:n, u, (4 * f + k) * P:(4 * f + k + 1) * P],
                                                      identity[0:n, 0:n])
                        ins.then_inc(tr_done, 1)

                pe.wait_ge(const_in, 48)
                with pe.Fori(0, TT // 2) as i:
                    for u in range(2):
                        turn(i * 2 + u, u, P)
                turn(TT, 0, M)


def mix(nc, sem, A, hT, identity, oall, yconv, at):
    m = Map(nc, at)
    w_head = m.take("w_head", [P, KD, 3 * P])
    w_glu = m.take("w_glu", [P, KD, 2 * P])
    b_head = m.take("b_head", [P, 3 * P])
    qkv = m.take("qkv", [P, TT + 1, 3 * P])
    qT = m.take("qT", [P, T])
    kT = m.take("kT", [P, L])
    prob = m.take("prob", [P, 2, 2, L])
    mixed = m.take("mixed", [P, L])
    second = m.take("second", [P, L])
    mixT = m.take("mixT", [P, T])
    mixTm = m.take("mixTm", [M, P])
    glu_t = m.take("glu_t", [P, L])
    glu_a = m.take("glu_a", [P, L])
    u_pad = m.take("u_pad", [P, PAD + L])
    y_sum = m.take("y_sum", [P, T])
    cos_t = m.take("cos_t", [P, TT + 1, ROT])
    sin_t = m.take("sin_t", [P, TT + 1, ROT])
    rot = m.take("rot", [P, 4, (TT + 1) * 4 * ROT])
    negmax = m.take("negmax", [P, 4])
    sums = m.take("sums", [P, 4])
    rr = m.take("rr", [P, 2])
    lamv = m.take("lamv", [P, 4, HD])
    lamp = m.take("lamp", [P, 2, HD])
    lam = m.take("lam", [P, 4])
    glu_b = m.take("glu_b", [P, 2, HEADS])
    glu_h = m.take("glu_h", [P, 2, HEADS])
    taps_w = m.take("taps_w", [P, HEADS, TAPS])
    taps_b = m.take("taps_b", [P, HEADS])

    nbatch = [(i + 4) // 4 for i in range(TT)]
    before = [sum(nbatch[:i]) + i for i in range(TT + 1)]
    NB = before[TT]
    TAPS_AT = [4, 4, 4, 4, 4, 4, 4, 2]
    DVE_PER = 1 + TAPS + 2 * TT + 3 * TT

    with nc.psum_tensor("mx_s", [P, 2, 3, BANK], F32) as S, nc.psum_tensor("mx_t", [P, BANK], F32) as TB, \
            nc.psum_tensor("mx_o", [P, BANK], F32) as OB:
        tab_in = sem("mx_tables_in")
        w_in, b_in, g_in = sem("mx_w_in"), sem("mx_b_in"), sem("mx_g_in")
        pj = sem("mx_pj")
        pj_ev = sem("mx_pj_ev")
        cv = sem("mx_cv")
        th_done = sem("mx_th")
        ga_done = sem("mx_ga")
        u_done = sem("mx_u")
        roped = sem("mx_roped")
        tq, tq_ev = sem("mx_tq"), sem("mx_tq_ev")
        s_done, mx_done, ex_done = sem("mx_s_done"), sem("mx_mx"), sem("mx_ex")
        w_done = sem("mx_w_done")
        wt, wt_ev = sem("mx_wt"), sem("mx_wt_ev")
        o_done, o_ev = sem("mx_o_done"), sem("mx_o_ev")
        chain = sem("mx_chain")
        pre = sem("mx_pre")
        lam_e = sem("mx_lam_e")
        init = sem("mx_init")

        with nc.Block() as block:
            @block.sync
            def _(sp):
                for dst, src in ((cos_t[:, :, :], A["rope_cos"]), (sin_t[:, :, :], A["rope_sin"]),
                                 (glu_b[:, :, :], A["chan"][:, 0:2, :]), (taps_b[:, :], A["chan"][:, 4, :]),
                                 (taps_w[:, :, :], A["taps"]),
                                 (lamv[:, 0, :], row(A["lambda_q1"])), (lamv[:, 1, :], row(A["lambda_k1"])),
                                 (lamv[:, 2, :], row(A["lambda_q2"])), (lamv[:, 3, :], row(A["lambda_k2"]))):
                    sp.dma_start(dst, src).then_inc(tab_in, 16)
                with sp.Fori(0, HEADS) as h:
                    sp.wait_ge(pj, h * (TT + 1))
                    sp.dma_start(w_head[:, :, :], A["w_qkv"][ds(h, 1)].rearrange("o p k c -> (o p) k c")
                                 ).then_inc(w_in, 16)
                    sp.wait_ge(pj_ev, h * (TT + 1))
                    sp.dma_start(b_head[:, :], A["b_qkv"][ds(h, 1), :].to_broadcast([P, 3 * P])).then_inc(b_in, 16)
                    sp.wait_ge(cv, h * 2)
                    sp.dma_start(w_glu[:, :, :], A["w_glu"][ds(h, 1)].rearrange("o p k c -> (o p) k c")
                                 ).then_inc(g_in, 16)

            @block.tensor
            def _(pe):
                with pe.Fori(0, HEADS) as h:
                    pe.wait_ge(w_in, h * 16 + 16)
                    pe.wait_ge(ex_done, h * 16)
                    for t in range(TT + 1):
                        n = P if t < TT else M
                        if t >= 6:
                            pe.wait_ge(pj_ev, h * (TT + 1) + t - 5)
                        for k in range(KD):
                            ins = nc.tensor.matmul(S[0:n, t % 6 // 3, t % 3, 0:3 * P], hT[:, k, t * P:t * P + n],
                                                   w_head[:, k, :], start=(k == 0), stop=(k == KD - 1))
                        ins.then_inc(pj, 1)
                    pe.wait_ge(g_in, h * 16 + 16)
                    pe.wait_ge(pj_ev, h * (TT + 1) + TT + 1)
                    for part in (1, 0):
                        for c0, n in ((0, BANK), (BANK, BANK), (T, M)):
                            for k in range(KD):
                                ins = nc.tensor.matmul(S[:, 1 - part, c0 // BANK, 0:n],
                                                       w_glu[:, k, part * P:part * P + P], hT[:, k, c0:c0 + n],
                                                       start=(k == 0), stop=(k == KD - 1))
                        ins.then_inc(cv, 1)
                    pe.wait_ge(roped, h + 1)
                    pe.wait_ge(wt_ev, h * NB)
                    pe.wait_ge(o_ev, h * TT)
                    for b in range(5):
                        bank = OB if b % 2 else TB
                        if b >= 2:
                            pe.wait_ge(tq_ev, h * 5 + b - 1)
                        if b == 4:
                            pe.nop(nofuse=True)
                            ins = nc.tensor.transpose(bank[:, 0:M], qkv[0:M, TT, P:2 * P], identity[0:M, 0:M])
                        else:
                            for c in range(4):
                                ins = nc.tensor.transpose(bank[:, c * P:c * P + P],
                                                          qkv[:, b % 2 * 4 + c, b // 2 * P:b // 2 * P + P],
                                                          identity[:, :])
                        ins.then_inc(tq, 1)

                    def scores(i):
                        nfr = (i + 1) * P
                        for mp in range(2):
                            r = slice(mp * HD, mp * HD + HD)
                            if i == 0:
                                pe.wait_ge(ga_done if mp else th_done, h + 1)
                            else:
                                pe.wait_ge(ex_done, h * 16 + 2 * (i - 1) + mp + 1)
                            for c0 in range(0, nfr, BANK):
                                n = min(BANK, nfr - c0)
                                nc.tensor.matmul(S[:, mp, c0 // BANK, 0:n], qT[r, i * P:i * P + P],
                                                 kT[r, c0:c0 + n], start=True, stop=True)
                            nc.tensor.matmul(S[:, mp, nfr // BANK, nfr % BANK:nfr % BANK + M],
                                             qT[r, i * P:i * P + P], kT[r, T:L], start=True,
                                             stop=True).then_inc(s_done, 1)

                    pe.wait_ge(tq_ev, h * 5 + 5)
                    scores(0)
                    for i in range(TT):
                        if i + 1 < TT:
                            scores(i + 1)
                        pe.wait_ge(w_done, h * TT + i + 1)
                        seen = h * NB + before[i]
                        pe.wait_ge(wt_ev, seen)
                        pe.wait_ge(o_ev, h * TT + i)
                        for b in range(nbatch[i]):
                            if b:
                                pe.wait_ge(wt_ev, seen + 1)
                            for j in range(4 * b, min(4 * b + 4, i + 1)):
                                ins = nc.tensor.transpose(TB[:, j % 4 * P:j % 4 * P + P],
                                                          mixed[:, j * P:j * P + P], identity[:, :])
                            ins.then_inc(wt, 1)
                            if b == 0:
                                nc.tensor.transpose(OB[0:M, 3 * P:4 * P], mixed[:, (i + 1) * P:(i + 1) * P + M],
                                                    identity[:, :]).then_inc(wt, 1)
                        pe.wait_ge(wt_ev, seen + 2)
                        nc.tensor.matmul(OB[:, 0:P], mixTm[:, :], qkv[0:M, TT, 2 * P:3 * P], start=True, stop=False)
                        for j in range(i + 1):
                            if j == 4:
                                pe.wait_ge(wt_ev, seen + 3)
                            ins = nc.tensor.matmul(OB[:, 0:P], mixT[:, j * P:j * P + P], qkv[:, j, 2 * P:3 * P],
                                                   start=False, stop=(j == i))
                        ins.then_inc(o_done, 1)

            @block.scalar
            def _(act):
                act.wait_ge(pre, 2)
                nc.scalar.activation(lam[:, 0:2], lam[:, 0:2], ACT.Exp).then_inc(lam_e, 1)
                act.wait_ge(pre, 3)
                with act.Fori(0, HEADS) as h:
                    act.wait_ge(u_done, h)
                    act.wait_ge(cv, h * 2 + 1)
                    act.nop(nofuse=True)
                    nc.scalar.activation(glu_t[:, :], S[:, 0, :, :].rearrange("p b c -> p (b c)")[:, 0:L], ACT.Tanh,
                                         bias=glu_h[:, 1, ds(h, 1)], scale=0.5).then_inc(th_done, 1)
                    act.wait_ge(cv, h * 2 + 2)
                    act.nop(nofuse=True)
                    nc.scalar.activation(glu_a[:, :], S[:, 1, :, :].rearrange("p b c -> p (b c)")[:, 0:L],
                                         ACT.Identity, bias=glu_h[:, 0, ds(h, 1)], scale=0.5).then_inc(ga_done, 1)
                    act.wait_ge(s_done, h * 16)
                    for b in range(5):
                        act.wait_ge(tq, h * 5 + b + 1)
                        bank = OB if b % 2 else TB
                        if b == 4:
                            nc.scalar.activation(kT[:, T:L], bank[:, 0:M], ACT.Copy).then_inc(tq_ev, 1)
                        else:
                            dst = (kT if b // 2 else qT)[:, b % 2 * BANK:b % 2 * BANK + BANK]
                            nc.scalar.activation(dst, bank[:, :], ACT.Copy,
                                                 scale=1.0 if b // 2 else HD ** -0.5).then_inc(tq_ev, 1)

                    def exps(i):
                        n = (i + 1) * P + M
                        act.wait_ge(w_done, h * TT + max(i - 1, 0))
                        for mp in range(2):
                            c = i % 2 * 2 + mp
                            act.wait_ge(mx_done, h * 16 + 2 * i + mp + 1)
                            nc.scalar.activation(prob[:, i % 2, mp, 0:n],
                                                 S[:, mp, :, :].rearrange("p b c -> p (b c)")[:, 0:n], ACT.Exp,
                                                 bias=negmax[:, c:c + 1],
                                                 accum_out=sums[:, c:c + 1]).then_inc(ex_done, 1)

                    exps(0)
                    for i in range(TT):
                        if i + 1 < TT:
                            exps(i + 1)
                        act.wait_ge(o_done, h * TT + i)
                        seen = h * NB + before[i]
                        act.wait_ge(wt, seen + 1)
                        n = min(4, i + 1) * P
                        nc.scalar.activation(mixT[:, 0:n], TB[:, 0:n], ACT.Copy).then_inc(wt_ev, 1)
                        act.wait_ge(wt, seen + 2)
                        nc.scalar.activation(mixTm[:, :], OB[0:M, 3 * P:4 * P], ACT.Copy).then_inc(wt_ev, 1)
                        if nbatch[i] == 2:
                            act.wait_ge(wt, seen + 3)
                            n = (i - 3) * P
                            nc.scalar.activation(mixT[:, BANK:BANK + n], TB[:, 0:n], ACT.Copy).then_inc(wt_ev, 1)
                        act.wait_ge(o_done, h * TT + i + 1)
                        act.nop(nofuse=True)
                        nc.scalar.activation(oall[:, i, ds(h, 1), :].rearrange("p o c -> p (o c)"), OB[:, 0:P],
                                             ACT.Copy).then_inc(o_ev, 1)

            @block.vector
            def _(dve):
                nc.vector.memset(qkv[:, TT, :], 0.0).then_inc(init, 1)
                nc.vector.memset(u_pad[:, 0:PAD], 0.0).then_inc(init, 1)
                dve.wait_ge(init, 2)
                dve.wait_ge(tab_in, 9 * 16)
                c0 = Chain(dve, sem("mx_lam_chain"))
                c0.then(nc.vector.tensor_tensor(lamp[:, :, :], lamv[:, 0:4:2, :], lamv[:, 1:4:2, :], ALU.mult))
                nc.vector.tensor_reduce(lam[:, 0:2], lamp[:, :, :], AX.X, ALU.add).then_inc(pre, 2)
                nc.vector.tensor_scalar(glu_h[:, :, :], glu_b[:, :, :], 0.5, None, ALU.mult).then_inc(pre, 1)
                dve.wait_ge(lam_e, 1)
                c0.then(nc.vector.tensor_tensor(lam[:, 2:3], lam[:, 0:1], lam[:, 1:2], ALU.subtract))
                c0.then(nc.vector.tensor_scalar(lam[:, 3:4], lam[:, 2:3], LAM_INIT, None, ALU.add))

                with dve.Fori(0, HEADS) as h:
                    c = Chain(dve, chain, h * DVE_PER)
                    dve.wait_ge(b_in, h * 16 + 16)
                    dve.wait_ge(o_done, h * TT)
                    for t in range(TT + 1):
                        n = P if t < TT else M
                        dve.wait_ge(pj, h * (TT + 1) + t + 1)
                        nc.vector.tensor_tensor(qkv[0:n, t, :], S[0:n, t % 6 // 3, t % 3, 0:3 * P], b_head[0:n, :],
                                                ALU.add).then_inc(pj_ev, 1)
                    dve.wait_ge(pj_ev, h * (TT + 1) + TT + 1)
                    qk = qkv[:, :, 0:2 * P].rearrange("p t (x d) -> p t x d", d=HD)
                    r1, r2 = qk[:, :, :, 0:ROT], qk[:, :, :, ROT:2 * ROT]
                    bc = [x[:, :, :].unsqueeze(2).to_broadcast([P, TT + 1, 4, ROT]) for x in (cos_t, sin_t)]
                    tmp = [rot[:, j, :].rearrange("p (t x d) -> p t x d", t=TT + 1, x=4) for j in range(4)]
                    for j, (a, b) in enumerate(((r1, bc[0]), (r2, bc[1]), (r2, bc[0]), (r1, bc[1]))):
                        ins = nc.vector.tensor_tensor(tmp[j], a, b, ALU.mult)
                    c.then(ins)
                    nc.vector.tensor_tensor(r1, tmp[0], tmp[1], ALU.subtract)
                    nc.vector.tensor_tensor(r2, tmp[2], tmp[3], ALU.add).then_inc(roped, 1)
                    dve.wait_ge(th_done, h + 1)
                    dve.wait_ge(ga_done, h + 1)
                    nc.vector.scalar_tensor_tensor(u_pad[:, PAD + M:PAD + L], glu_t[:, 0:T], 1.0, glu_a[:, 0:T],
                                                   ALU.add, ALU.mult)
                    nc.vector.scalar_tensor_tensor(u_pad[:, PAD:PAD + M], glu_t[:, T:L], 1.0, glu_a[:, T:L],
                                                   ALU.add, ALU.mult).then_inc(u_done, 1)
                    dve.wait_ge(u_done, h + 1)
                    c.then(nc.vector.tensor_scalar(y_sum[:, :], u_pad[:, M:M + T], taps_w[:, ds(h, 1), 0],
                                                   taps_b[:, ds(h, 1)], ALU.mult, ALU.add))

                    def tap(k):
                        out = y_sum[:, :] if k < TAPS - 1 else yconv[:, ds(h, 1), :].rearrange("p o t -> p (o t)")
                        c.then(nc.vector.scalar_tensor_tensor(out, u_pad[:, M + k:M + k + T], taps_w[:, ds(h, 1), k],
                                                              y_sum[:, :], ALU.mult, ALU.add))

                    def maxes(i):
                        nfr = (i + 1) * P
                        for mp in range(2):
                            dve.wait_ge(s_done, h * 16 + 2 * i + mp + 1)
                            s = S[:, mp, :, :].rearrange("p b c -> p (b c)")
                            c.then(nc.vector.memset(s[0:CHUNK, nfr - CHUNK:nfr], -1e30))
                            q = i % 2 * 2 + mp
                            nc.vector.tensor_reduce(negmax[:, q:q + 1], s[:, 0:nfr + M], AX.X, ALU.max,
                                                    negate=True).then_inc(mx_done, 1)

                    maxes(0)
                    k = 1
                    for i in range(TT):
                        for _ in range(TAPS_AT[i]):
                            tap(k)
                            k += 1
                        if i + 1 < TT:
                            maxes(i + 1)
                        n = (i + 1) * P + M
                        q = i % 2 * 2
                        dve.wait_ge(ex_done, h * 16 + 2 * i + 2)
                        c.then(nc.vector.reciprocal(rr[:, :], sums[:, q:q + 2]))
                        c.then(nc.vector.tensor_tensor(rr[:, 1:2], rr[:, 1:2], lam[:, 3:4], ALU.mult))
                        c.then(nc.vector.tensor_scalar(second[:, 0:n], prob[:, i % 2, 1, 0:n], rr[:, 1:2], None,
                                                       ALU.mult))
                        dve.wait_ge(wt, h * NB + before[i])
                        nc.vector.scalar_tensor_tensor(mixed[:, 0:n], prob[:, i % 2, 0, 0:n], rr[:, 0:1],
                                                       second[:, 0:n], ALU.mult, ALU.subtract).then_inc(w_done, 1)
                    assert k == TAPS
                    assert c.n == DVE_PER, c.n


def branch(nc, sem, A, hT, identity, oall, yconv, oT, at):
    m = Map(nc, at)
    sq = m.take("br_sq", [P, TT * HEADS, P])
    ms = m.take("br_ms", [P, 5, TT * HEADS])
    sub_g = m.take("br_g", [P, 2])
    chan = m.take("br_chan", [P, 2, HEADS])
    ones = m.take("br_ones", [P, P])
    sqc = m.take("br_sqc", [P, 2, T])
    rstd = m.take("br_rstd", [P, T])
    eps = m.take("br_eps", [P, 1])
    with nc.psum_tensor("br_t", [P, 2, BANK], F32) as TB, nc.psum_tensor("br_mean", [P, T], F32) as MEAN, \
            nc.psum_tensor("br_var", [P, T], F32) as VAR:
        eps_ready = sem("br_eps_ready")
        par_in = sem("br_par")
        ready = sem("br_ones_ready")
        chain = sem("br_chain")
        root = sem("br_root")
        rooted = sem("br_rooted")
        g8 = sem("br_g8")
        summed, small_sq = sem("br_summed"), sem("br_small_sq")
        o_norm = sem("br_o_norm")
        mean_done = sem("br_mean_s")
        cent = sem("br_cent")
        sq_done = sem("br_sq_done")
        var_done = sem("br_var_s")
        tr, tr_ev = sem("br_tr"), sem("br_tr_ev")
        z_done = sem("br_z")
        NH = TT * HEADS
        with nc.Block() as block:
            @block.sync
            def _(sp):
                sp.dma_start(sub_g[:, 0:1], A["subln_col"]).then_inc(par_in, 16)
                sp.dma_start(chan[:, :, :], A["chan"][:, 5:7, :]).then_inc(par_in, 16)

            @block.vector
            def _(dve):
                c = Chain(dve, chain)
                nc.vector.memset(ones[:, :], 1.0 / D).then_inc(ready, 1)
                dve.wait_ge(par_in, 32)
                nc.vector.tensor_scalar(sub_g[:, 1:2], sub_g[:, 0:1], 1.0 - LAM_INIT, None, ALU.mult).then_inc(g8, 1)
                o2 = oall[:, :, :, :].rearrange("p t h c -> p (t h) c")
                c.then(nc.vector.tensor_scalar(sq[:, :, :], o2, O_LIMIT, -O_LIMIT, ALU.min, ALU.max))
                c.then(nc.vector.tensor_tensor(sq[:, :, :], sq[:, :, :], sq[:, :, :], ALU.mult))
                nc.vector.tensor_reduce(ms[:, 0, :], sq[:, :, :], AX.X, ALU.add).then_inc(summed, 1)
                dve.wait_ge(small_sq, 1)
                c.then(nc.vector.tensor_reduce(ms[:, 3, :], sq[:, :, :], AX.X, ALU.add))
                c.then(nc.vector.tensor_scalar(ms[:, 2, :], ms[:, 3, :], 2.0 ** -60, None, ALU.is_ge))
                nc.vector.tensor_scalar(ms[:, 0, :], ms[:, 0, :], 1.0 / P, LN_EPS, ALU.mult, ALU.add)
                c.then(nc.vector.tensor_scalar(ms[:, 4, :], ms[:, 2, :], -1.0, 1.0, ALU.mult, ALU.add))
                nc.vector.scalar_tensor_tensor(ms[:, 1, :], ms[:, 3, :], 1.0 / P, ms[:, 2, :], ALU.mult, ALU.mult)
                c.then(nc.vector.tensor_tensor(ms[:, 0, :], ms[:, 0, :], ms[:, 4, :], ALU.mult))
                nc.vector.tensor_tensor(ms[:, 1, :], ms[:, 1, :], ms[:, 0, :], ALU.add).then_inc(root, 1)
                c.then(nc.vector.scalar_tensor_tensor(ms[:, 4, :], ms[:, 2, :], 2.0 ** -70, ms[:, 4, :], ALU.mult,
                                                      ALU.add))
                c.then(nc.vector.scalar_tensor_tensor(ms[:, 4, :], ms[:, 3, :], 2.0 ** -12, ms[:, 4, :], ALU.is_lt,
                                                      ALU.mult))
                dve.wait_ge(mean_done, 1)
                for h in range(HEADS):
                    nc.vector.tensor_tensor(yconv[:, h, :], yconv[:, h, :], MEAN[:, :], ALU.subtract).then_inc(cent, 1)
                dve.wait_ge(rooted, 1)
                c.then(nc.vector.reciprocal(ms[:, 2, :], ms[:, 1, :]))
                c.then(nc.vector.tensor_tensor(ms[:, 2, :], ms[:, 2, :], ms[:, 4, :], ALU.mult))
                nc.vector.tensor_tensor(o2, o2, ms[:, 2, :].unsqueeze(2).to_broadcast([P, NH, P]),
                                        ALU.mult).then_inc(o_norm, 1)
                dve.wait_ge(rooted, 2)
                c.then(nc.vector.reciprocal(rstd[:, :], rstd[:, :]))
                for h in range(HEADS):
                    nc.vector.tensor_tensor(yconv[:, h, :], yconv[:, h, :], rstd[:, :], ALU.mult).then_inc(z_done, 1)

            @block.tensor
            def _(pe):
                pe.wait_ge(ready, 1)
                for f in range(2):
                    for h in range(HEADS):
                        ins = nc.tensor.matmul(MEAN[:, f * BANK:f * BANK + BANK], ones[:, :],
                                               yconv[:, h, f * BANK:f * BANK + BANK], start=(h == 0),
                                               stop=(h == HEADS - 1))
                ins.then_inc(mean_done, 1)
                for h in range(HEADS):
                    pe.wait_ge(sq_done, h + 1)
                    for f in range(2):
                        ins = nc.tensor.matmul(VAR[:, f * BANK:f * BANK + BANK], ones[:, :],
                                               sqc[:, h % 2, f * BANK:f * BANK + BANK], start=(h == 0),
                                               stop=(h == HEADS - 1))
                    ins.then_inc(var_done, 1)
                pe.wait_ge(o_norm, 1)
                n = 0
                for h in range(HEADS):
                    for f in range(2):
                        if n >= 2:
                            pe.wait_ge(tr_ev, n - 1)
                        for t in range(4):
                            ins = nc.tensor.transpose(TB[:, n % 2, t * P:t * P + P], oall[:, 4 * f + t, h, :],
                                                      identity[:, :])
                        ins.then_inc(tr, 1)
                        n += 1

            @block.scalar
            def _(act):
                act.wait_ge(summed, 1)
                nc.scalar.activation(sq[:, :, :], oall[:, :, :, :].rearrange("p t h c -> p (t h) c"), ACT.Square,
                                     scale=2.0 ** -70).then_inc(small_sq, 1)
                for h in range(HEADS):
                    act.wait_ge(cent, h + 1)
                    if h >= 2:
                        act.wait_ge(var_done, h - 1)
                    nc.scalar.activation(sqc[:, h % 2, :], yconv[:, h, :], ACT.Square).then_inc(sq_done, 1)
                act.wait_ge(root, 1)
                nc.scalar.activation(ms[:, 1, :], ms[:, 1, :], ACT.Sqrt).then_inc(rooted, 1)
                act.wait_ge(var_done, HEADS)
                act.wait_ge(eps_ready, 1)
                nc.scalar.activation(rstd[:, :], VAR[:, :], ACT.Sqrt, bias=eps[:, :]).then_inc(rooted, 1)
                act.wait_ge(g8, 1)
                n = 0
                for h in range(HEADS):
                    for f in range(2):
                        act.wait_ge(tr, n + 1)
                        nc.scalar.activation(oT[:, h, f * BANK:f * BANK + BANK], TB[:, n % 2, :], ACT.Copy,
                                             scale=sub_g[:, 1:2]).then_inc(tr_ev, 1)
                        n += 1
                for h in range(HEADS):
                    act.wait_ge(z_done, h + 1)
                    nc.scalar.activation(yconv[:, h, :], yconv[:, h, :], ACT.Silu, bias=chan[:, 1, h:h + 1],
                                         scale=chan[:, 0, h:h + 1])

            @block.gpsimd
            def _(pool):
                nc.gpsimd.memset(eps[:, :], LN_EPS).then_inc(eps_ready, 1)


def merge(nc, sem, A, hT, oT, zT, mT, at):
    m = Map(nc, at)
    wg = m.take("mg_wg", [P, 2, KD, 2 * P])
    wa = m.take("mg_wa", [P, 2, KD, P])
    wc = m.take("mg_wc", [P, 2, KD, P])
    th = m.take("mg_th", [P, 2, 2, BANK])
    cd = m.take("mg_cd", [P, 2, BANK])
    part = m.take("mg_part", [P, 2, 2, BANK])
    bias = m.take("mg_bias", [P, 3, HEADS])
    half = m.take("mg_half", [P, 3, HEADS])
    with nc.psum_tensor("mg_ps", [P, 2, 4, BANK], F32) as PS:
        par_in = sem("mg_par")
        w_in = [sem("mg_w_in0"), sem("mg_w_in1")]
        halved = sem("mg_halved")
        pr = sem("mg_pr")
        th_done = sem("mg_th_done")
        part_done = sem("mg_part_done")
        m_done = sem("mg_m_done")
        with nc.Block() as block:
            @block.sync
            def _(sp):
                sp.dma_start(bias[:, 0:2, :], A["chan"][:, 2:4, :]).then_inc(par_in, 16)
                sp.dma_start(bias[:, 2, :], A["chan"][:, 7, :]).then_inc(par_in, 16)
                with sp.Fori(0, TT // 2) as i:
                    for u in range(2):
                        sp.wait_ge(m_done, i * 4 + 2 * u)
                        for dst, name in ((wg, "w_gate"), (wa, "w_attn"), (wc, "w_conv")):
                            sp.dma_start(dst[:, u, :, :], A[name][ds(i * 2 + u, 1)].rearrange("o p k c -> (o p) k c")
                                         ).then_inc(w_in[u], 16)

            @block.tensor
            def _(pe):
                with pe.Fori(0, TT // 2) as i:
                    for u in range(2):
                        pe.wait_ge(w_in[u], i * 48 + 48)
                        for f in range(2):
                            x = i * 4 + 2 * u + f
                            pe.wait_ge(m_done, x)
                            fr = slice(f * BANK, f * BANK + BANK)
                            for j, (w, src) in enumerate(((wg[:, u, :, 0:P], hT), (wg[:, u, :, P:2 * P], hT),
                                                          (wa[:, u, :, :], oT), (wc[:, u, :, :], zT))):
                                for k in range(KD):
                                    ins = nc.tensor.matmul(PS[:, f, j, :], w[:, k, :], src[:, k, fr],
                                                           start=(k == 0), stop=(k == KD - 1))
                            ins.then_inc(pr, 1)

            @block.scalar
            def _(act):
                act.wait_ge(halved, 1)
                with act.Fori(0, TT // 2) as i:
                    for u in range(2):
                        for f in range(2):
                            x = i * 4 + 2 * u + f
                            act.wait_ge(pr, x + 1)
                            act.wait_ge(m_done, x)
                            act.nop(nofuse=True)
                            for j in range(2):
                                nc.scalar.activation(th[:, f, j, :], PS[:, f, j, :], ACT.Tanh,
                                                     bias=half[:, j, ds(i * 2 + u, 1)], scale=0.5)
                            nc.scalar.activation(cd[:, f, :], PS[:, f, 3, :], ACT.Identity,
                                                 bias=half[:, 2, ds(i * 2 + u, 1)], scale=0.5).then_inc(th_done, 1)

            @block.vector
            def _(dve):
                dve.wait_ge(par_in, 32)
                nc.vector.tensor_scalar(half[:, :, :], bias[:, :, :], 0.5, None, ALU.mult).then_inc(halved, 1)
                dve.wait_ge(halved, 1)
                nc.vector.memset(part[:, :, :, :], 0.0).then_inc(m_done, 1)
                dve.wait_ge(m_done, 1)
                with dve.Fori(0, TT // 2) as i:
                    for u in range(2):
                        for f in range(2):
                            x = i * 4 + 2 * u + f
                            dve.wait_ge(th_done, x + 1)
                            nc.vector.scalar_tensor_tensor(part[:, f, 0, :], th[:, f, 0, :], 1.0, PS[:, f, 2, :],
                                                           ALU.add, ALU.mult)
                            nc.vector.scalar_tensor_tensor(part[:, f, 1, :], th[:, f, 1, :], 1.0, cd[:, f, :],
                                                           ALU.add, ALU.mult).then_inc(part_done, 1)
                            dve.wait_ge(part_done, x + 1)
                            nc.vector.scalar_tensor_tensor(
                                mT[:, ds(i * 2 + u, 1), f * BANK:f * BANK + BANK].rearrange("p o t -> p (o t)"),
                                part[:, f, 0, :], 0.5, part[:, f, 1, :], ALU.mult, ALU.add).then_inc(m_done, 1)


def layer_norm_tile(dve, c, nc, x, out, stats, mv, gamma, beta, root, rooted, n):
    nc.vector.bn_stats(stats[:, 0, :], x[:, 0:BANK])
    c.then(nc.vector.bn_stats(stats[:, 1, :], x[:, BANK:D]))
    c.then(nc.vector.bn_aggr(mv[:, 0:2], stats[:, :, :].rearrange("p a b -> p (a b)")))
    nc.vector.tensor_scalar(mv[:, 2:3], mv[:, 1:2], LN_EPS, None, ALU.add).then_inc(root, 1)
    dve.wait_ge(rooted, n + 1)
    c.then(nc.vector.reciprocal(mv[:, 3:4], mv[:, 3:4]))
    c.then(nc.vector.tensor_scalar(x, x, mv[:, 0:1], mv[:, 3:4], ALU.subtract, ALU.mult))
    c.then(nc.vector.tensor_tensor(x, x, gamma, ALU.mult))
    return nc.vector.tensor_tensor(out, x, beta, ALU.add)


def project(nc, sem, A, mT, identity, h_dram, h1T, acc, at_w, at):
    wout = Map(nc, at_w).take("pj_w", [P, KD, D])
    m = Map(nc, at)
    bout = m.take("pj_bout", [P, D])
    gamma = m.take("pj_gamma", [P, D])
    beta = m.take("pj_beta", [P, D])
    h_in = m.take("pj_h", [P, 2, D])
    r = m.take("pj_r", [P, 2, D])
    stats = m.take("pj_stats", [P, 2, 6])
    mv = m.take("pj_mv", [P, 4])
    with nc.psum_tensor("pj_y", [P, 2, D], F32) as Y, nc.psum_tensor("pj_t", [P, 4, BANK], F32) as TB:
        par_in, h_ld = sem("pj_par"), [sem("pj_h_in0"), sem("pj_h_in1")]
        y_done, r_done = sem("pj_y_done"), sem("pj_r_done")
        chain, root, rooted = sem("pj_chain"), sem("pj_root"), sem("pj_rooted")
        h1_done, tr, tr_ev, ac = sem("pj_h1"), sem("pj_tr"), sem("pj_tr_ev"), sem("pj_acc")
        with nc.Block() as block:
            @block.sync
            def _(sp):
                sp.dma_start(wout[:, :, :], A["w_out"]).then_inc(par_in, 16)
                for dst, name in ((bout, "b_out"), (gamma, "ln1_g"), (beta, "ln1_b")):
                    sp.dma_start(dst[:, :], row(A[name])).then_inc(par_in, 16)
                for t in range(TT):
                    if t >= 2:
                        sp.wait_ge(r_done, t - 1)
                    sp.dma_start(h_in[:, t % 2, :], h_dram[t]).then_inc(h_ld[t % 2], 16)

            @block.tensor
            def _(pe):
                pe.wait_ge(par_in, 64)

                def turn(t):
                    pe.wait_ge(h1_done, t + 1)
                    for f in range(2):
                        if t >= 2:
                            pe.wait_ge(tr_ev, 2 * (t - 2) + f + 1)
                        for k in range(4):
                            ins = nc.tensor.transpose(TB[:, t % 2 * 2 + f, k * P:k * P + P],
                                                      r[:, t % 2, (4 * f + k) * P:(4 * f + k + 1) * P], identity[:, :])
                        ins.then_inc(tr, 1)

                for t in range(TT):
                    if t >= 2:
                        pe.wait_ge(r_done, t - 1)
                    for f in range(2):
                        for k in range(KD):
                            ins = nc.tensor.matmul(Y[:, t % 2, f * BANK:f * BANK + BANK], mT[:, k, t * P:t * P + P],
                                                   wout[:, k, f * BANK:f * BANK + BANK], start=(k == 0),
                                                   stop=(k == KD - 1))
                    ins.then_inc(y_done, 1)
                    if t:
                        turn(t - 1)
                turn(TT - 1)

            @block.vector
            def _(dve):
                c = Chain(dve, chain)
                dve.wait_ge(par_in, 64)
                for t in range(TT):
                    u = t % 2
                    dve.wait_ge(y_done, t + 1)
                    if t >= 2:
                        dve.wait_ge(tr_ev, 2 * (t - 1))
                        dve.wait_ge(ac, t - 1)
                    c.then(nc.vector.tensor_tensor(r[:, u, :], Y[:, u, :], bout[:, :], ALU.add))
                    dve.wait_ge(h_ld[u], 16 * (t // 2 + 1))
                    nc.vector.scalar_tensor_tensor(r[:, u, :], h_in[:, u, :], ALPHA, r[:, u, :], ALU.mult,
                                                   ALU.add).then_inc(r_done, 1)
                    dve.wait_ge(r_done, t + 1)
                    layer_norm_tile(dve, c, nc, r[:, u, :], r[:, u, :], stats, mv, gamma[:, :], beta[:, :], root,
                                    rooted, t).then_inc(h1_done, 1)

            @block.scalar
            def _(act):
                def store(t):
                    act.wait_ge(h1_done, t + 1)
                    nc.scalar.activation(acc[:, t, :], r[:, t % 2, :], ACT.Copy, scale=ALPHA).then_inc(ac, 1)
                    for f in range(2):
                        act.wait_ge(tr, 2 * t + f + 1)
                        nc.scalar.activation(h1T[:, 4 * f:4 * f + 4, t * P:t * P + P],
                                             TB[:, t % 2 * 2 + f, :].rearrange("p (k c) -> p k c", k=4),
                                             ACT.Copy).then_inc(tr_ev, 1)

                for t in range(TT):
                    act.wait_ge(root, t + 1)
                    nc.scalar.activation(mv[:, 3:4], mv[:, 2:3], ACT.Sqrt).then_inc(rooted, 1)
                    if t:
                        store(t - 1)
                store(TT - 1)


def route(nc, sem, A, h1T, identity, picks, at, at2):
    m = Map(nc, at)
    HP = 2 * HEADS
    wq = m.take("rt_wq", [P, HP, KD, P])
    sub = m.take("rt_sub", [P, HP, KEYS])
    qt = m.take("rt_qt", [P, HP, P])
    s = m.take("rt_s", [P, HP, KEYS])
    s2 = m.take("rt_s2", [P, HP, KEYS])
    m = Map(nc, at2)
    sv = m.take("rt_sv", [P, HP, K])
    si = m.take("rt_si", [P, HP, K], U32)
    sf = m.take("rt_sf", [P, HP, K])
    cand = m.take("rt_cand", [P, HEADS, K * K])
    cand2 = m.take("rt_cand2", [P, HEADS, K * K])
    cv = m.take("rt_cv", [P, HEADS, K])
    ci = m.take("rt_ci", [P, HEADS, K], U32)
    cab = m.take("rt_cab", [P, 2, HEADS, K], U32)
    cf = m.take("rt_cf", [P, 2, HEADS, K])
    iota = m.take("rt_iota", [P, K])
    eq = m.take("rt_eq", [P, HEADS * K, K])
    pick = m.take("rt_pick", [P, 3, HEADS, K])
    gs = m.take("rt_gs", [P, 2, HEADS])
    PER = 20
    with nc.psum_tensor("rt_q", [P, 2, BANK], F32) as Q, nc.psum_tensor("rt_ps", [P, 4, BANK], F32) as S, \
            nc.psum_tensor("rt_t", [P, BANK], F32) as TB:
        par_in = sem("rt_par")
        q_done, q_ev = sem("rt_q_done"), sem("rt_q_ev")
        s_done, s_ev = sem("rt_s_done"), sem("rt_s_ev")
        s_used = sem("rt_s_used")
        chain = sem("rt_chain")
        ex, exd = sem("rt_ex"), sem("rt_exd")
        picked, tr, tr_ev = sem("rt_picked"), sem("rt_tr"), sem("rt_tr_ev")
        with nc.Block() as block:
            @block.sync
            def _(sp):
                for h in range(HEADS):
                    sp.dma_start(wq[:, 2 * h:2 * h + 2, :, :], A["w_query"][:, 2 * h:2 * h + 2, :, :]
                                 ).then_inc(par_in, 16)
                sp.dma_start(sub[:, :, :], A["subkeys"]).then_inc(par_in, 16)
                sp.dma_start(iota[:, :], A["iota"][:, 0:K]).then_inc(par_in, 16)

            @block.tensor
            def _(pe):
                pe.wait_ge(par_in, 160)
                with pe.Fori(0, TT) as t:
                    for b in range(4):
                        if b < 2:
                            pe.wait_ge(q_ev, t * 4)
                        else:
                            pe.wait_ge(q_ev, t * 4 + b - 1)
                        for x in range(4):
                            for k in range(KD):
                                ins = nc.tensor.matmul(Q[:, b % 2, x * P:x * P + P], wq[:, 4 * b + x, k, :],
                                                       h1T[:, k, ds(t * P, P)], start=(k == 0), stop=(k == KD - 1))
                        ins.then_inc(q_done, 1)
                    for b in range(4):
                        pe.wait_ge(q_ev, t * 4 + b + 1)
                        pe.wait_ge(s_ev, t * 4)
                        for x in range(4):
                            ins = nc.tensor.matmul(S[:, b, x * P:x * P + P], qt[:, 4 * b + x, :], sub[:, 4 * b + x, :],
                                                   start=True, stop=True)
                        ins.then_inc(s_done, 1)
                    pe.wait_ge(picked, t + 1)
                    pe.wait_ge(tr_ev, t)
                    for j in range(3):
                        ins = nc.tensor.transpose(TB[:, j * P:j * P + P], pick[:, j, :, :].rearrange("p h k -> p (h k)"),
                                                  identity[:, :])
                    ins.then_inc(tr, 1)

            @block.scalar
            def _(act):
                with act.Fori(0, TT) as t:
                    for b in range(4):
                        act.wait_ge(q_done, t * 4 + b + 1)
                        act.wait_ge(s_done, t * 4)
                        nc.scalar.activation(qt[:, 4 * b:4 * b + 4, :],
                                             Q[:, b % 2, :].rearrange("p (x c) -> p x c", x=4),
                                             ACT.Copy).then_inc(q_ev, 1)
                    act.wait_ge(s_used, t)
                    for b in range(4):
                        act.wait_ge(s_done, t * 4 + b + 1)
                        nc.scalar.activation(s[:, 4 * b:4 * b + 4, :], S[:, b, :].rearrange("p (x c) -> p x c", x=4),
                                             ACT.Copy).then_inc(s_ev, 1)
                    act.wait_ge(ex, t + 1)
                    nc.scalar.activation(pick[:, 2, :, :], pick[:, 2, :, :], ACT.Exp).then_inc(exd, 1)
                    act.wait_ge(tr, t + 1)
                    act.nop(nofuse=True)
                    nc.scalar.activation(picks[:, :, ds(t * P, P)], TB[:, 0:3 * P].rearrange("p (j c) -> p j c", j=3),
                                         ACT.Copy).then_inc(tr_ev, 1)

            @block.vector
            def _(dve):
                dve.wait_ge(par_in, 160)
                with dve.Fori(0, TT) as t:
                    c = Chain(dve, chain, t * PER)
                    dve.wait_ge(s_ev, t * 4 + 4)
                    dve.nop(nofuse=True)

                    def top16(vals, idx, src, spare, n, after=None):
                        for x in range(n):
                            ins = nc.vector.max(vals[:, x, 0:8], src[:, x, :])
                        c.then(ins, apart=True)
                        for x in range(n):
                            nc.vector.max_index(idx[:, x, 0:8], vals[:, x, 0:8], src[:, x, :])
                            ins = nc.vector.match_replace(spare[:, x, :], vals[:, x, 0:8], src[:, x, :], LOWEST)
                        c.then(ins, apart=True)
                        for x in range(n):
                            ins = nc.vector.max(vals[:, x, 8:16], spare[:, x, :])
                        c.then(ins, apart=True)
                        for x in range(n):
                            ins = nc.vector.max_index(idx[:, x, 8:16], vals[:, x, 8:16], spare[:, x, :])
                        c.then(ins, apart=True)

                    top16(sv, si, s, s2, HP)
                    c.then(nc.vector.tensor_copy(sf[:, :, :], si[:, :, :]))
                    nc.vector.tensor_copy(gs[:, 0, :], sf[:, 0:HEADS, 0]).then_inc(s_used, 1)
                    s4 = sv[:, :, :].rearrange("p (h m) k -> p h m k", m=2)
                    c.then(nc.vector.tensor_tensor(cand[:, :, :].rearrange("p h (a b) -> p h a b", a=K),
                                                   s4[:, :, 0, :].unsqueeze(3).to_broadcast([P, HEADS, K, K]),
                                                   s4[:, :, 1, :].unsqueeze(2).to_broadcast([P, HEADS, K, K]),
                                                   ALU.add), apart=True)
                    top16(cv, ci, cand, cand2, HEADS)
                    dve.wait_ge(tr, t)
                    nc.vector.tensor_tensor(pick[:, 2, :, :], cv[:, :, :],
                                            cv[:, :, 0:1].to_broadcast([P, HEADS, K]), ALU.subtract).then_inc(ex, 1)
                    nc.vector.tensor_scalar(cab[:, 0, :, :], ci[:, :, :], 4, None, ALU.logical_shift_right)
                    c.then(nc.vector.tensor_scalar(cab[:, 1, :, :], ci[:, :, :], K - 1, None, ALU.bitwise_and))
                    c.then(nc.vector.tensor_copy(cf[:, :, :, :], cab[:, :, :, :]))
                    f4 = sf[:, :, :].rearrange("p (h m) k -> p h m k", m=2)
                    e4 = eq[:, :, :].rearrange("p (h k) a -> p h k a", h=HEADS)
                    for j in range(2):
                        c.then(nc.vector.tensor_tensor(
                            eq[:, :, :], cf[:, j, :, :].rearrange("p h k -> p (h k)").unsqueeze(2)
                            .to_broadcast([P, HEADS * K, K]),
                            iota[:, :].unsqueeze(1).to_broadcast([P, HEADS * K, K]), ALU.is_equal))
                        c.then(nc.vector.tensor_tensor(e4, e4, f4[:, :, j, :].unsqueeze(2)
                                                       .to_broadcast([P, HEADS, K, K]), ALU.mult))
                        c.then(nc.vector.tensor_reduce(pick[:, j, :, :].rearrange("p h k -> p (h k)"), eq[:, :, :],
                                                       AX.X, ALU.add))
                    dve.wait_ge(exd, t + 1)
                    c.then(nc.vector.tensor_reduce(gs[:, 0, :], pick[:, 2, :, :], AX.X, ALU.add))
                    c.then(nc.vector.reciprocal(gs[:, 1, :], gs[:, 0, :]))
                    nc.vector.tensor_tensor(pick[:, 2, :, :], pick[:, 2, :, :],
                                            gs[:, 1, :].unsqueeze(2).to_broadcast([P, HEADS, K]),
                                            ALU.mult).then_inc(picked, 1)
                    assert c.n == PER, c.n


def gates(nc, sem, A, h1T, h_hi, h_lo, picks, g_dram, at_hot, at_g0, at_g1, at_small):
    QUADS = GT // 4
    m = Map(nc, at_hot)
    hot1 = m.take("gt_hot1", [P, 4, 4, KEYS])
    hot2 = m.take("gt_hot2", [P, 4, 4, KEYS])
    stage = [Map(nc, at_g0).take("gt_stage0", [P, KEYS, GT]), Map(nc, at_g1).take("gt_stage1", [P, KEYS, GT])]
    m = Map(nc, at_small)
    iota = m.take("gt_iota", [P, KEYS])
    part = m.take("gt_part", [P, 3, GT])
    with nc.psum_tensor("gt_ps", [P, 8, BANK], F32) as PS:
        par_in, chain = sem("gt_par"), sem("gt_chain")
        hi_done, lo_done = sem("gt_hi"), sem("gt_lo")
        hot_ready = sem("gt_hot")
        mm_done = sem("gt_mm")
        ev_done = sem("gt_ev")
        g_out = [sem("gt_out0"), sem("gt_out1")]
        with nc.Block() as block:
            @block.sync
            def _(sp):
                sp.dma_start(iota[:, :], A["iota"]).then_inc(par_in, 16)
                with sp.Fori(0, GROUPS // 2) as i:
                    for u in range(2):
                        sp.wait_ge(ev_done, (i * 2 + u + 1) * QUADS + 7)
                        sp.dma_start(g_dram[:, ds(i * 2 + u, 1), :, :].rearrange("p o a t -> p (o a) t"),
                                     stage[u][:, :, :]).then_inc(g_out[u], 16)
                for u in range(2):
                    sp.wait_ge(g_out[u], 16 * GROUPS // 2)

            @block.vector
            def _(dve):
                dve.wait_ge(par_in, 16)
                nc.vector.memset(part[:, 0, :], 0.0).then_inc(mm_done, 3)
                dve.wait_ge(mm_done, 3)
                nc.vector.memset(part[:, 1, :], 0.0).then_inc(ev_done, 7)
                dve.wait_ge(ev_done, 7)
                for k in range(KD):
                    dve.wait_ge(hi_done, k + 1)
                    nc.vector.tensor_tensor(h_lo[:, k, :], h1T[:, k, :], h_hi[:, k, :].bitcast(F32),
                                            ALU.subtract).then_inc(lo_done, 1)
                dve.wait_ge(lo_done, KD)
                with dve.Fori(0, GROUPS // 2) as i:
                    for u in range(2):
                        g = i * 2 + u
                        dve.wait_ge(mm_done, g * QUADS + 3)
                        nc.vector.tensor_copy(part[:, :, :], picks[:, :, ds(g * GT, GT)]).then_inc(chain, 1)
                        dve.wait_ge(chain, g + 1)
                        for q in range(QUADS):
                            dve.wait_ge(mm_done, g * QUADS + q)
                            for x in range(4):
                                t = 4 * q + x
                                nc.vector.tensor_scalar(hot1[:, q % 4, x, :], iota[:, :], part[:, 0, t:t + 1], None,
                                                        ALU.is_equal)
                                ins = nc.vector.tensor_scalar(hot2[:, q % 4, x, :], iota[:, :], part[:, 1, t:t + 1],
                                                              part[:, 2, t:t + 1], ALU.is_equal, ALU.mult)
                            ins.then_inc(hot_ready, 1)

            @block.tensor
            def _(pe):
                with pe.Fori(0, GROUPS // 2) as i:
                    for u in range(2):
                        for q in range(QUADS):
                            x0 = (i * 2 + u) * QUADS + q
                            pe.wait_ge(hot_ready, x0 + 1)
                            pe.wait_ge(ev_done, x0)
                            for x in range(4):
                                ins = nc.tensor.matmul(PS[:, q % 8, x * P:x * P + P], hot2[:, q % 4, x, :],
                                                       hot1[:, q % 4, x, :], start=True, stop=True)
                            ins.then_inc(mm_done, 1)

            @block.scalar
            def _(act):
                for k in range(KD):
                    nc.scalar.activation(h_hi[:, k, :], h1T[:, k, :], ACT.Copy).then_inc(hi_done, 1)
                act.wait_ge(lo_done, KD)
                with act.Fori(0, GROUPS // 2) as i:
                    for u in range(2):
                        act.wait_ge(g_out[u], i * 16)
                        for q in range(QUADS):
                            act.wait_ge(mm_done, (i * 2 + u) * QUADS + q + 4)
                            nc.scalar.activation(stage[u][:, :, 4 * q:4 * q + 4],
                                                 PS[:, q % 8, :].rearrange("p (t a) -> p a t", t=4),
                                                 ACT.Copy).then_inc(ev_done, 1)


def experts(nc, sem, A, h_hi, h_lo, acc, g_dram, at, at2):
    m = Map(nc, at)
    u_raw = m.take("ex_u_raw", [P, 2, KD, E2 * P])
    v_raw = m.take("ex_v_raw", [P, 2, E2, D])
    u_hi = m.take("ex_u_hi", [P, KD, E2 * P], F32R)
    u_lo = m.take("ex_u_lo", [P, KD, E2 * P], F32R)
    v_hi = m.take("ex_v_hi", [P, E2, D], F32R)
    v_lo = m.take("ex_v_lo", [P, E2, D], F32R)
    m = Map(nc, at2)
    gate = m.take("ex_gate", [P, 2, GROUPS, E2, GT])
    c_hi = m.take("ex_c_hi", [P, E2, T], F32R)
    c_lo = m.take("ex_c_lo", [P, E2, T], F32R)
    coef = m.take("ex_coef", [P, E2, T])
    with nc.psum_tensor("ex_a", [P, E2, T], F32) as PA, nc.psum_tensor("ex_f", [P, 2, D], F32) as PF:
        u_in = [sem("ex_u_in0"), sem("ex_u_in1")]
        v_in = [sem("ex_v_in0"), sem("ex_v_in1")]
        g_in = [sem("ex_g_in0"), sem("ex_g_in1")]
        uh, ul = sem("ex_uh"), sem("ex_ul")
        vh, vl = sem("ex_vh"), sem("ex_vl")
        up = sem("ex_up")
        ge = sem("ex_ge")
        gated = sem("ex_gated")
        ch, cl = sem("ex_ch"), sem("ex_cl")
        down = sem("ex_down")
        added = sem("ex_added")
        with nc.Block() as block:
            @block.sync
            def _(sp):
                with sp.Fori(0, STEPS // 2) as i:
                    for u in range(2):
                        s = i * 2 + u
                        sp.wait_ge(ul, s)
                        sp.dma_start(u_raw[:, u, :, :], A["u_t"][ds(s, 1)].rearrange("o p k e -> (o p) k e")
                                     ).then_inc(u_in[u], 16)
                        sp.wait_ge(gated, s)
                        sp.dma_start(gate[:, u, :, :, :].rearrange("p g j t -> p g (j t)"),
                                     g_dram[:, :, ds(s * E2, E2), :].rearrange("p g j t -> p g (j t)")
                                     ).then_inc(g_in[u], 16)
                        sp.wait_ge(vl, s)
                        sp.dma_start(v_raw[:, u, :, :], A["v"][ds(s, 1)].rearrange("o j p d -> p (o j) d")
                                     ).then_inc(v_in[u], 16)

            def unit(t, hi, lo, w_hi, w_lo, out, n):
                for a in range(n):
                    for j, (w, x) in enumerate(((w_hi, hi), (w_hi, lo), (w_lo, hi))):
                        ins = nc.tensor.matmul(out, w(a), x(a), start=(a == 0 and j == 0),
                                               stop=(a == n - 1 and j == 2))
                return ins

            @block.tensor
            def _(pe):
                def upward(s, first=False):
                    pe.wait_ge(ul, s + 2)
                    for j in range(E2):
                        if not first:
                            pe.wait_ge(ge, (s - 1) * E2 + j + 1)
                        for f in range(2):
                            ins = unit(0, lambda k: h_hi[:, k, f * BANK:f * BANK + BANK],
                                       lambda k: h_lo[:, k, f * BANK:f * BANK + BANK],
                                       lambda k: u_hi[:, k, j * P:j * P + P], lambda k: u_lo[:, k, j * P:j * P + P],
                                       PA[:, j, f * BANK:f * BANK + BANK], KD)
                        ins.then_inc(up, 1)

                def downward(s):
                    pe.wait_ge(cl, s + 1)
                    pe.wait_ge(vl, s + 2)
                    for t in range(TT):
                        pe.wait_ge(added, s * TT + t)
                        for f in range(2):
                            ins = unit(0, lambda j: v_hi[:, j, f * BANK:f * BANK + BANK],
                                       lambda j: v_lo[:, j, f * BANK:f * BANK + BANK],
                                       lambda j: c_hi[:, j, t * P:t * P + P], lambda j: c_lo[:, j, t * P:t * P + P],
                                       PF[:, t % 2, f * BANK:f * BANK + BANK], E2)
                        ins.then_inc(down, 1)

                upward(0, first=True)
                with pe.Fori(0, STEPS - 1) as i:
                    upward(i + 1)
                    downward(i)
                downward(STEPS - 1)

            @block.scalar
            def _(act):
                def split_u(s, u, i):
                    act.wait_ge(u_in[u], i * 16 + 16)
                    act.wait_ge(up, s * E2)
                    nc.scalar.activation(u_hi[:, :, :], u_raw[:, u, :, :], ACT.Copy).then_inc(uh, 1)

                def rest(s, u, i):
                    act.wait_ge(cl, s)
                    for j in range(E2):
                        act.wait_ge(up, s * E2 + j + 1)
                        nc.scalar.activation(coef[:, j, :], PA[:, j, :], ACT.Gelu).then_inc(ge, 1)
                    act.wait_ge(down, s * TT)
                    act.wait_ge(v_in[u], i * 16 + 16)
                    nc.scalar.activation(v_hi[:, :, :], v_raw[:, u, :, :], ACT.Copy).then_inc(vh, 1)
                    act.wait_ge(gated, s + 2)
                    nc.scalar.activation(c_hi[:, :, :], coef[:, :, :], ACT.Copy).then_inc(ch, 1)

                split_u(0, 0, 0)
                with act.Fori(0, STEPS // 2 - 1) as i:
                    split_u(i * 2 + 1, 1, i)
                    rest(i * 2, 0, i)
                    split_u(i * 2 + 2, 0, i + 1)
                    rest(i * 2 + 1, 1, i)
                split_u(STEPS - 1, 1, STEPS // 2 - 1)
                rest(STEPS - 2, 0, STEPS // 2 - 1)
                rest(STEPS - 1, 1, STEPS // 2 - 1)

            @block.vector
            def _(dve):
                for x, q in enumerate((ul, vl, gated, added)):
                    nc.vector.memset(coef[:, x % 2, 0:8], 0.0).then_inc(q, 1)
                    dve.wait_ge(q, 1)

                def split_u(s, u):
                    dve.wait_ge(uh, s + 1)
                    nc.vector.tensor_tensor(u_lo[:, :, :], u_raw[:, u, :, :], u_hi[:, :, :].bitcast(F32),
                                            ALU.subtract).then_inc(ul, 1)

                def add(s):
                    for t in range(TT):
                        dve.wait_ge(down, s * TT + t + 1)
                        nc.vector.tensor_tensor(acc[:, t, :], acc[:, t, :], PF[:, t % 2, :], ALU.add).then_inc(added, 1)

                def rest(s, u, i):
                    dve.wait_ge(ge, s * E2 + E2)
                    dve.wait_ge(g_in[u], i * 16 + 16)
                    c4 = coef[:, :, :].rearrange("p j (g t) -> p j g t", t=GT)
                    nc.vector.tensor_tensor(c4, c4, gate[:, u, :, :, :].rearrange("p g j t -> p j g t"),
                                            ALU.mult).then_inc(gated, 1)
                    dve.wait_ge(vh, s + 1)
                    nc.vector.tensor_tensor(v_lo[:, :, :], v_raw[:, u, :, :], v_hi[:, :, :].bitcast(F32),
                                            ALU.subtract).then_inc(vl, 1)
                    dve.wait_ge(ch, s + 1)
                    nc.vector.tensor_tensor(c_lo[:, :, :], coef[:, :, :], c_hi[:, :, :].bitcast(F32),
                                            ALU.subtract).then_inc(cl, 1)

                split_u(0, 0)
                split_u(1, 1)
                rest(0, 0, 0)
                with dve.Fori(0, STEPS // 2 - 1) as i:
                    split_u(i * 2 + 2, 0)
                    add(i * 2)
                    rest(i * 2 + 1, 1, i)
                    split_u(i * 2 + 3, 1)
                    add(i * 2 + 1)
                    rest(i * 2 + 2, 0, i + 1)
                add(STEPS - 2)
                rest(STEPS - 1, 1, STEPS // 2 - 1)
                add(STEPS - 1)


def norm_out(nc, sem, A, acc, out, at):
    m = Map(nc, at)
    gamma = m.take("no_gamma", [P, D])
    beta = m.take("no_beta", [P, D])
    stats = m.take("no_stats", [P, 2, 6])
    mv = m.take("no_mv", [P, 4])
    par_in, chain = sem("no_par"), sem("no_chain")
    root, rooted, ready = sem("no_root"), sem("no_rooted"), sem("no_ready")
    y_out = sem("no_out")
    with nc.Block() as block:
        @block.sync
        def _(sp):
            sp.dma_start(gamma[:, :], row(A["ln2_g"])).then_inc(par_in, 16)
            sp.dma_start(beta[:, :], row(A["ln2_b"])).then_inc(par_in, 16)
            o = out.rearrange("b (t p) d -> (b t) p d", p=P)
            for t in range(TT):
                sp.wait_ge(ready, t + 1)
                sp.dma_start(o[t], acc[:, t, :]).then_inc(y_out, 16)
            sp.wait_ge(y_out, 16 * TT)

        @block.vector
        def _(dve):
            dve.wait_ge(par_in, 32)
            c = Chain(dve, chain)
            for t in range(TT):
                layer_norm_tile(dve, c, nc, acc[:, t, :], acc[:, t, :], stats, mv, gamma[:, :], beta[:, :], root,
                                rooted, t).then_inc(ready, 1)

        @block.scalar
        def _(act):
            for t in range(TT):
                act.wait_ge(root, t + 1)
                nc.scalar.activation(mv[:, 3:4], mv[:, 2:3], ACT.Sqrt).then_inc(rooted, 1)


def encoder_block(nc, A, out, stop=None):
    ctx = ExitStack()
    with ctx:
        def sem(name):
            return ctx.enter_context(nc.semaphore(name))

        h_dram = nc.dram_tensor("h_dram", [TT, P, D], F32, kind="Internal").ap()
        g_dram = nc.dram_tensor("g_dram", [P, GROUPS, KEYS, GT], F32, kind="Internal").ap()
        W = KD * T * 4
        base = 16512
        ident_at, ht_at = base, base + 512
        a0 = ht_at + KD * L * 4
        identity = Map(nc, ident_at).take("identity", [P, P])
        hT = Map(nc, ht_at).take("hT", [P, KD, L])
        oall = Map(nc, a0).take("oall", [P, TT, HEADS, P])
        yconv = Map(nc, a0 + W).take("yconv", [P, HEADS, T])
        oT = Map(nc, a0 + 2 * W).take("oT", [P, HEADS, T])
        mT = Map(nc, a0).take("mT", [P, KD, T])
        h1T = Map(nc, a0 + 2 * W).take("h1T", [P, KD, T])
        acc = Map(nc, a0 + 3 * W).take("acc", [P, TT, D])
        picks = Map(nc, 229344 - 3 * T * 4).take("picks", [P, 3, T])
        h_hi = Map(nc, ht_at).take("h_hi", [P, KD, T], F32R)
        h_lo = Map(nc, ht_at + W).take("h_lo", [P, KD, T], F32R)

        norm_in(nc, sem, A, hT, h_dram, identity, a0)
        mix(nc, sem, A, hT, identity, oall, yconv, a0 + 2 * W)
        branch(nc, sem, A, hT, identity, oall, yconv, oT, a0 + 3 * W)
        merge(nc, sem, A, hT, oT, yconv, mT, a0 + 3 * W)
        project(nc, sem, A, mT, identity, h_dram, h1T, acc, a0 + W, a0 + 4 * W)
        route(nc, sem, A, h1T, identity, picks, ht_at, a0 + 4 * W)
        hot_at = ht_at + 2 * W
        gates(nc, sem, A, h1T, h_hi, h_lo, picks, g_dram, hot_at, a0 + 4 * W, hot_at + 16384, 229344 - 3 * T * 4 - 1280)
        experts(nc, sem, A, h_hi, h_lo, acc, g_dram, hot_at, a0 + 4 * W)
        norm_out(nc, sem, A, acc, out, a0 + 4 * W)


def _layout(inputs):
    import numpy as np

    def f(name):
        a = np.asarray(inputs[name])
        return a if name in ("x", "meta", "ln_in_g", "ln_in_b") else a[0]

    def tiles(w, parts):
        n = w.shape[1] // (parts * P)
        return w.reshape(w.shape[0] // P, P, parts, n, P).transpose(3, 1, 0, 2, 4).reshape(n, P, w.shape[0] // P,
                                                                                          parts * P)

    def col(v):
        return v.reshape(-1, P).T

    w, b = f("w_in"), f("b_in")
    q3, c2 = 3 * HEADS * P, 3 * HEADS * P + 2 * D
    pos = np.arange(L, dtype=np.float32)
    inv = np.float32(500000.0) ** (-np.arange(0, 2 * ROT, 2, dtype=np.float32) / np.float32(2 * ROT))
    ang = (pos[:, None] * inv[None, :]).astype(np.float32)
    order = np.concatenate([np.arange(M, L), np.arange(M), np.zeros(P - M, np.int64)])

    def rope(fn):
        return fn(ang).astype(np.float32)[order].reshape(TT + 1, P, ROT).transpose(1, 0, 2)

    return {
        "x": f("x"), "meta": f("meta"), "ln_in_g": f("ln_in_g"), "ln_in_b": f("ln_in_b"),
        "w_qkv": tiles(w[:, :q3], 3), "w_glu": tiles(w[:, q3:c2], 2), "w_gate": tiles(w[:, c2:], 2),
        "b_qkv": b[:q3].reshape(3, HEADS, P).transpose(1, 0, 2).reshape(HEADS, 3 * P),
        "chan": np.stack([col(v) for v in (b[q3:q3 + D], b[q3 + D:c2], b[c2:c2 + D], b[c2 + D:], f("dw_bias"),
                                           f("conv_ln_g"), f("conv_ln_b"), f("b_conv_proj"))], axis=1),
        "taps": f("dw_kernel").reshape(TAPS, HEADS, P).transpose(2, 1, 0),
        "lambda_q1": f("lambda_q1"), "lambda_k1": f("lambda_k1"), "lambda_q2": f("lambda_q2"),
        "lambda_k2": f("lambda_k2"), "subln_col": f("subln_g").reshape(P, 1),
        "w_attn": tiles(f("w_attn_proj"), 1), "w_conv": tiles(f("w_conv_proj"), 1),
        "w_out": f("w_out").reshape(KD, P, D).transpose(1, 0, 2),
        "b_out": f("b_out"), "ln1_g": f("ln1_g"), "ln1_b": f("ln1_b"), "ln2_g": f("ln2_g"), "ln2_b": f("ln2_b"),
        "w_query": f("peer_wq").reshape(KD, P, 2 * HEADS, P).transpose(1, 2, 0, 3),
        "subkeys": f("peer_subkeys").reshape(2 * HEADS, KEYS, P).transpose(2, 0, 1),
        "u_t": f("peer_u").reshape(STEPS, E2, KEYS, KD, P).transpose(0, 4, 3, 1, 2).reshape(STEPS, P, KD, E2 * P),
        "v": f("peer_v").reshape(STEPS, E2, P, D),
        "rope_cos": rope(np.cos), "rope_sin": rope(np.sin),
        "identity": np.eye(P, dtype=np.float32),
        "iota": np.broadcast_to(np.arange(KEYS, dtype=np.float32), (P, KEYS)),
    }


def kernel(**inputs):
    import numpy as np
    import concourse.bacc as bacc
    from concourse.bass_utils import run_bass_kernel_spmd

    nc = bacc.Bacc("TRN2", target_bir_lowering=False, num_devices=1)
    arrays, args = {}, {}
    for name, a in _layout(inputs).items():
        a = np.ascontiguousarray(a)
        arrays[f"in_{name}"] = a
        args[name] = nc.dram_tensor(f"in_{name}", a.shape, mybir.dt.from_np(a.dtype), kind="ExternalInput").ap()
    out = nc.dram_tensor("out", (1, T, D), F32, kind="ExternalOutput").ap()
    encoder_block(nc, args, out)
    r = run_bass_kernel_spmd(nc, [arrays], core_ids=[0])
    return r.results[0]["out"]
```

```python
import math
from contextlib import ExitStack

import concourse.bass as bass
from concourse import mybir

F32 = mybir.dt.float32
F32R = mybir.dt.float32r
BF16 = mybir.dt.bfloat16
U32 = mybir.dt.uint32
ACT = mybir.ActivationFunctionType
ALU = mybir.AluOpType
AX = mybir.AxisListType
ds = bass.ds

P = 128
D = 1024
KD = D // P
T = 1024
TT = T // P
M = 16
L = T + M
CHUNK = 64
HEADS = 8
HD = 64
ROT = HD // 8
TAPS = 31
PAD = TAPS - 1
K = 16
KEYS = 128
E2 = 2
STEPS = KEYS // E2
AHEAD = 2 * TT + 16
GT = 64
GROUPS = T // GT
LN_EPS = 1e-5
ALPHA = 2.0 ** 0.25
LAM_INIT = 0.8 - 0.6 * math.exp(0.0)
BANK = 512
LOWEST = -3.0e38
O_LIMIT = 1.6e18


class Chain:

    def __init__(self, eng, sem, base=0):
        self.eng, self.sem, self.base, self.n = eng, sem, base, 0

    def mark(self, ins):
        ins.then_inc(self.sem, 1)
        self.n += 1
        return self.base + self.n

    def then(self, ins, apart=False):
        self.eng.wait_ge(self.sem, self.mark(ins))
        if apart:
            self.eng.nop(nofuse=True)



class Map:

    def __init__(self, nc, at=0):
        self.nc, self.at = nc, at

    def take(self, name, shape, dt=F32):
        n = 2 if dt == BF16 else 4
        for s in shape[1:]:
            n *= s
        h = self.nc.alloc_sbuf_tensor_at(name, shape, dt, offset=self.at)
        self.at += (n + 31) // 32 * 32
        return h


def row(ap, n=P):
    return ap.rearrange("(o d) -> o d", o=1).to_broadcast([n, ap.shape[0]])


def matmul3(nc, out, ws, xs, n):
    for a in range(n):
        for j, (w, x) in enumerate(((ws[0], xs[0]), (ws[0], xs[1]), (ws[1], xs[0]))):
            ins = nc.tensor.matmul(out, w(a), x(a), start=(a == 0 and j == 0), stop=(a == n - 1 and j == 2))
    return ins


def norm_in(nc, sem, A, hT, h_dram, identity, at):
    m = Map(nc, at)
    xin = m.take("xin", [P, 2, D])
    xn = m.take("xn", [P, 2, D])
    gamma = m.take("ni_gamma", [P, D])
    beta = m.take("ni_beta", [P, D])
    stats = m.take("ni_stats", [P, 2, 6])
    mv = m.take("ni_mv", [P, 2])
    std = m.take("ni_std", [P, 2])
    hT_hi, hT_lo = hT
    with nc.psum_tensor("ni_tp", [P, 4, BANK], F32) as tp:
        const_in = sem("ni_const_in")
        x_in = [sem("ni_x_in0"), sem("ni_x_in1")]
        x_used = sem("ni_x_used")
        chain = sem("ni_chain")
        var_ready = sem("ni_var")
        std_ready = sem("ni_std_s")
        gb = sem("ni_gamma_done")
        xn_ready = sem("ni_xn")
        tr_done = sem("ni_tr")
        hi_done = sem("ni_hi")
        lo_done = sem("ni_lo")
        h_out = [sem("ni_h_out0"), sem("ni_h_out1")]
        x_t = A["x"].rearrange("b (t p) d -> (b t) p d", p=P)
        PER = 3

        def half(t, u, f, n):
            at = 0 if n == M else t * P + M
            return (tp[:, 2 * u + f, :].rearrange("p (k c) -> p k c", k=4)[:, :, 0:n],
                    hT_hi[:, 4 * f:4 * f + 4, ds(at, n)], hT_lo[:, 4 * f:4 * f + 4, ds(at, n)])

        with nc.Block() as block:
            @block.sync
            def _(sp):
                sp.dma_start(gamma[:, :], row(A["ln_in_g"])).then_inc(const_in, 16)
                sp.dma_start(beta[:, :], row(A["ln_in_b"])).then_inc(const_in, 16)
                sp.dma_start(identity[:, :], A["identity"]).then_inc(const_in, 16)
                with sp.Fori(0, TT // 2) as i:
                    for u in range(2):
                        sp.wait_ge(x_used, i * 2 + u)
                        sp.dma_start(xin[:, u, :], x_t[ds(i * 2 + u, 1)].rearrange("o p d -> (o p) d")
                                     ).then_inc(x_in[u], 16)
                sp.wait_ge(x_used, TT)
                sp.dma_start(xin[0:M, 0, :], A["meta"]).then_inc(x_in[0], 16)

            @block.gpsimd
            def _(pool):
                with pool.Fori(0, TT // 2) as i:
                    for u in range(2):
                        pool.wait_ge(xn_ready, i * 2 + u + 1)
                        pool.nop(nofuse=True)
                        pool.dma_start(h_dram[ds(i * 2 + u, 1)].rearrange("o p d -> (o p) d"), xn[:, u, :]
                                       ).then_inc(h_out[u], 16)
                for u in range(2):
                    pool.wait_ge(h_out[u], 16 * TT // 2)

            @block.vector
            def _(dve):
                def normalise(t, u, i, n):
                    c = Chain(dve, chain, t * PER)
                    dve.wait_ge(x_in[u], i * 16 + 16)
                    nc.vector.bn_stats(stats[0:n, 0, :], xin[0:n, u, 0:BANK])
                    c.then(nc.vector.bn_stats(stats[0:n, 1, :], xin[0:n, u, BANK:D]), apart=True)
                    c.then(nc.vector.bn_aggr(mv[0:n, :], stats[0:n, :, :].rearrange("p a b -> p (a b)")))
                    nc.vector.tensor_scalar(std[0:n, 0:1], mv[0:n, 1:2], LN_EPS, None,
                                            ALU.add).then_inc(var_ready, 1)
                    dve.wait_ge(std_ready, t + 1)
                    c.then(nc.vector.reciprocal(std[0:n, 1:2], std[0:n, 1:2]))
                    dve.wait_ge(h_out[u], i * 16)
                    nc.vector.tensor_scalar(xn[0:n, u, :], xin[0:n, u, :], mv[0:n, 0:1], std[0:n, 1:2],
                                            ALU.subtract, ALU.mult).then_inc(x_used, 1)
                    dve.wait_ge(x_used, t + 2)
                    nc.vector.tensor_tensor(xn[0:n, u, :], xn[0:n, u, :], gamma[0:n, :], ALU.mult).then_inc(gb, 1)
                    dve.wait_ge(gb, t + 1)
                    nc.vector.tensor_tensor(xn[0:n, u, :], xn[0:n, u, :], beta[0:n, :],
                                            ALU.add).then_inc(xn_ready, 1)

                def low(t, u, n):
                    for f in range(2):
                        ps, hi, lo = half(t, u, f, n)
                        dve.wait_ge(hi_done, t * 2 + f + 1)
                        nc.vector.tensor_tensor(lo, ps, hi.bitcast(F32), ALU.subtract).then_inc(lo_done, 1)

                nc.vector.memset(stats[:, :, :], 0.0).then_inc(x_used, 1)
                dve.wait_ge(x_used, 1)
                nc.vector.memset(mv[:, :], 0.0).then_inc(lo_done, 4)
                dve.wait_ge(lo_done, 4)
                dve.wait_ge(const_in, 48)
                normalise(0, 0, 0, P)
                with dve.Fori(0, TT // 2 - 1) as i:
                    normalise(i * 2 + 1, 1, i, P)
                    low(i * 2, 0, P)
                    normalise(i * 2 + 2, 0, i + 1, P)
                    low(i * 2 + 1, 1, P)
                normalise(TT - 1, 1, TT // 2 - 1, P)
                low(TT - 2, 0, P)
                normalise(TT, 0, TT // 2, M)
                low(TT - 1, 1, P)
                low(TT, 0, M)

            @block.scalar
            def _(act):
                def root(t, n):
                    act.wait_ge(var_ready, t + 1)
                    nc.scalar.activation(std[0:n, 1:2], std[0:n, 0:1], ACT.Sqrt).then_inc(std_ready, 1)

                def high(t, u, n):
                    for f in range(2):
                        ps, hi, _ = half(t, u, f, n)
                        act.wait_ge(tr_done, t * 2 + f + 1)
                        act.nop(nofuse=True)
                        nc.scalar.activation(hi, ps, ACT.Copy).then_inc(hi_done, 1)

                root(0, P)
                with act.Fori(0, TT // 2 - 1) as i:
                    for u in range(2):
                        root(i * 2 + u + 1, P)
                        high(i * 2 + u, u, P)
                root(TT - 1, P)
                high(TT - 2, 0, P)
                root(TT, M)
                high(TT - 1, 1, P)
                high(TT, 0, M)

            @block.tensor
            def _(pe):
                def turn(t, u, n):
                    pe.wait_ge(xn_ready, t + 1)
                    for f in range(2):
                        pe.wait_ge(lo_done, t * 2 + f + 1)
                        for k in range(4):
                            ins = nc.tensor.transpose(tp[:, 2 * u + f, k * P:k * P + n],
                                                      xn[0:n, u, (4 * f + k) * P:(4 * f + k + 1) * P],
                                                      identity[0:n, 0:n])
                        ins.then_inc(tr_done, 1)

                pe.wait_ge(const_in, 48)
                with pe.Fori(0, TT // 2) as i:
                    for u in range(2):
                        turn(i * 2 + u, u, P)
                turn(TT, 0, M)


def mix(nc, sem, A, hT, identity, o_dram, y_dram, at):
    m = Map(nc, at)
    w_raw = m.take("w_raw", [P, KD, 3 * P])
    w_head = [m.take(f"w_head{j}", [P, KD, 3 * P], F32R) for j in range(2)]
    g_raw = m.take("g_raw", [P, KD, 2 * P])
    w_glu = [m.take(f"w_glu{j}", [P, KD, 2 * P], F32R) for j in range(2)]
    b_head = m.take("b_head", [P, 3 * P])
    qkv = m.take("qkv", [P, TT + 1, 3 * P])
    qT = m.take("qT", [P, T])
    kT = m.take("kT", [P, L])
    prob = m.take("prob", [P, 2, 2, L])
    mixed = m.take("mixed", [P, L])
    v_use = m.take("v_use", [P, TT + 1, P])
    mixT = m.take("mixT", [P, T])
    mixTm = m.take("mixTm", [M, P])
    glu_t = m.take("glu_t", [P, L])
    glu_a = m.take("glu_a", [P, L])
    u_pad = m.take("u_pad", [P, PAD + L])
    y_sum = m.take("y_sum", [P, T])
    o_head = m.take("o_head", [P, TT, P])
    cos_t = m.take("cos_t", [P, TT + 1, ROT])
    sin_t = m.take("sin_t", [P, TT + 1, ROT])
    rot = m.take("rot", [P, 4, (TT + 1) * 4 * ROT])
    negmax = m.take("negmax", [P, 4])
    sums = m.take("sums", [P, 4])
    rr = m.take("rr", [P, 2])
    lamv = m.take("lamv", [P, 4, HD])
    lamp = m.take("lamp", [P, 2, HD])
    lam = m.take("lam", [P, 4])
    glu_b = m.take("glu_b", [P, 2, HEADS])
    glu_h = m.take("glu_h", [P, 2, HEADS])
    taps_w = m.take("taps_w", [P, HEADS, TAPS])
    taps_b = m.take("taps_b", [P, HEADS])

    nbatch = [(i + 4) // 4 for i in range(TT)]
    before = [sum(nbatch[:i]) + i for i in range(TT + 1)]
    NB = before[TT]
    DVE_PER = TAPS + 2 * TT + 3 * TT
    GLU = [(part, c0, n) for part in (1, 0) for c0, n in ((0, BANK), (BANK, BANK), (T, M))]
    NG = len(GLU)
    NP = TT + 1
    LAST = HEADS - 1

    def pieces(start, n):
        out, c = [], start
        while c < start + n:
            e = min(start + n, c // BANK * BANK + BANK)
            out.append((c, e - c))
            c = e
        return out

    with nc.psum_tensor("mx_s", [P, 5 * BANK], F32) as S, nc.psum_tensor("mx_t", [P, BANK], F32) as TB, \
            nc.psum_tensor("mx_o", [P, BANK], F32) as OB, nc.psum_tensor("mx_p", [P, BANK], F32) as PB:
        tab_in = sem("mx_tables_in")
        w_in, b_in, g_in = sem("mx_w_in"), sem("mx_b_in"), sem("mx_g_in")
        wh, wl = sem("mx_wh"), sem("mx_wl")
        gh, gl = sem("mx_gh"), sem("mx_gl")
        y_done, y_out = sem("mx_y_done"), sem("mx_y_out")
        o_out = sem("mx_o_out")
        pj, pj_ev = sem("mx_pj"), sem("mx_pj_ev")
        cv, cv_ev = sem("mx_cv"), sem("mx_cv_ev")
        v_kept = sem("mx_v_kept")
        u_done = sem("mx_u")
        roped = sem("mx_roped")
        tq, tq_ev = sem("mx_tq"), sem("mx_tq_ev")
        s_done, mx_done, ex_done = sem("mx_s_done"), sem("mx_mx"), sem("mx_ex")
        map0 = sem("mx_map0")
        w_done = sem("mx_w_done")
        wt, wt_ev = sem("mx_wt"), sem("mx_wt_ev")
        o_done, o_ev = sem("mx_o_done"), sem("mx_o_ev")
        chain = sem("mx_chain")
        pre = sem("mx_pre")
        lam_e = sem("mx_lam_e")
        init = sem("mx_init")

        with nc.Block() as block:
            @block.sync
            def _(sp):
                def load_w(h):
                    sp.dma_start(w_raw[:, :, :], A["w_qkv"][ds(h, 1)].rearrange("o p k c -> (o p) k c")
                                 ).then_inc(w_in, 16)

                def load_g(h):
                    sp.dma_start(g_raw[:, :, :], A["w_glu"][ds(h, 1)].rearrange("o p k c -> (o p) k c")
                                 ).then_inc(g_in, 16)

                def load_bias(h):
                    sp.dma_start(b_head[:, :], A["b_qkv"][ds(h, 1), :].to_broadcast([P, 3 * P])).then_inc(b_in, 16)

                load_g(0)
                load_w(0)
                load_bias(0)
                for dst, src in ((cos_t[:, :, :], A["rope_cos"]), (sin_t[:, :, :], A["rope_sin"]),
                                 (glu_b[:, :, :], A["chan"][:, 0:2, :]), (taps_b[:, :], A["chan"][:, 4, :]),
                                 (taps_w[:, :, :], A["taps"]),
                                 (lamv[:, 0, :], row(A["lambda_q1"])), (lamv[:, 1, :], row(A["lambda_k1"])),
                                 (lamv[:, 2, :], row(A["lambda_q2"])), (lamv[:, 3, :], row(A["lambda_k2"]))):
                    sp.dma_start(dst, src).then_inc(tab_in, 16)
                sp.wait_ge(gl, 1)
                load_g(1)
                sp.wait_ge(wl, 1)
                load_w(1)
                with sp.Fori(0, HEADS - 2) as h:
                    sp.wait_ge(pj_ev, h * NP + NP)
                    load_bias(h + 1)
                    sp.wait_ge(gl, h + 2)
                    load_g(h + 2)
                    sp.wait_ge(wl, h + 2)
                    load_w(h + 2)
                sp.wait_ge(pj_ev, LAST * NP)
                load_bias(LAST)
                sp.wait_ge(gl, HEADS)
                load_g(LAST)

            @block.gpsimd
            def _(pool):
                with pool.Fori(0, HEADS) as h:
                    pool.wait_ge(y_done, h + 1)
                    pool.nop(nofuse=True)
                    pool.dma_start(y_dram[ds(h, 1)].rearrange("o p t -> (o p) t"), y_sum[:, :]).then_inc(y_out, 16)
                    pool.wait_ge(o_ev, h * TT + TT)
                    pool.nop(nofuse=True)
                    pool.dma_start(o_dram[ds(h, 1)].rearrange("o p t c -> (o p) (t c)"),
                                   o_head[:, :, :].rearrange("p t c -> p (t c)")).then_inc(o_out, 16)
                pool.wait_ge(y_out, 16 * HEADS)
                pool.wait_ge(o_out, 16 * HEADS)

            @block.tensor
            def _(pe):
                def glu_unit(g, k, first=False):
                    part, c0, n = GLU[k]
                    if k:
                        pe.wait_ge(cv_ev, g * NG + k)
                    else:
                        pe.wait_ge(gl, g + 1)
                        if not first:
                            pe.wait_ge(pj_ev, g * NP)
                    matmul3(nc, PB[:, 0:n], [lambda k, x=x: x[:, k, part * P:part * P + P] for x in w_glu],
                            [lambda k, x=x: x[:, k, c0:c0 + n] for x in hT], KD).then_inc(cv, 1)

                def proj_unit(g, t):
                    if t:
                        pe.wait_ge(pj_ev, g * NP + t)
                    else:
                        pe.wait_ge(wl, g + 1)
                        pe.wait_ge(cv_ev, g * NG + NG)
                    c0 = t * P + M if t < TT else 0
                    matmul3(nc, PB[:, 0:3 * P], [lambda k, x=x: x[:, k, c0:c0 + P] for x in hT],
                            [lambda k, x=x: x[:, k, :] for x in w_head], KD).then_inc(pj, 1)

                def scores(h, i):
                    nfr = (i + 1) * P
                    for mp in range(2):
                        r = slice(mp * HD, mp * HD + HD)
                        if i == 0:
                            pe.wait_ge(ex_done, h * 16)
                        elif i < TT - 1:
                            pe.wait_ge(ex_done, h * 16 + 2 * (i - 1) + mp + 1)
                        elif mp == 0:
                            pe.wait_ge(ex_done, h * 16 + 2 * i)
                        else:
                            pe.wait_ge(map0, h + 1)
                        for c, n in pieces(mp * L, nfr):
                            k0 = c - mp * L
                            nc.tensor.matmul(S[:, c:c + n], qT[r, i * P:i * P + P], kT[r, k0:k0 + n], start=True,
                                             stop=True)
                        c = mp * L + nfr
                        ins = nc.tensor.matmul(S[:, c:c + M], qT[r, i * P:i * P + P], kT[r, T:L], start=True,
                                               stop=True)
                        if i < TT - 1:
                            ins.then_inc(s_done, 1)
                        elif mp == 0:
                            ins.then_inc(map0, 1)
                        else:
                            ins.then_inc(s_done, 2)

                def attend(h, last):
                    g = h + 1
                    if not last:
                        for k in range(3):
                            glu_unit(g, k)
                    pe.wait_ge(roped, h + 1)
                    pe.wait_ge(wt_ev, h * NB)
                    pe.wait_ge(o_ev, h * TT)
                    for b in range(5):
                        bank = OB if b % 2 else TB
                        if b >= 2:
                            pe.wait_ge(tq_ev, h * 5 + b - 1)
                        if b == 4:
                            pe.nop(nofuse=True)
                            ins = nc.tensor.transpose(bank[:, 0:M], qkv[0:M, TT, P:2 * P], identity[0:M, 0:M])
                        else:
                            for c in range(4):
                                ins = nc.tensor.transpose(bank[:, c * P:c * P + P],
                                                          qkv[:, b % 2 * 4 + c, b // 2 * P:b // 2 * P + P],
                                                          identity[:, :])
                        ins.then_inc(tq, 1)
                    pe.wait_ge(tq_ev, h * 5 + 5)
                    scores(h, 0)
                    if not last:
                        glu_unit(g, 3)
                    pe.wait_ge(v_kept, h + 1)
                    for i in range(TT):
                        if i + 1 < TT:
                            scores(h, i + 1)
                        pe.wait_ge(w_done, h * TT + i + 1)
                        seen = h * NB + before[i]
                        pe.wait_ge(wt_ev, seen)
                        pe.wait_ge(o_ev, h * TT + i)
                        for b in range(nbatch[i]):
                            if b:
                                pe.wait_ge(wt_ev, seen + 1)
                            for j in range(4 * b, min(4 * b + 4, i + 1)):
                                ins = nc.tensor.transpose(TB[:, j % 4 * P:j % 4 * P + P],
                                                          mixed[:, j * P:j * P + P], identity[:, :])
                            ins.then_inc(wt, 1)
                            if b == 0:
                                nc.tensor.transpose(OB[0:M, 3 * P:4 * P], mixed[:, (i + 1) * P:(i + 1) * P + M],
                                                    identity[:, :]).then_inc(wt, 1)
                                if not last and i == 0:
                                    glu_unit(g, 4)
                                elif not last:
                                    proj_unit(g, i if i == 1 else i + 1)
                        pe.wait_ge(wt_ev, seen + 2)
                        nc.tensor.matmul(OB[:, 0:P], mixTm[:, :], v_use[0:M, TT, :], start=True, stop=False)
                        for j in range(i + 1):
                            if j == 4:
                                pe.wait_ge(wt_ev, seen + 3)
                            ins = nc.tensor.matmul(OB[:, 0:P], mixT[:, j * P:j * P + P], v_use[:, j, :],
                                                   start=False, stop=(j == i))
                        ins.then_inc(o_done, 1)
                        if not last and i == 0:
                            glu_unit(g, 5)
                            proj_unit(g, 0)
                        elif not last and i == 1:
                            proj_unit(g, 2)

                for k in range(NG):
                    glu_unit(0, k, first=True)
                for t in range(NP):
                    proj_unit(0, t)
                with pe.Fori(0, LAST) as h:
                    attend(h, False)
                attend(LAST, True)

            @block.scalar
            def _(act):
                def high_w(n):
                    act.wait_ge(w_in, n * 16 + 16)
                    act.wait_ge(pj, n * NP)
                    nc.scalar.activation(w_head[0][:, :, :], w_raw[:, :, :], ACT.Copy).then_inc(wh, 1)

                def high_g(n):
                    act.wait_ge(g_in, n * 16 + 16)
                    act.wait_ge(cv, n * NG)
                    nc.scalar.activation(w_glu[0][:, :, :], g_raw[:, :, :], ACT.Copy).then_inc(gh, 1)

                def glu_out(g, k):
                    part, c0, n = GLU[k]
                    act.wait_ge(cv, g * NG + k + 1)
                    act.nop(nofuse=True)
                    if part:
                        nc.scalar.activation(glu_t[:, c0:c0 + n], PB[:, 0:n], ACT.Tanh,
                                             bias=glu_h[:, 1, ds(g, 1)], scale=0.5).then_inc(cv_ev, 1)
                    else:
                        nc.scalar.activation(glu_a[:, c0:c0 + n], PB[:, 0:n], ACT.Identity,
                                             bias=glu_h[:, 0, ds(g, 1)], scale=0.5).then_inc(cv_ev, 1)

                def exps(h, i):
                    n = (i + 1) * P + M
                    act.wait_ge(w_done, h * TT + max(i - 1, 0))
                    for mp in range(2):
                        c = i % 2 * 2 + mp
                        act.wait_ge(mx_done, h * 16 + 2 * i + (mp + 1 if i < TT - 1 else 2))
                        nc.scalar.activation(prob[:, i % 2, mp, 0:n], S[:, mp * L:mp * L + n], ACT.Exp,
                                             bias=negmax[:, c:c + 1],
                                             accum_out=sums[:, c:c + 1]).then_inc(ex_done, 1)

                def attend(h, last):
                    g = h + 1
                    if not last:
                        high_w(g)
                        act.wait_ge(u_done, h + 1)
                        glu_out(g, 0)
                    act.wait_ge(pj_ev, h * NP + NP)
                    act.wait_ge(o_done, h * TT)
                    nc.scalar.activation(v_use[:, :, :], qkv[:, :, 2 * P:3 * P], ACT.Copy).then_inc(v_kept, 1)
                    if not last:
                        glu_out(g, 1)
                        glu_out(g, 2)
                    act.wait_ge(s_done, h * 16)
                    for b in range(5):
                        act.wait_ge(tq, h * 5 + b + 1)
                        bank = OB if b % 2 else TB
                        if b == 4:
                            nc.scalar.activation(kT[:, T:L], bank[:, 0:M], ACT.Copy).then_inc(tq_ev, 1)
                        else:
                            dst = (kT if b // 2 else qT)[:, b % 2 * BANK:b % 2 * BANK + BANK]
                            nc.scalar.activation(dst, bank[:, :], ACT.Copy,
                                                 scale=1.0 if b // 2 else HD ** -0.5).then_inc(tq_ev, 1)
                    exps(h, 0)
                    if not last:
                        glu_out(g, 3)
                    act.wait_ge(o_out, h * 16)
                    for i in range(TT):
                        act.wait_ge(o_done, h * TT + i)
                        seen = h * NB + before[i]
                        act.wait_ge(wt, seen + 1)
                        n = min(4, i + 1) * P
                        nc.scalar.activation(mixT[:, 0:n], TB[:, 0:n], ACT.Copy).then_inc(wt_ev, 1)
                        act.wait_ge(wt, seen + 2)
                        nc.scalar.activation(mixTm[:, :], OB[0:M, 3 * P:4 * P], ACT.Copy).then_inc(wt_ev, 1)
                        if i + 1 < TT:
                            exps(h, i + 1)
                        if nbatch[i] == 2:
                            act.wait_ge(wt, seen + 3)
                            n = (i - 3) * P
                            nc.scalar.activation(mixT[:, BANK:BANK + n], TB[:, 0:n], ACT.Copy).then_inc(wt_ev, 1)
                        if not last and i == 0:
                            glu_out(g, 4)
                        act.wait_ge(o_done, h * TT + i + 1)
                        nc.scalar.activation(o_head[:, i, :], OB[:, 0:P], ACT.Copy).then_inc(o_ev, 1)
                        if not last and i == 0:
                            glu_out(g, 5)
                        if not last and i == 2:
                            high_g(g + 1)

                high_g(0)
                high_w(0)
                act.wait_ge(pre, 2)
                nc.scalar.activation(lam[:, 0:2], lam[:, 0:2], ACT.Exp).then_inc(lam_e, 1)
                act.wait_ge(pre, 3)
                for k in range(NG):
                    glu_out(0, k)
                high_g(1)
                with act.Fori(0, LAST) as h:
                    attend(h, False)
                attend(LAST, True)

            @block.vector
            def _(dve):
                def low_w(n):
                    dve.wait_ge(wh, n + 1)
                    nc.vector.tensor_tensor(w_head[1][:, :, :], w_raw[:, :, :], w_head[0][:, :, :].bitcast(F32),
                                            ALU.subtract).then_inc(wl, 1)

                def low_g(n):
                    dve.wait_ge(gh, n + 1)
                    nc.vector.tensor_tensor(w_glu[1][:, :, :], g_raw[:, :, :], w_glu[0][:, :, :].bitcast(F32),
                                            ALU.subtract).then_inc(gl, 1)

                def proj_out(g, t):
                    n = P if t < TT else M
                    dve.wait_ge(pj, g * NP + t + 1)
                    nc.vector.tensor_tensor(qkv[0:n, t, :], PB[0:n, 0:3 * P], b_head[0:n, :],
                                            ALU.add).then_inc(pj_ev, 1)

                def tap(c, h, k):
                    if k == 0:
                        dve.wait_ge(u_done, h + 1)
                        dve.wait_ge(y_out, h * 16)
                        c.then(nc.vector.tensor_scalar(y_sum[:, :], u_pad[:, M:M + T], taps_w[:, ds(h, 1), 0],
                                                       taps_b[:, ds(h, 1)], ALU.mult, ALU.add))
                        return
                    ins = nc.vector.scalar_tensor_tensor(y_sum[:, :], u_pad[:, M + k:M + k + T],
                                                         taps_w[:, ds(h, 1), k], y_sum[:, :], ALU.mult, ALU.add)
                    if k == TAPS - 1:
                        ins.then_inc(y_done, 1)
                    else:
                        c.then(ins)

                def maxes(c, h, i):
                    nfr = (i + 1) * P
                    for mp in range(2):
                        dve.wait_ge(s_done, h * 16 + 2 * i + mp + 1)
                        s = S[:, mp * L:mp * L + nfr + M]
                        c.then(nc.vector.memset(s[0:CHUNK, nfr - CHUNK:nfr], -1e30))
                        q = i % 2 * 2 + mp
                        nc.vector.tensor_reduce(negmax[:, q:q + 1], s, AX.X, ALU.max, negate=True).then_inc(mx_done, 1)

                def attend(h, last):
                    g = h + 1
                    c = Chain(dve, chain, h * DVE_PER)
                    dve.wait_ge(pj_ev, h * NP + NP)
                    qk = qkv[:, :, 0:2 * P].rearrange("p t (x d) -> p t x d", d=HD)
                    r1, r2 = qk[:, :, :, 0:ROT], qk[:, :, :, ROT:2 * ROT]
                    bc = [x[:, :, :].unsqueeze(2).to_broadcast([P, TT + 1, 4, ROT]) for x in (cos_t, sin_t)]
                    tmp = [rot[:, j, :].rearrange("p (t x d) -> p t x d", t=TT + 1, x=4) for j in range(4)]
                    for j, (a, b) in enumerate(((r1, bc[0]), (r2, bc[1]), (r2, bc[0]), (r1, bc[1]))):
                        ins = nc.vector.tensor_tensor(tmp[j], a, b, ALU.mult)
                    c.then(ins)
                    nc.vector.tensor_tensor(r1, tmp[0], tmp[1], ALU.subtract)
                    nc.vector.tensor_tensor(r2, tmp[2], tmp[3], ALU.add).then_inc(roped, 1)
                    dve.wait_ge(cv_ev, h * NG + NG)
                    dve.wait_ge(y_done, h)
                    nc.vector.scalar_tensor_tensor(u_pad[:, PAD:PAD + L], glu_t[:, :], 1.0, glu_a[:, :],
                                                   ALU.add, ALU.mult).then_inc(u_done, 1)
                    if not last:
                        low_w(g)
                    k = 3
                    for j in range(k):
                        tap(c, h, j)
                    maxes(c, h, 0)
                    for i in range(TT):
                        n = (i + 1) * P + M
                        q = i % 2 * 2
                        dve.wait_ge(w_done, h * TT + i)
                        dve.wait_ge(ex_done, h * 16 + 2 * i + 2)
                        c.then(nc.vector.reciprocal(rr[:, :], sums[:, q:q + 2]))
                        c.then(nc.vector.tensor_tensor(rr[:, 1:2], rr[:, 1:2], lam[:, 3:4], ALU.mult))
                        second = prob[:, i % 2, 1, 0:n]
                        c.then(nc.vector.tensor_scalar(second, second, rr[:, 1:2], None, ALU.mult))
                        dve.wait_ge(wt, h * NB + before[i])
                        nc.vector.scalar_tensor_tensor(mixed[:, 0:n], prob[:, i % 2, 0, 0:n], rr[:, 0:1],
                                                       second, ALU.mult, ALU.subtract).then_inc(w_done, 1)
                        if not last and i == 1:
                            dve.wait_ge(tq, h * 5 + 5)
                            dve.wait_ge(v_kept, h + 1)
                            dve.wait_ge(b_in, g * 16 + 16)
                            proj_out(g, 0)
                        if not last and i == 2:
                            proj_out(g, 2)
                        if i + 1 < TT:
                            maxes(c, h, i + 1)
                        more = (TAPS - k) // (TT - i)
                        for j in range(k, k + more):
                            tap(c, h, j)
                        k += more
                        if not last and i >= 1:
                            proj_out(g, i if i == 1 else i + 1)
                        if not last and i == 3:
                            low_g(g + 1)
                    assert k == TAPS and c.n == DVE_PER, (k, c.n)

                nc.vector.memset(qkv[:, TT, :], 0.0).then_inc(init, 1)
                nc.vector.memset(u_pad[:, :], 0.0).then_inc(init, 1)
                dve.wait_ge(init, 2)
                low_g(0)
                low_w(0)
                dve.wait_ge(tab_in, 9 * 16)
                c0 = Chain(dve, sem("mx_lam_chain"))
                c0.then(nc.vector.tensor_tensor(lamp[:, :, :], lamv[:, 0:4:2, :], lamv[:, 1:4:2, :], ALU.mult))
                nc.vector.tensor_reduce(lam[:, 0:2], lamp[:, :, :], AX.X, ALU.add).then_inc(pre, 2)
                nc.vector.tensor_scalar(glu_h[:, :, :], glu_b[:, :, :], 0.5, None, ALU.mult).then_inc(pre, 1)
                dve.wait_ge(lam_e, 1)
                c0.then(nc.vector.tensor_tensor(lam[:, 2:3], lam[:, 0:1], lam[:, 1:2], ALU.subtract))
                c0.then(nc.vector.tensor_scalar(lam[:, 3:4], lam[:, 2:3], LAM_INIT, None, ALU.add))
                dve.wait_ge(b_in, 16)
                for t in range(NP):
                    proj_out(0, t)
                low_g(1)
                with dve.Fori(0, LAST) as h:
                    attend(h, False)
                attend(LAST, True)


def branch(nc, sem, A, identity, o_dram, y_dram, yconv, oT, at):
    m = Map(nc, at)
    oall = m.take("oall", [P, HEADS, TT, P])
    sq = m.take("br_sq", [P, 2, TT, P])
    ms = m.take("br_ms", [P, 5, TT * HEADS])
    sub_g = m.take("br_g", [P, 2])
    chan = m.take("br_chan", [P, 2, HEADS])
    ones = m.take("br_ones", [P, P])
    sqc = m.take("br_sqc", [P, 2, T])
    rstd = m.take("br_rstd", [P, T])
    eps = m.take("br_eps", [P, 1])
    with nc.psum_tensor("br_t", [P, 2, BANK], F32) as TB, nc.psum_tensor("br_mean", [P, T], F32) as MEAN, \
            nc.psum_tensor("br_var", [P, T], F32) as VAR:
        y_in = [sem(f"br_y_in{j}") for j in range(4)]
        o_in = [sem(f"br_o_in{j}") for j in range(HEADS)]
        eps_ready = sem("br_eps_ready")
        par_in = sem("br_par")
        ready = sem("br_ones_ready")
        chain = sem("br_chain")
        root = sem("br_root")
        rooted = sem("br_rooted")
        g8 = sem("br_g8")
        summed, small_sq = sem("br_summed"), sem("br_small_sq")
        o_norm = sem("br_o_norm")
        mean_done = sem("br_mean_s")
        cent = sem("br_cent")
        sq_done = sem("br_sq_done")
        var_done = sem("br_var_s")
        tr, tr_ev = sem("br_tr"), sem("br_tr_ev")
        z_done = sem("br_z")
        NH = TT * HEADS
        with nc.Block() as block:
            @block.sync
            def _(sp):
                for h in range(HEADS):
                    sp.dma_start(yconv[:, h, :], y_dram[h]).then_inc(y_in[h % 4], 16)
                for h in range(HEADS):
                    sp.dma_start(oall[:, h, :, :], o_dram[h]).then_inc(o_in[h], 16)
                sp.dma_start(sub_g[:, 0:1], A["subln_col"]).then_inc(par_in, 16)
                sp.dma_start(chan[:, :, :], A["chan"][:, 5:7, :]).then_inc(par_in, 16)

            @block.vector
            def _(dve):
                c = Chain(dve, chain)
                nc.vector.memset(ones[:, :], 1.0 / D).then_inc(ready, 1)
                dve.wait_ge(par_in, 32)
                nc.vector.tensor_scalar(sub_g[:, 1:2], sub_g[:, 0:1], 1.0 - LAM_INIT, None, ALU.mult).then_inc(g8, 1)
                for h in range(HEADS):
                    o = slice(h * TT, h * TT + TT)
                    dve.wait_ge(o_in[h], 16)
                    c.then(nc.vector.tensor_scalar(sq[:, 0, :, :], oall[:, h, :, :], O_LIMIT, -O_LIMIT, ALU.min,
                                                   ALU.max))
                    c.then(nc.vector.tensor_tensor(sq[:, 0, :, :], sq[:, 0, :, :], sq[:, 0, :, :], ALU.mult))
                    c.then(nc.vector.tensor_reduce(ms[:, 0, o], sq[:, 0, :, :], AX.X, ALU.add))
                    dve.wait_ge(small_sq, h + 1)
                    nc.vector.tensor_reduce(ms[:, 3, o], sq[:, 1, :, :], AX.X, ALU.add).then_inc(summed, 1)
                dve.wait_ge(summed, HEADS)
                c.then(nc.vector.tensor_scalar(ms[:, 2, :], ms[:, 3, :], 2.0 ** -60, None, ALU.is_ge))
                nc.vector.tensor_scalar(ms[:, 0, :], ms[:, 0, :], 1.0 / P, LN_EPS, ALU.mult, ALU.add)
                c.then(nc.vector.tensor_scalar(ms[:, 4, :], ms[:, 2, :], -1.0, 1.0, ALU.mult, ALU.add))
                nc.vector.scalar_tensor_tensor(ms[:, 1, :], ms[:, 3, :], 1.0 / P, ms[:, 2, :], ALU.mult, ALU.mult)
                c.then(nc.vector.tensor_tensor(ms[:, 0, :], ms[:, 0, :], ms[:, 4, :], ALU.mult))
                nc.vector.tensor_tensor(ms[:, 1, :], ms[:, 1, :], ms[:, 0, :], ALU.add).then_inc(root, 1)
                c.then(nc.vector.scalar_tensor_tensor(ms[:, 4, :], ms[:, 2, :], 2.0 ** -70, ms[:, 4, :], ALU.mult,
                                                      ALU.add))
                c.then(nc.vector.scalar_tensor_tensor(ms[:, 4, :], ms[:, 3, :], 2.0 ** -12, ms[:, 4, :], ALU.is_lt,
                                                      ALU.mult))
                dve.wait_ge(mean_done, 1)
                for h in range(HEADS):
                    nc.vector.tensor_tensor(yconv[:, h, :], yconv[:, h, :], MEAN[:, :], ALU.subtract).then_inc(cent, 1)
                dve.wait_ge(rooted, 1)
                c.then(nc.vector.reciprocal(ms[:, 2, :], ms[:, 1, :]))
                c.then(nc.vector.tensor_tensor(ms[:, 2, :], ms[:, 2, :], ms[:, 4, :], ALU.mult))
                o2 = oall[:, :, :, :].rearrange("p h t c -> p (h t) c")
                nc.vector.tensor_tensor(o2, o2, ms[:, 2, :].unsqueeze(2).to_broadcast([P, NH, P]),
                                        ALU.mult).then_inc(o_norm, 1)
                dve.wait_ge(rooted, 2)
                c.then(nc.vector.reciprocal(rstd[:, :], rstd[:, :]))
                for h in range(HEADS):
                    nc.vector.tensor_tensor(yconv[:, h, :], yconv[:, h, :], rstd[:, :], ALU.mult).then_inc(z_done, 1)

            @block.tensor
            def _(pe):
                pe.wait_ge(ready, 1)
                for q in y_in:
                    pe.wait_ge(q, 16 * HEADS // 4)
                for f in range(2):
                    for h in range(HEADS):
                        ins = nc.tensor.matmul(MEAN[:, f * BANK:f * BANK + BANK], ones[:, :],
                                               yconv[:, h, f * BANK:f * BANK + BANK], start=(h == 0),
                                               stop=(h == HEADS - 1))
                ins.then_inc(mean_done, 1)
                for h in range(HEADS):
                    pe.wait_ge(sq_done, h + 1)
                    for f in range(2):
                        ins = nc.tensor.matmul(VAR[:, f * BANK:f * BANK + BANK], ones[:, :],
                                               sqc[:, h % 2, f * BANK:f * BANK + BANK], start=(h == 0),
                                               stop=(h == HEADS - 1))
                    ins.then_inc(var_done, 1)
                pe.wait_ge(o_norm, 1)
                n = 0
                for h in range(HEADS):
                    for f in range(2):
                        if n >= 2:
                            pe.wait_ge(tr_ev, n - 1)
                        for t in range(4):
                            ins = nc.tensor.transpose(TB[:, n % 2, t * P:t * P + P], oall[:, h, 4 * f + t, :],
                                                      identity[:, :])
                        ins.then_inc(tr, 1)
                        n += 1

            @block.scalar
            def _(act):
                for h in range(HEADS):
                    act.wait_ge(o_in[h], 16)
                    act.wait_ge(summed, h)
                    nc.scalar.activation(sq[:, 1, :, :], oall[:, h, :, :], ACT.Square,
                                         scale=2.0 ** -70).then_inc(small_sq, 1)
                for h in range(HEADS):
                    act.wait_ge(cent, h + 1)
                    if h >= 2:
                        act.wait_ge(var_done, h - 1)
                    nc.scalar.activation(sqc[:, h % 2, :], yconv[:, h, :], ACT.Square).then_inc(sq_done, 1)
                act.wait_ge(root, 1)
                nc.scalar.activation(ms[:, 1, :], ms[:, 1, :], ACT.Sqrt).then_inc(rooted, 1)
                act.wait_ge(var_done, HEADS)
                act.wait_ge(eps_ready, 1)
                nc.scalar.activation(rstd[:, :], VAR[:, :], ACT.Sqrt, bias=eps[:, :]).then_inc(rooted, 1)
                act.wait_ge(g8, 1)
                n = 0
                for h in range(HEADS):
                    for f in range(2):
                        act.wait_ge(tr, n + 1)
                        nc.scalar.activation(oT[:, h, f * BANK:f * BANK + BANK], TB[:, n % 2, :], ACT.Copy,
                                             scale=sub_g[:, 1:2]).then_inc(tr_ev, 1)
                        n += 1
                for h in range(HEADS):
                    act.wait_ge(z_done, h + 1)
                    nc.scalar.activation(yconv[:, h, :], yconv[:, h, :], ACT.Silu, bias=chan[:, 1, h:h + 1],
                                         scale=chan[:, 0, h:h + 1])

            @block.gpsimd
            def _(pool):
                nc.gpsimd.memset(eps[:, :], LN_EPS).then_inc(eps_ready, 1)


def merge(nc, sem, A, hT, oT, zT, m_dram, at):
    m = Map(nc, at)
    g_raw = m.take("mg_g_raw", [P, 2, KD, 2 * P])
    wg = [m.take(f"mg_wg{j}", [P, KD, 2 * P], F32R) for j in range(2)]
    wa = m.take("mg_wa", [P, 2, KD, P])
    wc = m.take("mg_wc", [P, 2, KD, P])
    th = m.take("mg_th", [P, 2, 2, BANK])
    cd = m.take("mg_cd", [P, 2, BANK])
    part = m.take("mg_part", [P, 2, 2, BANK])
    done = m.take("mg_done", [P, 2, BANK])
    bias = m.take("mg_bias", [P, 3, HEADS])
    half = m.take("mg_half", [P, 3, HEADS])
    with nc.psum_tensor("mg_ps", [P, 2, 4, BANK], F32) as PS:
        par_in = sem("mg_par")
        w_in = [sem("mg_w_in0"), sem("mg_w_in1")]
        halved = sem("mg_halved")
        gh, gl = sem("mg_gh"), sem("mg_gl")
        gate_pr = sem("mg_gate_pr")
        pr = sem("mg_pr")
        th_done, cd_done = sem("mg_th_done"), sem("mg_cd_done")
        part_done = sem("mg_part_done")
        m_done = sem("mg_m_done")
        m_out = [sem("mg_m_out0"), sem("mg_m_out1")]
        with nc.Block() as block:
            @block.sync
            def _(sp):
                sp.dma_start(bias[:, 0:2, :], A["chan"][:, 2:4, :]).then_inc(par_in, 16)
                sp.dma_start(bias[:, 2, :], A["chan"][:, 7, :]).then_inc(par_in, 16)

                def load(t, u):
                    for dst, name in ((g_raw, "w_gate"), (wa, "w_attn"), (wc, "w_conv")):
                        sp.dma_start(dst[:, u, :, :], A[name][ds(t, 1)].rearrange("o p k c -> (o p) k c")
                                     ).then_inc(w_in[u], 16)

                load(0, 0)
                with sp.Fori(0, TT // 2 - 1) as i:
                    for u in (1, 0):
                        t = i * 2 + 2 - u
                        sp.wait_ge(m_done, t * 2 - 1)
                        load(t, u)
                for x, u in ((TT - 1, 1), (TT, 0)):
                    sp.wait_ge(m_done, x * 2 - 1)
                    load(TT - 1, u)

            @block.tensor
            def _(pe):
                with pe.Fori(0, TT // 2) as i:
                    for u in range(2):
                        t = i * 2 + u
                        pe.wait_ge(gl, t + 1)
                        pe.wait_ge(w_in[u], i * 48 + 48)
                        for f in range(2):
                            pe.wait_ge(th_done, t * 2)
                            for j in range(2):
                                ins = matmul3(nc, PS[:, f, j, :],
                                              [lambda k, x=x: x[:, k, j * P:j * P + P] for x in wg],
                                              [lambda k, x=x: x[:, k, M + f * BANK:M + f * BANK + BANK] for x in hT],
                                              KD)
                            ins.then_inc(gate_pr, 1)
                        for f in range(2):
                            pe.wait_ge(m_done, t * 2 + f)
                            for j, (w, src) in enumerate(((wa, oT), (wc, zT))):
                                for k in range(KD):
                                    ins = nc.tensor.matmul(PS[:, f, 2 + j, :], w[:, u, k, :],
                                                           src[:, k, f * BANK:f * BANK + BANK], start=(k == 0),
                                                           stop=(k == KD - 1))
                            ins.then_inc(pr, 1)

            @block.scalar
            def _(act):
                act.wait_ge(halved, 1)

                def high(t, u, i):
                    act.wait_ge(w_in[u], i * 48 + 48)
                    act.wait_ge(gate_pr, t * 2)
                    nc.scalar.activation(wg[0][:, :, :], g_raw[:, u, :, :], ACT.Copy).then_inc(gh, 1)

                high(0, 0, 0)
                with act.Fori(0, TT // 2) as i:
                    for u in range(2):
                        t = i * 2 + u
                        for f in range(2):
                            act.wait_ge(m_done, t * 2 + f)
                            act.wait_ge(gate_pr, t * 2 + f + 1)
                            act.nop(nofuse=True)
                            for j in range(2):
                                ins = nc.scalar.activation(th[:, f, j, :], PS[:, f, j, :], ACT.Tanh,
                                                           bias=half[:, j, ds(t, 1)], scale=0.5)
                            ins.then_inc(th_done, 1)
                        high(t + 1, 1 - u, i + u)
                        for f in range(2):
                            act.wait_ge(pr, t * 2 + f + 1)
                            act.nop(nofuse=True)
                            nc.scalar.activation(cd[:, f, :], PS[:, f, 3, :], ACT.Identity,
                                                 bias=half[:, 2, ds(t, 1)], scale=0.5).then_inc(cd_done, 1)

            @block.gpsimd
            def _(pool):
                with pool.Fori(0, TT) as t:
                    for f in range(2):
                        pool.wait_ge(m_done, t * 2 + f + 2)
                        pool.nop(nofuse=True)
                        pool.dma_start(m_dram[ds(t, 1), :, f * BANK:f * BANK + BANK].rearrange("o p t -> (o p) t"),
                                       done[:, f, :]).then_inc(m_out[f], 16)
                for f in range(2):
                    pool.wait_ge(m_out[f], 16 * TT)

            @block.vector
            def _(dve):
                dve.wait_ge(par_in, 32)
                nc.vector.tensor_scalar(half[:, :, :], bias[:, :, :], 0.5, None, ALU.mult).then_inc(halved, 1)
                dve.wait_ge(halved, 1)
                nc.vector.memset(part[:, :, :, :], 0.0).then_inc(m_done, 1)
                dve.wait_ge(m_done, 1)

                def low(t, u):
                    dve.wait_ge(gh, t + 1)
                    nc.vector.tensor_tensor(wg[1][:, :, :], g_raw[:, u, :, :], wg[0][:, :, :].bitcast(F32),
                                            ALU.subtract).then_inc(gl, 1)

                low(0, 0)
                with dve.Fori(0, TT // 2) as i:
                    for u in range(2):
                        t = i * 2 + u
                        low(t + 1, 1 - u)
                        for f in range(2):
                            dve.wait_ge(cd_done, t * 2 + f + 1)
                            nc.vector.scalar_tensor_tensor(part[:, f, 0, :], th[:, f, 0, :], 1.0, PS[:, f, 2, :],
                                                           ALU.add, ALU.mult)
                            nc.vector.scalar_tensor_tensor(part[:, f, 1, :], th[:, f, 1, :], 1.0, cd[:, f, :],
                                                           ALU.add, ALU.mult).then_inc(part_done, 1)
                            dve.wait_ge(m_out[f], t * 16)
                            dve.wait_ge(part_done, t * 2 + f + 1)
                            nc.vector.scalar_tensor_tensor(done[:, f, :], part[:, f, 0, :], 0.5, part[:, f, 1, :],
                                                           ALU.mult, ALU.add).then_inc(m_done, 1)


def layer_norm_tile(dve, c, nc, x, out, stats, mv, gamma, beta, root, rooted, n):
    nc.vector.bn_stats(stats[:, 0, :], x[:, 0:BANK])
    c.then(nc.vector.bn_stats(stats[:, 1, :], x[:, BANK:D]))
    c.then(nc.vector.bn_aggr(mv[:, 0:2], stats[:, :, :].rearrange("p a b -> p (a b)")))
    nc.vector.tensor_scalar(mv[:, 2:3], mv[:, 1:2], LN_EPS, None, ALU.add).then_inc(root, 1)
    dve.wait_ge(rooted, n + 1)
    c.then(nc.vector.reciprocal(mv[:, 3:4], mv[:, 3:4]))
    c.then(nc.vector.tensor_scalar(x, x, mv[:, 0:1], mv[:, 3:4], ALU.subtract, ALU.mult))
    c.then(nc.vector.tensor_tensor(x, x, gamma, ALU.mult))
    return nc.vector.tensor_tensor(out, x, beta, ALU.add)


def project(nc, sem, A, m_dram, identity, h_dram, h1T, acc_dram, at):
    m = Map(nc, at)
    mT = m.take("pj_m", [P, KD, T])
    wout = m.take("pj_w", [P, KD, D])
    bout = m.take("pj_bout", [P, D])
    gamma = m.take("pj_gamma", [P, D])
    beta = m.take("pj_beta", [P, D])
    h_in = m.take("pj_h", [P, 2, D])
    r = m.take("pj_r", [P, 2, D])
    scaled = m.take("pj_scaled", [P, 2, D])
    stats = m.take("pj_stats", [P, 2, 6])
    mv = m.take("pj_mv", [P, 4])
    with nc.psum_tensor("pj_y", [P, 2, D], F32) as Y, nc.psum_tensor("pj_t", [P, 4, BANK], F32) as TB:
        par_in, h_ld = sem("pj_par"), [sem("pj_h_in0"), sem("pj_h_in1")]
        mw_in = [sem(f"pj_mw_in{k}") for k in range(KD)]
        y_done, r_done = sem("pj_y_done"), sem("pj_r_done")
        chain, root, rooted = sem("pj_chain"), sem("pj_root"), sem("pj_rooted")
        h1_done, tr, ac = sem("pj_h1"), sem("pj_tr"), sem("pj_acc")
        hi_done, lo_done = sem("pj_hi"), sem("pj_lo")
        acc_out = [sem("pj_acc_out0"), sem("pj_acc_out1")]

        def half(t, f):
            fr = slice(t * P, t * P + P)
            return (TB[:, t % 2 * 2 + f, :].rearrange("p (k c) -> p k c", k=4),
                    h1T[0][:, 4 * f:4 * f + 4, fr], h1T[1][:, 4 * f:4 * f + 4, fr])

        with nc.Block() as block:
            @block.sync
            def _(sp):
                for k in range(KD):
                    sp.dma_start(mT[:, k, :], m_dram[k]).then_inc(mw_in[k], 16)
                    sp.dma_start(wout[:, k, :], A["w_out"][:, k, :]).then_inc(mw_in[k], 16)
                for dst, name in ((bout, "b_out"), (gamma, "ln1_g"), (beta, "ln1_b")):
                    sp.dma_start(dst[:, :], row(A[name])).then_inc(par_in, 16)
                for t in range(TT):
                    if t >= 2:
                        sp.wait_ge(r_done, t - 1)
                    sp.dma_start(h_in[:, t % 2, :], h_dram[t]).then_inc(h_ld[t % 2], 16)

            @block.gpsimd
            def _(pool):
                for t in range(TT):
                    pool.wait_ge(ac, t + 1)
                    pool.dma_start(acc_dram[t], scaled[:, t % 2, :]).then_inc(acc_out[t % 2], 16)
                for q in acc_out:
                    pool.wait_ge(q, 16 * TT // 2)

            @block.tensor
            def _(pe):
                def turn(t):
                    pe.wait_ge(h1_done, t + 1)
                    for f in range(2):
                        if t >= 2:
                            pe.wait_ge(lo_done, 2 * (t - 2) + f + 1)
                        for k in range(4):
                            ins = nc.tensor.transpose(TB[:, t % 2 * 2 + f, k * P:k * P + P],
                                                      r[:, t % 2, (4 * f + k) * P:(4 * f + k + 1) * P], identity[:, :])
                        ins.then_inc(tr, 1)

                for t in range(TT):
                    if t >= 2:
                        pe.wait_ge(r_done, t - 1)
                    for f in range(2):
                        for k in range(KD):
                            if t == 0 and f == 0:
                                pe.wait_ge(mw_in[k], 32)
                            ins = nc.tensor.matmul(Y[:, t % 2, f * BANK:f * BANK + BANK], mT[:, k, t * P:t * P + P],
                                                   wout[:, k, f * BANK:f * BANK + BANK], start=(k == 0),
                                                   stop=(k == KD - 1))
                    ins.then_inc(y_done, 1)
                    if t:
                        turn(t - 1)
                turn(TT - 1)

            @block.vector
            def _(dve):
                c = Chain(dve, chain)
                dve.wait_ge(par_in, 48)

                def low(t):
                    for f in range(2):
                        ps, hi, lo = half(t, f)
                        dve.wait_ge(hi_done, 2 * t + f + 1)
                        nc.vector.tensor_tensor(lo, ps, hi.bitcast(F32), ALU.subtract).then_inc(lo_done, 1)

                for t in range(TT):
                    u = t % 2
                    dve.wait_ge(y_done, t + 1)
                    if t >= 2:
                        dve.wait_ge(ac, t - 1)
                    c.then(nc.vector.tensor_tensor(r[:, u, :], Y[:, u, :], bout[:, :], ALU.add))
                    dve.wait_ge(h_ld[u], 16 * (t // 2 + 1))
                    nc.vector.scalar_tensor_tensor(r[:, u, :], h_in[:, u, :], ALPHA, r[:, u, :], ALU.mult,
                                                   ALU.add).then_inc(r_done, 1)
                    dve.wait_ge(r_done, t + 1)
                    layer_norm_tile(dve, c, nc, r[:, u, :], r[:, u, :], stats, mv, gamma[:, :], beta[:, :], root,
                                    rooted, t).then_inc(h1_done, 1)
                    if t:
                        low(t - 1)
                low(TT - 1)

            @block.scalar
            def _(act):
                def store(t):
                    act.wait_ge(h1_done, t + 1)
                    if t >= 2:
                        act.wait_ge(acc_out[t % 2], 16 * (t // 2))
                    nc.scalar.activation(scaled[:, t % 2, :], r[:, t % 2, :], ACT.Copy, scale=ALPHA).then_inc(ac, 1)
                    for f in range(2):
                        ps, hi, _ = half(t, f)
                        act.wait_ge(tr, 2 * t + f + 1)
                        nc.scalar.activation(hi, ps, ACT.Copy).then_inc(hi_done, 1)

                for t in range(TT):
                    act.wait_ge(root, t + 1)
                    nc.scalar.activation(mv[:, 3:4], mv[:, 2:3], ACT.Sqrt).then_inc(rooted, 1)
                    if t:
                        store(t - 1)
                store(TT - 1)


class Ahead:

    def __init__(self, nc, sem, name, m, banks, h1T, splits):
        self.nc, self.banks, self.h1T, self.splits = nc, banks, h1T, splits
        self.raw = m.take(name + "_u_raw", [P, 2, KD, E2 * P])
        self.parts = [m.take(name + f"_u{j}", [P, splits, KD, E2 * P], F32R) for j in range(2)]
        self.coef = m.take(name + "_coef", [P, 2, E2, T])
        self.u_in = [sem(name + "_u_in0"), sem(name + "_u_in1")]
        self.high_made = sem(name + "_u_high")
        self.low_made = sem(name + "_u_low")
        self.up_done = sem(name + "_up")
        self.gelu_done = sem(name + "_gelu")
        self.stored = [sem(name + "_a_out0"), sem(name + "_a_out1")]

    def credits(self, dve):
        for q, n in ((self.low_made, 1), (self.up_done, 2), (self.gelu_done, 2)):
            self.nc.vector.memset(self.coef[:, 0, 0, 0:8], 0.0).then_inc(q, n)
            dve.wait_ge(q, n)

    def load(self, sp, A, first, n, slot):
        sp.wait_ge(self.low_made, n)
        sp.dma_start(self.raw[:, slot, :, :], A["u_t"][ds(n + first, 1)].rearrange("o p k e -> (o p) k e")
                     ).then_inc(self.u_in[slot], 16)

    def high(self, act, n, slot, i):
        act.wait_ge(self.u_in[slot], i * 16 + 16)
        act.wait_ge(self.up_done, n * E2 + (0 if self.splits == 2 else E2))
        self.nc.scalar.activation(self.parts[0][:, slot % self.splits, :, :], self.raw[:, slot, :, :],
                                  ACT.Copy).then_inc(self.high_made, 1)

    def low(self, dve, n, slot):
        dve.wait_ge(self.high_made, n + 1)
        x = slot % self.splits
        self.nc.vector.tensor_tensor(self.parts[1][:, x, :, :], self.raw[:, slot, :, :],
                                     self.parts[0][:, x, :, :].bitcast(F32), ALU.subtract).then_inc(self.low_made, 1)

    def up(self, pe, n, slot, first=0, last=E2 * 2 * KD):
        x = slot % self.splits
        if first == 0:
            pe.wait_ge(self.low_made, n + 2)
        for c in range(first, last):
            j, f, k = c // (2 * KD), c // KD % 2, c % KD
            if f == 0 and k == 0:
                pe.wait_ge(self.gelu_done, n * E2 + j + 1)
            fr = slice(f * BANK, f * BANK + BANK)
            for y, (w, h) in enumerate(((0, 0), (0, 1), (1, 0))):
                ins = self.nc.tensor.matmul(self.banks[:, j, fr], self.parts[w][:, x, k, j * P:j * P + P],
                                            self.h1T[h][:, k, fr], start=(k == 0 and y == 0),
                                            stop=(k == KD - 1 and y == 2))
            if f == 1 and k == KD - 1:
                ins.then_inc(self.up_done, 1)

    def gelu(self, act, n, slot, i, j):
        act.wait_ge(self.stored[slot], i * 16)
        act.wait_ge(self.up_done, n * E2 + j + 1 + 2)
        self.nc.scalar.activation(self.coef[:, slot, j, :], self.banks[:, j, :], ACT.Gelu).then_inc(self.gelu_done, 1)

    def store(self, pool, a_dram, first, n, slot):
        pool.wait_ge(self.gelu_done, n * E2 + E2 + 2)
        pool.nop(nofuse=True)
        pool.dma_start(a_dram[ds(n + first, 1)].rearrange("o p j t -> (o p) (j t)"),
                       self.coef[:, slot, :, :].rearrange("p j t -> p (j t)")).then_inc(self.stored[slot], 16)


def search(nc, sem, A, h1T, a_dram, identity, picks, at):
    m = Map(nc, at)
    PER = 20
    SEARCHED = 2
    with nc.psum_tensor("se_a", [P, E2, T], F32) as PA, nc.psum_tensor("se_q", [P, 2, BANK], F32) as Q, \
            nc.psum_tensor("se_s", [P, TT, KEYS], F32) as S:
        ahead = Ahead(nc, sem, "se", m, PA, h1T, 2)
        raw = m.take("se_raw", [P, 2, KD, P])
        wq = [m.take(f"se_w{j}", [P, 2, KD, P], F32R) for j in range(2)]
        sub = m.take("se_sub", [P, 2, KEYS])
        qt = m.take("se_qt", [P, 2, T])
        sv = m.take("se_sv", [P, 2 * TT, K])
        si = m.take("se_si", [P, 2 * TT, K], U32)
        sf = m.take("se_sf", [P, 2 * TT, K])
        cv = m.take("se_cv", [P, TT, K])
        ci = m.take("se_ci", [P, TT, K], U32)
        cab = m.take("se_cab", [P, 2, TT, K], U32)
        cf = m.take("se_cf", [P, 2, TT, K])
        iota = m.take("se_iota", [P, K])
        gs = m.take("se_gs", [P, 2, TT])
        pick = m.take("se_pick", [P, 3, TT, K])
        pick_all = m.take("se_pick_all", [P, 3 * TT, HEADS, K])
        s = m.take("se_s", [P, 2 * TT, KEYS])
        cand_mem, left_mem = m.take("se_cand", [P, TT * K * K]), m.take("se_left", [P, 2 * TT * KEYS])
        cand = cand_mem[:, :].rearrange("p (t c) -> p t c", t=TT)
        eq = cand_mem[:, :].rearrange("p (x a) -> p x a", a=K)
        s_left = left_mem[:, :].rearrange("p (x n) -> p x n", n=KEYS)
        cand_left = left_mem[:, :].rearrange("p (t c) -> p t c", t=TT)
        par_in = sem("se_par")
        w_in = [sem("se_w_in0"), sem("se_w_in1")]
        wh, wl = sem("se_wh"), sem("se_wl")
        q_done, q_ev, s_done, s_ev = (sem("se_" + x) for x in ("q_done", "q_ev", "s_done", "s_ev"))
        chain = sem("se_chain")
        ex, exd = sem("se_ex"), sem("se_exd")
        picked, kept = sem("se_picked"), sem("se_kept")
        tr, tr_ev = sem("se_tr"), sem("se_tr_ev")
        with nc.Block() as block:
            @block.sync
            def _(sp):
                def load(x, u):
                    sp.dma_start(raw[:, u, :, :], A["w_query"][ds(x, 1)].rearrange("o p k c -> (o p) k c")
                                 ).then_inc(w_in[u], 16)
                    sp.dma_start(sub[:, u, :], A["subkeys"][ds(x, 1)].rearrange("o p c -> (o p) c")
                                 ).then_inc(w_in[u], 16)

                sp.dma_start(iota[:, :], A["iota"][:, 0:K]).then_inc(par_in, 16)
                load(0, 0)
                load(1, 1)
                with sp.Fori(0, HEADS - 1) as h:
                    for u in range(2):
                        ahead.load(sp, A, 0, h * 2 + u, u)
                    for u in range(2):
                        sp.wait_ge(wl, h * 2 + u + 1)
                        sp.wait_ge(s_done, h * 2 + u + 1)
                        load(h * 2 + 2 + u, u)
                for u in range(2):
                    ahead.load(sp, A, 0, (HEADS - 1) * 2 + u, u)

            @block.gpsimd
            def _(pool):
                with pool.Fori(0, HEADS) as h:
                    for u in range(2):
                        ahead.store(pool, a_dram, 0, h * 2 + u, u)
                for q in ahead.stored:
                    pool.wait_ge(q, 16 * HEADS)

            @block.tensor
            def _(pe):
                def queries(x, u):
                    pe.wait_ge(wl, x + 1)
                    pe.wait_ge(q_ev, x)
                    for f in range(2):
                        ins = matmul3(nc, Q[:, f, :], [lambda k, w=w: w[:, u, k, :] for w in wq],
                                      [lambda k, y=y: y[:, k, f * BANK:f * BANK + BANK] for y in h1T], KD)
                    ins.then_inc(q_done, 1)

                def score(x, u):
                    pe.wait_ge(q_ev, x + 1)
                    pe.wait_ge(s_ev, x)
                    for t in range(TT):
                        ins = nc.tensor.matmul(S[:, t, :], qt[:, u, t * P:t * P + P], sub[:, u, :], start=True,
                                               stop=True)
                    ins.then_inc(s_done, 1)

                half = 2 * KD
                queries(0, 0)
                queries(1, 1)
                score(0, 0)
                score(1, 1)
                with pe.Fori(0, HEADS - 1) as h:
                    ahead.up(pe, h * 2, 0)
                    queries(h * 2 + 2, 0)
                    ahead.up(pe, h * 2 + 1, 1, 0, half)
                    score(h * 2 + 2, 0)
                    queries(h * 2 + 3, 1)
                    ahead.up(pe, h * 2 + 1, 1, half, 2 * half)
                    score(h * 2 + 3, 1)
                for u in range(2):
                    ahead.up(pe, (HEADS - 1) * 2 + u, u)
                pe.wait_ge(kept, HEADS)
                for t in range(TT):
                    if t >= 2:
                        pe.wait_ge(tr_ev, t - 1)
                    for j in range(3):
                        ins = nc.tensor.transpose(Q[:, t % 2, j * P:j * P + P],
                                                  pick_all[:, j * TT + t, :, :].rearrange("p h k -> p (h k)"),
                                                  identity[:, :])
                    ins.then_inc(tr, 1)

            @block.scalar
            def _(act):
                def high(h, u):
                    act.wait_ge(w_in[u], h * 32 + 32)
                    nc.scalar.activation(wq[0][:, u, :, :], raw[:, u, :, :], ACT.Copy).then_inc(wh, 1)

                def query_out(x, u):
                    act.wait_ge(q_done, x + 1)
                    nc.scalar.activation(qt[:, u, :], Q[:, :, :].rearrange("p f c -> p (f c)"),
                                         ACT.Copy).then_inc(q_ev, 1)

                def score_out(x, u):
                    act.wait_ge(s_done, x + 1)
                    nc.scalar.activation(s[:, u * TT:u * TT + TT, :], S[:, :, :], ACT.Copy).then_inc(s_ev, 1)

                def exps(h):
                    act.wait_ge(ex, h + 1)
                    nc.scalar.activation(pick[:, 2, :, :], pick[:, 2, :, :], ACT.Exp).then_inc(exd, 1)

                def keep(h):
                    act.wait_ge(picked, h + 1)
                    act.nop(nofuse=True)
                    nc.scalar.activation(pick_all[:, :, ds(h, 1), :].rearrange("p j o k -> p j (o k)"),
                                         pick[:, :, :, :].rearrange("p j t k -> p (j t) k"),
                                         ACT.Copy).then_inc(kept, 1)

                for u in range(2):
                    high(0, u)
                ahead.high(act, 0, 0, 0)
                for u in range(2):
                    query_out(u, u)
                for u in range(2):
                    score_out(u, u)
                with act.Fori(0, HEADS - 1) as h:
                    for u in range(2):
                        act.wait_ge(q_done, h * 2 + u + 1)
                        high(h + 1, u)
                    ahead.high(act, h * 2 + 1, 1, h)
                    for j in range(E2):
                        ahead.gelu(act, h * 2, 0, h, j)
                    act.wait_ge(s_done, h * 2 + 1)
                    query_out(h * 2 + 2, 0)
                    ahead.high(act, h * 2 + 2, 0, h + 1)
                    ahead.gelu(act, h * 2 + 1, 1, h, 0)
                    act.wait_ge(chain, h * PER + SEARCHED)
                    score_out(h * 2 + 2, 0)
                    act.wait_ge(s_done, h * 2 + 2)
                    query_out(h * 2 + 3, 1)
                    exps(h)
                    ahead.gelu(act, h * 2 + 1, 1, h, 1)
                    score_out(h * 2 + 3, 1)
                    keep(h)
                ahead.high(act, (HEADS - 1) * 2 + 1, 1, HEADS - 1)
                for j in range(E2):
                    ahead.gelu(act, (HEADS - 1) * 2, 0, HEADS - 1, j)
                exps(HEADS - 1)
                for j in range(E2):
                    ahead.gelu(act, (HEADS - 1) * 2 + 1, 1, HEADS - 1, j)
                keep(HEADS - 1)
                for t in range(TT):
                    act.wait_ge(tr, t + 1)
                    nc.scalar.activation(picks[:, :, t * P:t * P + P],
                                         Q[:, t % 2, 0:3 * P].rearrange("p (j c) -> p j c", j=3),
                                         ACT.Copy).then_inc(tr_ev, 1)

            @block.vector
            def _(dve):
                def low(x, u):
                    dve.wait_ge(wh, x + 1)
                    nc.vector.tensor_tensor(wq[1][:, u, :, :], raw[:, u, :, :], wq[0][:, u, :, :].bitcast(F32),
                                            ALU.subtract).then_inc(wl, 1)

                def search_head(h, c, last):
                    def top16(vals, idx, src, left, n):
                        for x in range(n):
                            ins = nc.vector.max(vals[:, x, 0:8], src[:, x, :])
                        c.then(ins, apart=True)
                        for x in range(n):
                            nc.vector.max_index(idx[:, x, 0:8], vals[:, x, 0:8], src[:, x, :])
                            ins = nc.vector.match_replace(left[:, x, :], vals[:, x, 0:8], src[:, x, :], LOWEST)
                        c.then(ins, apart=True)
                        for x in range(n):
                            ins = nc.vector.max(vals[:, x, 8:16], left[:, x, :])
                        c.then(ins, apart=True)
                        for x in range(n):
                            ins = nc.vector.max_index(idx[:, x, 8:16], vals[:, x, 8:16], left[:, x, :])
                        c.then(ins, apart=True)

                    dve.wait_ge(s_ev, h * 2 + 2)
                    dve.nop(nofuse=True)
                    if not last:
                        for u in range(2):
                            low(h * 2 + 2 + u, u)
                    ahead.low(dve, h * 2 + 1, 1)
                    dve.nop(nofuse=True)
                    top16(sv, si, s, s_left, 2 * TT)
                    c.then(nc.vector.tensor_copy(sf[:, :, :], si[:, :, :]))
                    c.then(nc.vector.tensor_tensor(cand.rearrange("p t (a b) -> p t a b", a=K),
                                                   sv[:, 0:TT, :].unsqueeze(3).to_broadcast([P, TT, K, K]),
                                                   sv[:, TT:2 * TT, :].unsqueeze(2).to_broadcast([P, TT, K, K]),
                                                   ALU.add), apart=True)
                    if not last:
                        ahead.low(dve, h * 2 + 2, 0)
                        dve.nop(nofuse=True)
                    top16(cv, ci, cand, cand_left, TT)
                    dve.wait_ge(kept, h)
                    nc.vector.tensor_tensor(pick[:, 2, :, :], cv[:, :, :],
                                            cv[:, :, 0:1].to_broadcast([P, TT, K]), ALU.subtract).then_inc(ex, 1)
                    nc.vector.tensor_scalar(cab[:, 0, :, :], ci[:, :, :], 4, None, ALU.logical_shift_right)
                    c.then(nc.vector.tensor_scalar(cab[:, 1, :, :], ci[:, :, :], K - 1, None, ALU.bitwise_and))
                    c.then(nc.vector.tensor_copy(cf[:, :, :, :], cab[:, :, :, :]))
                    e4 = eq.rearrange("p (t k) a -> p t k a", t=TT)
                    for j in range(2):
                        c.then(nc.vector.tensor_tensor(
                            eq, cf[:, j, :, :].rearrange("p t k -> p (t k)").unsqueeze(2)
                            .to_broadcast([P, TT * K, K]),
                            iota[:, :].unsqueeze(1).to_broadcast([P, TT * K, K]), ALU.is_equal))
                        c.then(nc.vector.tensor_tensor(e4, e4, sf[:, j * TT:j * TT + TT, :].unsqueeze(2)
                                                       .to_broadcast([P, TT, K, K]), ALU.mult))
                        c.then(nc.vector.tensor_reduce(pick[:, j, :, :].rearrange("p t k -> p (t k)"), eq,
                                                       AX.X, ALU.add))
                    dve.wait_ge(exd, h + 1)
                    c.then(nc.vector.tensor_reduce(gs[:, 0, :], pick[:, 2, :, :], AX.X, ALU.add))
                    c.then(nc.vector.reciprocal(gs[:, 1, :], gs[:, 0, :]))
                    nc.vector.tensor_tensor(pick[:, 2, :, :], pick[:, 2, :, :],
                                            gs[:, 1, :].unsqueeze(2).to_broadcast([P, TT, K]),
                                            ALU.mult).then_inc(picked, 1)
                    assert c.n == PER, c.n

                ahead.credits(dve)
                dve.wait_ge(par_in, 16)
                for u in range(2):
                    low(u, u)
                ahead.low(dve, 0, 0)
                with dve.Fori(0, HEADS - 1) as h:
                    search_head(h, Chain(dve, chain, h * PER), False)
                search_head(HEADS - 1, Chain(dve, chain, (HEADS - 1) * PER), True)


def gates(nc, sem, A, h1T, picks, g_dram, a_dram, at):
    QUADS = GT // 4
    m = Map(nc, at)
    with nc.psum_tensor("gt_a", [P, E2, T], F32) as PA, nc.psum_tensor("gt_ps", [P, 4, BANK], F32) as PS:
        ahead = Ahead(nc, sem, "gt", m, PA, h1T, 1)
        hot1 = m.take("gt_hot1", [P, 4, 4, KEYS])
        hot2 = m.take("gt_hot2", [P, 4, 4, KEYS])
        stage = [m.take(f"gt_stage{j}", [P, KEYS, GT]) for j in range(2)]
        iota = m.take("gt_iota", [P, KEYS])
        part = m.take("gt_part", [P, 3, GT])
        par_in, chain = sem("gt_par"), sem("gt_chain")
        hot_ready = sem("gt_hot")
        mm_done = sem("gt_mm")
        ev_done = sem("gt_ev")
        g_out = [sem("gt_out0"), sem("gt_out1")]
        with nc.Block() as block:
            @block.sync
            def _(sp):
                sp.dma_start(iota[:, :], A["iota"]).then_inc(par_in, 16)
                with sp.Fori(0, GROUPS // 2) as i:
                    for u in range(2):
                        ahead.load(sp, A, 2 * TT, i * 2 + u, u)

            @block.gpsimd
            def _(pool):
                with pool.Fori(0, GROUPS // 2) as i:
                    for u in range(2):
                        pool.wait_ge(ev_done, (i * 2 + u + 1) * QUADS + 3)
                        pool.nop(nofuse=True)
                        pool.dma_start(g_dram[:, ds(i * 2 + u, 1), :, :].rearrange("p o a t -> p (o a) t"),
                                       stage[u][:, :, :]).then_inc(g_out[u], 16)
                        ahead.store(pool, a_dram, 2 * TT, i * 2 + u, u)
                for u in range(2):
                    pool.wait_ge(g_out[u], 16 * GROUPS // 2)
                    pool.wait_ge(ahead.stored[u], 16 * GROUPS // 2)

            @block.vector
            def _(dve):
                dve.wait_ge(par_in, 16)
                ahead.credits(dve)
                nc.vector.memset(part[:, 0, :], 0.0).then_inc(mm_done, 3)
                dve.wait_ge(mm_done, 3)
                nc.vector.memset(part[:, 1, :], 0.0).then_inc(ev_done, 3)
                dve.wait_ge(ev_done, 3)
                with dve.Fori(0, GROUPS // 2) as i:
                    for u in range(2):
                        g = i * 2 + u
                        dve.wait_ge(hot_ready, g * QUADS)
                        nc.vector.tensor_copy(part[:, :, :], picks[:, :, ds(g * GT, GT)]).then_inc(chain, 1)
                        dve.wait_ge(chain, g + 1)
                        for q in range(QUADS):
                            if q == 2:
                                ahead.low(dve, g, u)
                            dve.wait_ge(mm_done, g * QUADS + q)
                            for x in range(4):
                                t = 4 * q + x
                                nc.vector.tensor_scalar(hot1[:, q % 4, x, :], iota[:, :], part[:, 0, t:t + 1], None,
                                                        ALU.is_equal)
                                ins = nc.vector.tensor_scalar(hot2[:, q % 4, x, :], iota[:, :], part[:, 1, t:t + 1],
                                                              part[:, 2, t:t + 1], ALU.is_equal, ALU.mult)
                            ins.then_inc(hot_ready, 1)

            @block.tensor
            def _(pe):
                with pe.Fori(0, GROUPS // 2) as i:
                    for u in range(2):
                        for q in range(QUADS):
                            x0 = (i * 2 + u) * QUADS + q
                            pe.wait_ge(hot_ready, x0 + 1)
                            pe.wait_ge(ev_done, x0)
                            for x in range(4):
                                ins = nc.tensor.matmul(PS[:, q % 4, x * P:x * P + P], hot2[:, q % 4, x, :],
                                                       hot1[:, q % 4, x, :], start=True, stop=True)
                            ins.then_inc(mm_done, 1)
                            if q >= 4:
                                c = [x * E2 * 2 * KD // (QUADS - 4) for x in (q - 4, q - 3)]
                                ahead.up(pe, i * 2 + u, u, c[0], c[1])

            @block.scalar
            def _(act):
                with act.Fori(0, GROUPS // 2) as i:
                    for u in range(2):
                        g = i * 2 + u
                        ahead.high(act, g, u, i)
                        act.wait_ge(g_out[u], i * 16)
                        for q in range(QUADS):
                            act.wait_ge(mm_done, g * QUADS + q + 4)
                            nc.scalar.activation(stage[u][:, :, 4 * q:4 * q + 4],
                                                 PS[:, q % 4, :].rearrange("p (t a) -> p a t", t=4),
                                                 ACT.Copy).then_inc(ev_done, 1)
                            if q == 11:
                                ahead.gelu(act, g, u, i, 0)
                        ahead.gelu(act, g, u, i, 1)


def experts_ahead(nc, sem, A, acc, g_dram, a_dram, acc_dram, at):
    m = Map(nc, at)
    v_raw = m.take("ea_v_raw", [P, E2, D])
    v = [m.take(f"ea_v{j}", [P, 2, E2, D], F32R) for j in range(2)]
    gate = m.take("ea_gate", [P, 2, GROUPS, E2, GT])
    coef = m.take("ea_coef", [P, 2, E2, T])
    c = [m.take(f"ea_c{j}", [P, 2, E2, T], F32R) for j in range(2)]
    with nc.psum_tensor("ea_f", [P, 4, D], F32) as PF:
        acc_in = sem("ea_acc_in")
        v_in = sem("ea_v_in")
        g_in = [sem("ea_g_in0"), sem("ea_g_in1")]
        a_in = [sem("ea_a_in0"), sem("ea_a_in1")]
        vh, vl, gated, ch, cl = (sem("ea_" + x) for x in ("vh", "vl", "gated", "ch", "cl"))
        down = sem("ea_down")
        added = sem("ea_added")
        with nc.Block() as block:
            @block.sync
            def _(sp):
                with sp.Fori(0, AHEAD // 2) as i:
                    for u in range(2):
                        s = i * 2 + u
                        sp.wait_ge(cl, s)
                        sp.dma_start(coef[:, u, :, :], a_dram[ds(s, 1)].rearrange("o p j t -> (o p) j t")
                                     ).then_inc(a_in[u], 16)
                        sp.dma_start(gate[:, u, :, :, :].rearrange("p g j t -> p g (j t)"),
                                     g_dram[:, :, ds(s * E2, E2), :].rearrange("p g j t -> p g (j t)")
                                     ).then_inc(g_in[u], 16)
                        sp.wait_ge(vl, s)
                        sp.dma_start(v_raw[:, :, :], A["v"][ds(s, 1)].rearrange("o j p d -> p (o j) d")
                                     ).then_inc(v_in, 16)

            @block.gpsimd
            def _(pool):
                pool.dma_start(acc[:, :, :], acc_dram.rearrange("t p d -> p t d")).then_inc(acc_in, 16)

            @block.tensor
            def _(pe):
                with pe.Fori(0, AHEAD // 2) as i:
                    for u in range(2):
                        s = i * 2 + u
                        pe.wait_ge(cl, s + 2)
                        pe.wait_ge(vl, s + 1)
                        for t in range(TT):
                            pe.wait_ge(added, s * TT + t)
                            for f in range(2):
                                ins = matmul3(nc, PF[:, t % 4, f * BANK:f * BANK + BANK],
                                              [lambda j, x=x: x[:, u, j, t * P:t * P + P] for x in c],
                                              [lambda j, x=x: x[:, u, j, f * BANK:f * BANK + BANK] for x in v], E2)
                            ins.then_inc(down, 1)

            @block.scalar
            def _(act):
                with act.Fori(0, AHEAD // 2) as i:
                    for u in range(2):
                        s = i * 2 + u
                        act.wait_ge(v_in, s * 16 + 16)
                        act.wait_ge(down, s * TT)
                        nc.scalar.activation(v[0][:, u, :, :], v_raw[:, :, :], ACT.Copy).then_inc(vh, 1)
                        act.wait_ge(gated, s + 1)
                        nc.scalar.activation(c[0][:, u, :, :], coef[:, u, :, :], ACT.Copy).then_inc(ch, 1)

            @block.vector
            def _(dve):
                for q, n in ((cl, 1), (down, TT), (added, 3)):
                    nc.vector.memset(c[1][:, 0, 0, 0:8].bitcast(F32), 0.0).then_inc(q, n)
                    dve.wait_ge(q, n)

                def prepare(s, u, i, x):
                    if x == 0:
                        dve.wait_ge(g_in[u], i * 16 + 16)
                        dve.wait_ge(a_in[u], i * 16 + 16)
                        c4 = coef[:, u, :, :].rearrange("p j (g t) -> p j g t", t=GT)
                        nc.vector.tensor_tensor(c4, c4, gate[:, u, :, :, :].rearrange("p g j t -> p j g t"),
                                                ALU.mult).then_inc(gated, 1)
                    elif x == 1:
                        dve.wait_ge(vh, s + 1)
                        nc.vector.tensor_tensor(v[1][:, u, :, :], v_raw[:, :, :], v[0][:, u, :, :].bitcast(F32),
                                                ALU.subtract).then_inc(vl, 1)
                    else:
                        dve.wait_ge(ch, s + 1)
                        nc.vector.tensor_tensor(c[1][:, u, :, :], coef[:, u, :, :], c[0][:, u, :, :].bitcast(F32),
                                                ALU.subtract).then_inc(cl, 1)

                def add(s, t):
                    dve.wait_ge(down, s * TT + t + 1 + TT)
                    nc.vector.tensor_tensor(acc[:, t, :], acc[:, t, :], PF[:, t % 4, :], ALU.add).then_inc(added, 1)

                def step(s, u, i):
                    for x in range(3):
                        prepare(s, u, i, x)
                        add(s - 1, 2 * x)
                        add(s - 1, 2 * x + 1)
                    add(s - 1, TT - 2)
                    add(s - 1, TT - 1)

                for x in range(3):
                    prepare(0, 0, 0, x)
                dve.wait_ge(acc_in, 16)
                with dve.Fori(0, AHEAD // 2 - 1) as i:
                    step(i * 2 + 1, 1, i)
                    step(i * 2 + 2, 0, i + 1)
                step(AHEAD - 1, 1, AHEAD // 2 - 1)
                for t in range(TT):
                    add(AHEAD - 1, t)


def experts(nc, sem, A, h1T, acc, g_dram, at):
    h_hi, h_lo = h1T
    STEPS = KEYS // E2 - AHEAD
    m = Map(nc, at)
    u_raw = m.take("ex_u_raw", [P, 2, KD, E2 * P])
    v_raw = m.take("ex_v_raw", [P, 2, E2, D])
    u_hi = m.take("ex_u_hi", [P, KD, E2 * P], F32R)
    u_lo = m.take("ex_u_lo", [P, KD, E2 * P], F32R)
    v_hi = m.take("ex_v_hi", [P, E2, D], F32R)
    v_lo = m.take("ex_v_lo", [P, E2, D], F32R)
    gate = m.take("ex_gate", [P, 2, GROUPS, E2, GT])
    c_hi = m.take("ex_c_hi", [P, E2, T], F32R)
    c_lo = m.take("ex_c_lo", [P, E2, T], F32R)
    coef = m.take("ex_coef", [P, E2, T])
    with nc.psum_tensor("ex_a", [P, E2, T], F32) as PA, nc.psum_tensor("ex_f", [P, 2, D], F32) as PF:
        u_in = [sem("ex_u_in0"), sem("ex_u_in1")]
        v_in = [sem("ex_v_in0"), sem("ex_v_in1")]
        g_in = [sem("ex_g_in0"), sem("ex_g_in1")]
        uh, ul = sem("ex_uh"), sem("ex_ul")
        vh, vl = sem("ex_vh"), sem("ex_vl")
        up = sem("ex_up")
        ge = sem("ex_ge")
        gated = sem("ex_gated")
        ch, cl = sem("ex_ch"), sem("ex_cl")
        down = sem("ex_down")
        added = sem("ex_added")
        with nc.Block() as block:
            @block.sync
            def _(sp):
                with sp.Fori(0, STEPS // 2) as i:
                    for u in range(2):
                        s = i * 2 + u
                        sp.wait_ge(ul, s)
                        sp.dma_start(u_raw[:, u, :, :], A["u_t"][ds(s + AHEAD, 1)].rearrange("o p k e -> (o p) k e")
                                     ).then_inc(u_in[u], 16)
                        sp.wait_ge(gated, s)
                        sp.dma_start(gate[:, u, :, :, :].rearrange("p g j t -> p g (j t)"),
                                     g_dram[:, :, ds((s + AHEAD) * E2, E2), :].rearrange("p g j t -> p g (j t)")
                                     ).then_inc(g_in[u], 16)
                        sp.wait_ge(vl, s)
                        sp.dma_start(v_raw[:, u, :, :], A["v"][ds(s + AHEAD, 1)].rearrange("o j p d -> p (o j) d")
                                     ).then_inc(v_in[u], 16)

            @block.tensor
            def _(pe):
                def upward(s, first=False):
                    pe.wait_ge(ul, s + 2)
                    for j in range(E2):
                        if not first:
                            pe.wait_ge(ge, (s - 1) * E2 + j + 1)
                        for f in range(2):
                            ins = matmul3(nc, PA[:, j, f * BANK:f * BANK + BANK],
                                          [lambda k, x=x: x[:, k, j * P:j * P + P] for x in (u_hi, u_lo)],
                                          [lambda k, x=x: x[:, k, f * BANK:f * BANK + BANK] for x in h1T], KD)
                        ins.then_inc(up, 1)

                def downward(s):
                    pe.wait_ge(cl, s + 1)
                    pe.wait_ge(vl, s + 2)
                    for t in range(TT):
                        pe.wait_ge(added, s * TT + t)
                        for f in range(2):
                            ins = matmul3(nc, PF[:, t % 2, f * BANK:f * BANK + BANK],
                                          [lambda j, x=x: x[:, j, t * P:t * P + P] for x in (c_hi, c_lo)],
                                          [lambda j, x=x: x[:, j, f * BANK:f * BANK + BANK] for x in (v_hi, v_lo)],
                                          E2)
                        ins.then_inc(down, 1)

                upward(0, first=True)
                with pe.Fori(0, STEPS - 1) as i:
                    upward(i + 1)
                    downward(i)
                downward(STEPS - 1)

            @block.scalar
            def _(act):
                def split_u(s, u, i):
                    act.wait_ge(u_in[u], i * 16 + 16)
                    act.wait_ge(up, s * E2)
                    nc.scalar.activation(u_hi[:, :, :], u_raw[:, u, :, :], ACT.Copy).then_inc(uh, 1)

                def rest(s, u, i):
                    act.wait_ge(cl, s)
                    for j in range(E2):
                        act.wait_ge(up, s * E2 + j + 1)
                        nc.scalar.activation(coef[:, j, :], PA[:, j, :], ACT.Gelu).then_inc(ge, 1)
                    act.wait_ge(down, s * TT)
                    act.wait_ge(v_in[u], i * 16 + 16)
                    nc.scalar.activation(v_hi[:, :, :], v_raw[:, u, :, :], ACT.Copy).then_inc(vh, 1)
                    act.wait_ge(gated, s + 2)
                    nc.scalar.activation(c_hi[:, :, :], coef[:, :, :], ACT.Copy).then_inc(ch, 1)

                split_u(0, 0, 0)
                with act.Fori(0, STEPS // 2 - 1) as i:
                    split_u(i * 2 + 1, 1, i)
                    rest(i * 2, 0, i)
                    split_u(i * 2 + 2, 0, i + 1)
                    rest(i * 2 + 1, 1, i)
                split_u(STEPS - 1, 1, STEPS // 2 - 1)
                rest(STEPS - 2, 0, STEPS // 2 - 1)
                rest(STEPS - 1, 1, STEPS // 2 - 1)

            @block.vector
            def _(dve):
                for x, q in enumerate((ul, vl, gated, added)):
                    nc.vector.memset(coef[:, x % 2, 0:8], 0.0).then_inc(q, 1)
                    dve.wait_ge(q, 1)

                def split_u(s, u):
                    dve.wait_ge(uh, s + 1)
                    nc.vector.tensor_tensor(u_lo[:, :, :], u_raw[:, u, :, :], u_hi[:, :, :].bitcast(F32),
                                            ALU.subtract).then_inc(ul, 1)

                def add(s):
                    for t in range(TT):
                        dve.wait_ge(down, s * TT + t + 1)
                        nc.vector.tensor_tensor(acc[:, t, :], acc[:, t, :], PF[:, t % 2, :], ALU.add).then_inc(added, 1)

                def rest(s, u, i):
                    dve.wait_ge(ge, s * E2 + E2)
                    dve.wait_ge(g_in[u], i * 16 + 16)
                    c4 = coef[:, :, :].rearrange("p j (g t) -> p j g t", t=GT)
                    nc.vector.tensor_tensor(c4, c4, gate[:, u, :, :, :].rearrange("p g j t -> p j g t"),
                                            ALU.mult).then_inc(gated, 1)
                    dve.wait_ge(vh, s + 1)
                    nc.vector.tensor_tensor(v_lo[:, :, :], v_raw[:, u, :, :], v_hi[:, :, :].bitcast(F32),
                                            ALU.subtract).then_inc(vl, 1)
                    dve.wait_ge(ch, s + 1)
                    nc.vector.tensor_tensor(c_lo[:, :, :], coef[:, :, :], c_hi[:, :, :].bitcast(F32),
                                            ALU.subtract).then_inc(cl, 1)

                split_u(0, 0)
                split_u(1, 1)
                rest(0, 0, 0)
                with dve.Fori(0, STEPS // 2 - 1) as i:
                    split_u(i * 2 + 2, 0)
                    add(i * 2)
                    rest(i * 2 + 1, 1, i)
                    split_u(i * 2 + 3, 1)
                    add(i * 2 + 1)
                    rest(i * 2 + 2, 0, i + 1)
                add(STEPS - 2)
                rest(STEPS - 1, 1, STEPS // 2 - 1)
                add(STEPS - 1)


def norm_out(nc, sem, A, acc, out, at):
    m = Map(nc, at)
    gamma = m.take("no_gamma", [P, D])
    beta = m.take("no_beta", [P, D])
    stats = m.take("no_stats", [P, 2, 6])
    mv = m.take("no_mv", [P, 4])
    par_in, chain = sem("no_par"), sem("no_chain")
    root, rooted, ready = sem("no_root"), sem("no_rooted"), sem("no_ready")
    y_out = sem("no_out")
    with nc.Block() as block:
        @block.sync
        def _(sp):
            sp.dma_start(gamma[:, :], row(A["ln2_g"])).then_inc(par_in, 16)
            sp.dma_start(beta[:, :], row(A["ln2_b"])).then_inc(par_in, 16)
            o = out.rearrange("b (t p) d -> (b t) p d", p=P)
            for t in range(TT):
                sp.wait_ge(ready, t + 1)
                sp.dma_start(o[t], acc[:, t, :]).then_inc(y_out, 16)
            sp.wait_ge(y_out, 16 * TT)

        @block.vector
        def _(dve):
            dve.wait_ge(par_in, 32)
            c = Chain(dve, chain)
            for t in range(TT):
                layer_norm_tile(dve, c, nc, acc[:, t, :], acc[:, t, :], stats, mv, gamma[:, :], beta[:, :], root,
                                rooted, t).then_inc(ready, 1)

        @block.scalar
        def _(act):
            for t in range(TT):
                act.wait_ge(root, t + 1)
                nc.scalar.activation(mv[:, 3:4], mv[:, 2:3], ACT.Sqrt).then_inc(rooted, 1)


def encoder_block(nc, A, out, stop=None):
    ctx = ExitStack()
    with ctx:
        def sem(name):
            return nc.alloc_semaphore(name=name)

        def dram(name, shape):
            return nc.dram_tensor(name, shape, F32, kind="Internal").ap()

        h_dram = dram("h_dram", [TT, P, D])
        y_dram = dram("y_dram", [HEADS, P, T])
        o_dram = dram("o_dram", [HEADS, P, TT, P])
        m_dram = dram("m_dram", [KD, P, T])
        acc_dram = dram("acc_dram", [TT, P, D])
        a_dram = dram("a_dram", [AHEAD, P, E2, T])
        g_dram = dram("g_dram", [P, GROUPS, KEYS, GT])
        W = KD * T * 4
        WL = KD * L * 4
        ident_at, top = 16512, 229344
        at = ident_at + P * 4
        identity = Map(nc, ident_at).take("identity", [P, P])
        hT = [Map(nc, at + j * WL).take(f"hT{j}", [P, KD, L], F32R) for j in range(2)]
        a1 = at + 2 * WL
        oT = Map(nc, a1).take("oT", [P, HEADS, T])
        yconv = Map(nc, a1 + W).take("yconv", [P, HEADS, T])
        h1T = [Map(nc, at + j * W).take(f"h1T{j}", [P, KD, T], F32R) for j in range(2)]
        a2 = at + 2 * W
        acc = Map(nc, a2).take("acc", [P, TT, D])
        picks = Map(nc, top - 3 * T * 4).take("picks", [P, 3, T])

        with nc.cleanup_on_exit():
            norm_in(nc, sem, A, hT, h_dram, identity, a1)
            mix(nc, sem, A, hT, identity, o_dram, y_dram, a1)
        with nc.cleanup_on_exit():
            branch(nc, sem, A, identity, o_dram, y_dram, yconv, oT, a1 + 2 * W)
            merge(nc, sem, A, hT, oT, yconv, m_dram, a1 + 2 * W)
            project(nc, sem, A, m_dram, identity, h_dram, h1T, acc_dram, a2)
        with nc.cleanup_on_exit():
            search(nc, sem, A, h1T, a_dram, identity, picks, a2)
            gates(nc, sem, A, h1T, picks, g_dram, a_dram, a2)
        with nc.cleanup_on_exit():
            experts_ahead(nc, sem, A, acc, g_dram, a_dram, acc_dram, a2 + W)
            experts(nc, sem, A, h1T, acc, g_dram, a2 + W)
            norm_out(nc, sem, A, acc, out, a2 + W)


def _layout(inputs):
    import numpy as np

    def f(name):
        a = np.asarray(inputs[name])
        return a if name in ("x", "meta", "ln_in_g", "ln_in_b") else a[0]

    def tiles(w, parts):
        n = w.shape[1] // (parts * P)
        return w.reshape(w.shape[0] // P, P, parts, n, P).transpose(3, 1, 0, 2, 4).reshape(n, P, w.shape[0] // P,
                                                                                          parts * P)

    def col(v):
        return v.reshape(-1, P).T

    w, b = f("w_in"), f("b_in")
    q3, c2 = 3 * HEADS * P, 3 * HEADS * P + 2 * D
    pos = np.arange(L, dtype=np.float32)
    inv = np.float32(500000.0) ** (-np.arange(0, 2 * ROT, 2, dtype=np.float32) / np.float32(2 * ROT))
    ang = (pos[:, None] * inv[None, :]).astype(np.float32)
    order = np.concatenate([np.arange(M, L), np.arange(M), np.zeros(P - M, np.int64)])

    def rope(fn):
        return fn(ang).astype(np.float32)[order].reshape(TT + 1, P, ROT).transpose(1, 0, 2)

    return {
        "x": f("x"), "meta": f("meta"), "ln_in_g": f("ln_in_g"), "ln_in_b": f("ln_in_b"),
        "w_qkv": tiles(w[:, :q3], 3), "w_glu": tiles(w[:, q3:c2], 2), "w_gate": tiles(w[:, c2:], 2),
        "b_qkv": b[:q3].reshape(3, HEADS, P).transpose(1, 0, 2).reshape(HEADS, 3 * P),
        "chan": np.stack([col(v) for v in (b[q3:q3 + D], b[q3 + D:c2], b[c2:c2 + D], b[c2 + D:], f("dw_bias"),
                                           f("conv_ln_g"), f("conv_ln_b"), f("b_conv_proj"))], axis=1),
        "taps": f("dw_kernel").reshape(TAPS, HEADS, P).transpose(2, 1, 0),
        "lambda_q1": f("lambda_q1"), "lambda_k1": f("lambda_k1"), "lambda_q2": f("lambda_q2"),
        "lambda_k2": f("lambda_k2"), "subln_col": f("subln_g").reshape(P, 1),
        "w_attn": tiles(f("w_attn_proj"), 1), "w_conv": tiles(f("w_conv_proj"), 1),
        "w_out": f("w_out").reshape(KD, P, D).transpose(1, 0, 2),
        "b_out": f("b_out"), "ln1_g": f("ln1_g"), "ln1_b": f("ln1_b"), "ln2_g": f("ln2_g"), "ln2_b": f("ln2_b"),
        "w_query": f("peer_wq").reshape(KD, P, 2 * HEADS, P).transpose(2, 1, 0, 3),
        "subkeys": f("peer_subkeys").reshape(2 * HEADS, KEYS, P).transpose(0, 2, 1),
        "u_t": f("peer_u").reshape(STEPS, E2, KEYS, KD, P).transpose(0, 4, 3, 1, 2).reshape(STEPS, P, KD, E2 * P),
        "v": f("peer_v").reshape(STEPS, E2, P, D),
        "rope_cos": rope(np.cos), "rope_sin": rope(np.sin),
        "identity": np.eye(P, dtype=np.float32),
        "iota": np.broadcast_to(np.arange(KEYS, dtype=np.float32), (P, KEYS)),
    }


def kernel(**inputs):
    import numpy as np
    import concourse.bacc as bacc
    from concourse.bass_utils import run_bass_kernel_spmd

    nc = bacc.Bacc("TRN2", target_bir_lowering=False, num_devices=1)
    arrays, args = {}, {}
    for name, a in _layout(inputs).items():
        a = np.ascontiguousarray(a)
        arrays[f"in_{name}"] = a
        args[name] = nc.dram_tensor(f"in_{name}", a.shape, mybir.dt.from_np(a.dtype), kind="ExternalInput").ap()
    out = nc.dram_tensor("out", (1, T, D), F32, kind="ExternalOutput").ap()
    encoder_block(nc, args, out)
    r = run_bass_kernel_spmd(nc, [arrays], core_ids=[0])
    return r.results[0]["out"]
```

```python
import math

import concourse.bass as bass
from concourse import mybir

F32 = mybir.dt.float32
F32R = mybir.dt.float32r
BF16 = mybir.dt.bfloat16
U32 = mybir.dt.uint32
ACT = mybir.ActivationFunctionType
ALU = mybir.AluOpType
AX = mybir.AxisListType
ds = bass.ds

P = 128
D = 1024
KD = D // P
T = 1024
TT = T // P
M = 16
L = T + M
CHUNK = 64
HEADS = 8
HD = 64
ROT = HD // 8
TAPS = 31
PAD = TAPS - 1
K = 16
KEYS = 128
E2 = 2
STEPS = KEYS // E2
GT = 64
GROUPS = T // GT
AHEAD = 2 * HEADS + GROUPS
LN_EPS = 1e-5
ALPHA = 2.0 ** 0.25
LAM_INIT = 0.8 - 0.6 * math.exp(0.0)
BANK = 512
LOWEST = -3.0e38
O_LIMIT = 1.6e18


class Chain:

    def __init__(self, eng, sem, base=0):
        self.eng, self.sem, self.base, self.n = eng, sem, base, 0

    def mark(self, ins):
        ins.then_inc(self.sem, 1)
        self.n += 1
        return self.base + self.n

    def then(self, ins, apart=False):
        self.eng.wait_ge(self.sem, self.mark(ins))
        if apart:
            self.eng.nop(nofuse=True)



class Map:

    def __init__(self, nc, at=0):
        self.nc, self.at = nc, at

    def take(self, name, shape, dt=F32):
        n = 2 if dt == BF16 else 4
        for s in shape[1:]:
            n *= s
        h = self.nc.alloc_sbuf_tensor_at(name, shape, dt, offset=self.at)
        self.at += (n + 31) // 32 * 32
        return h


def row(ap, n=P):
    return ap.rearrange("(o d) -> o d", o=1).to_broadcast([n, ap.shape[0]])


def matmul3(nc, out, ws, xs, n):
    for a in range(n):
        for j, (w, x) in enumerate(((ws[0], xs[0]), (ws[0], xs[1]), (ws[1], xs[0]))):
            ins = nc.tensor.matmul(out, w(a), x(a), start=(a == 0 and j == 0), stop=(a == n - 1 and j == 2))
    return ins


def norm_in(nc, sem, A, hT, h_dram, identity, at):
    m = Map(nc, at)
    xin = m.take("xin", [P, 2, D])
    xn = m.take("xn", [P, 2, D])
    gamma = m.take("ni_gamma", [P, D])
    beta = m.take("ni_beta", [P, D])
    stats = m.take("ni_stats", [P, 2, 6])
    mv = m.take("ni_mv", [P, 2])
    std = m.take("ni_std", [P, 2])
    hT_hi, hT_lo = hT
    with nc.psum_tensor("ni_tp", [P, 4, BANK], F32) as tp:
        const_in = sem("ni_const_in")
        x_in = [sem("ni_x_in0"), sem("ni_x_in1")]
        x_used = sem("ni_x_used")
        chain = sem("ni_chain")
        var_ready = sem("ni_var")
        std_ready = sem("ni_std_s")
        gb = sem("ni_gamma_done")
        xn_ready = sem("ni_xn")
        tr_done = sem("ni_tr")
        hi_done = sem("ni_hi")
        lo_done = sem("ni_lo")
        h_out = [sem("ni_h_out0"), sem("ni_h_out1")]
        x_t = A["x"].rearrange("b (t p) d -> (b t) p d", p=P)
        PER = 3

        def half(t, u, f, n):
            at = 0 if n == M else t * P + M
            return (tp[:, 2 * u + f, :].rearrange("p (k c) -> p k c", k=4)[:, :, 0:n],
                    hT_hi[:, 4 * f:4 * f + 4, ds(at, n)], hT_lo[:, 4 * f:4 * f + 4, ds(at, n)])

        with nc.Block() as block:
            @block.sync
            def _(sp):
                sp.dma_start(gamma[:, :], row(A["ln_in_g"])).then_inc(const_in, 16)
                sp.dma_start(beta[:, :], row(A["ln_in_b"])).then_inc(const_in, 16)
                sp.dma_start(identity[:, :], A["identity"]).then_inc(const_in, 16)
                with sp.Fori(0, TT // 2) as i:
                    for u in range(2):
                        sp.wait_ge(x_used, i * 2 + u)
                        sp.dma_start(xin[:, u, :], x_t[ds(i * 2 + u, 1)].rearrange("o p d -> (o p) d")
                                     ).then_inc(x_in[u], 16)
                sp.wait_ge(x_used, TT)
                sp.dma_start(xin[0:M, 0, :], A["meta"]).then_inc(x_in[0], 16)

            @block.gpsimd
            def _(pool):
                with pool.Fori(0, TT // 2) as i:
                    for u in range(2):
                        pool.wait_ge(xn_ready, i * 2 + u + 1)
                        pool.nop(nofuse=True)
                        pool.dma_start(h_dram[ds(i * 2 + u, 1)].rearrange("o p d -> (o p) d"), xn[:, u, :]
                                       ).then_inc(h_out[u], 16)
                for u in range(2):
                    pool.wait_ge(h_out[u], 16 * TT // 2)

            @block.vector
            def _(dve):
                def normalise(t, u, i, n):
                    c = Chain(dve, chain, t * PER)
                    dve.wait_ge(x_in[u], i * 16 + 16)
                    nc.vector.bn_stats(stats[0:n, 0, :], xin[0:n, u, 0:BANK])
                    c.then(nc.vector.bn_stats(stats[0:n, 1, :], xin[0:n, u, BANK:D]), apart=True)
                    c.then(nc.vector.bn_aggr(mv[0:n, :], stats[0:n, :, :].rearrange("p a b -> p (a b)")))
                    nc.vector.tensor_scalar(std[0:n, 0:1], mv[0:n, 1:2], LN_EPS, None,
                                            ALU.add).then_inc(var_ready, 1)
                    dve.wait_ge(std_ready, t + 1)
                    c.then(nc.vector.reciprocal(std[0:n, 1:2], std[0:n, 1:2]))
                    dve.wait_ge(h_out[u], i * 16)
                    nc.vector.tensor_scalar(xn[0:n, u, :], xin[0:n, u, :], mv[0:n, 0:1], std[0:n, 1:2],
                                            ALU.subtract, ALU.mult).then_inc(x_used, 1)
                    dve.wait_ge(x_used, t + 2)
                    nc.vector.tensor_tensor(xn[0:n, u, :], xn[0:n, u, :], gamma[0:n, :], ALU.mult).then_inc(gb, 1)
                    dve.wait_ge(gb, t + 1)
                    nc.vector.tensor_tensor(xn[0:n, u, :], xn[0:n, u, :], beta[0:n, :],
                                            ALU.add).then_inc(xn_ready, 1)

                def low(t, u, n):
                    for f in range(2):
                        ps, hi, lo = half(t, u, f, n)
                        dve.wait_ge(hi_done, t * 2 + f + 1)
                        nc.vector.tensor_tensor(lo, ps, hi.bitcast(F32), ALU.subtract).then_inc(lo_done, 1)

                nc.vector.memset(stats[:, :, :], 0.0).then_inc(x_used, 1)
                dve.wait_ge(x_used, 1)
                nc.vector.memset(mv[:, :], 0.0).then_inc(lo_done, 4)
                dve.wait_ge(lo_done, 4)
                dve.wait_ge(const_in, 48)
                normalise(0, 0, 0, P)
                with dve.Fori(0, TT // 2 - 1) as i:
                    normalise(i * 2 + 1, 1, i, P)
                    low(i * 2, 0, P)
                    normalise(i * 2 + 2, 0, i + 1, P)
                    low(i * 2 + 1, 1, P)
                normalise(TT - 1, 1, TT // 2 - 1, P)
                low(TT - 2, 0, P)
                normalise(TT, 0, TT // 2, M)
                low(TT - 1, 1, P)
                low(TT, 0, M)

            @block.scalar
            def _(act):
                def root(t, n):
                    act.wait_ge(var_ready, t + 1)
                    nc.scalar.activation(std[0:n, 1:2], std[0:n, 0:1], ACT.Sqrt).then_inc(std_ready, 1)

                def high(t, u, n):
                    for f in range(2):
                        ps, hi, _ = half(t, u, f, n)
                        act.wait_ge(tr_done, t * 2 + f + 1)
                        act.nop(nofuse=True)
                        nc.scalar.activation(hi, ps, ACT.Copy).then_inc(hi_done, 1)

                root(0, P)
                with act.Fori(0, TT // 2 - 1) as i:
                    for u in range(2):
                        root(i * 2 + u + 1, P)
                        high(i * 2 + u, u, P)
                root(TT - 1, P)
                high(TT - 2, 0, P)
                root(TT, M)
                high(TT - 1, 1, P)
                high(TT, 0, M)

            @block.tensor
            def _(pe):
                def turn(t, u, n):
                    pe.wait_ge(xn_ready, t + 1)
                    for f in range(2):
                        pe.wait_ge(lo_done, t * 2 + f + 1)
                        for k in range(4):
                            ins = nc.tensor.transpose(tp[:, 2 * u + f, k * P:k * P + n],
                                                      xn[0:n, u, (4 * f + k) * P:(4 * f + k + 1) * P],
                                                      identity[0:n, 0:n])
                        ins.then_inc(tr_done, 1)

                pe.wait_ge(const_in, 48)
                with pe.Fori(0, TT // 2) as i:
                    for u in range(2):
                        turn(i * 2 + u, u, P)
                turn(TT, 0, M)


def mix(nc, sem, A, hT, identity, o_dram, y_dram, at):
    m = Map(nc, at)
    w_raw = m.take("w_raw", [P, KD, 3 * P])
    w_head = [m.take(f"w_head{j}", [P, KD, 3 * P], F32R) for j in range(2)]
    g_raw = m.take("g_raw", [P, KD, 2 * P])
    w_glu = [m.take(f"w_glu{j}", [P, KD, 2 * P], F32R) for j in range(2)]
    b_head = m.take("b_head", [P, 3 * P])
    qkv = m.take("qkv", [P, TT + 1, 3 * P])
    qT = m.take("qT", [P, T])
    kT = m.take("kT", [P, L])
    prob = m.take("prob", [P, 2, 2, L])
    mixed = m.take("mixed", [P, L])
    v_use = m.take("v_use", [P, TT + 1, P])
    mixT = m.take("mixT", [P, T])
    mixTm = m.take("mixTm", [M, P])
    glu_t = m.take("glu_t", [P, L])
    glu_a = m.take("glu_a", [P, L])
    u_pad = m.take("u_pad", [P, PAD + L])
    y_sum = m.take("y_sum", [P, T])
    o_head = m.take("o_head", [P, TT, P])
    cos_t = m.take("cos_t", [P, TT + 1, ROT])
    sin_t = m.take("sin_t", [P, TT + 1, ROT])
    rot = m.take("rot", [P, 4, (TT + 1) * 4 * ROT])
    negmax = m.take("negmax", [P, 4])
    sums = m.take("sums", [P, 4])
    rr = m.take("rr", [P, 2])
    lamv = m.take("lamv", [P, 4, HD])
    lamp = m.take("lamp", [P, 2, HD])
    lam = m.take("lam", [P, 4])
    glu_b = m.take("glu_b", [P, 2, HEADS])
    glu_h = m.take("glu_h", [P, 2, HEADS])
    taps_w = m.take("taps_w", [P, HEADS, TAPS])
    taps_b = m.take("taps_b", [P, HEADS])

    nbatch = [(i + 4) // 4 for i in range(TT)]
    before = [sum(nbatch[:i]) + i for i in range(TT + 1)]
    NB = before[TT]
    DVE_PER = TAPS + 2 * TT + 3 * TT
    GLU = [(part, c0, n) for part in (1, 0) for c0, n in ((0, BANK), (BANK, BANK), (T, M))]
    NG = len(GLU)
    NP = TT + 1
    LAST = HEADS - 1

    def unit_bank(k, first):
        return S if first and k % 2 else PB

    def pieces(start, n):
        out, c = [], start
        while c < start + n:
            e = min(start + n, c // BANK * BANK + BANK)
            out.append((c, e - c))
            c = e
        return out

    with nc.psum_tensor("mx_s", [P, 5 * BANK], F32) as S, nc.psum_tensor("mx_t", [P, BANK], F32) as TB, \
            nc.psum_tensor("mx_o", [P, BANK], F32) as OB, nc.psum_tensor("mx_p", [P, BANK], F32) as PB:
        tab_in = sem("mx_tables_in")
        w_in, b_in, g_in = sem("mx_w_in"), sem("mx_b_in"), sem("mx_g_in")
        wh, wl = sem("mx_wh"), sem("mx_wl")
        gh, gl = sem("mx_gh"), sem("mx_gl")
        y_done, y_out = sem("mx_y_done"), sem("mx_y_out")
        o_out = sem("mx_o_out")
        pj, pj_ev = sem("mx_pj"), sem("mx_pj_ev")
        cv, cv_ev = sem("mx_cv"), sem("mx_cv_ev")
        v_kept = sem("mx_v_kept")
        u_done = sem("mx_u")
        roped = sem("mx_roped")
        tq, tq_ev = sem("mx_tq"), sem("mx_tq_ev")
        s_done, mx_done, ex_done = sem("mx_s_done"), sem("mx_mx"), sem("mx_ex")
        map0 = sem("mx_map0")
        w_done = sem("mx_w_done")
        wt, wt_ev = sem("mx_wt"), sem("mx_wt_ev")
        o_done, o_ev = sem("mx_o_done"), sem("mx_o_ev")
        chain = sem("mx_chain")
        pre = sem("mx_pre")
        lam_e = sem("mx_lam_e")
        init = sem("mx_init")

        with nc.Block() as block:
            @block.sync
            def _(sp):
                def load_w(h):
                    sp.dma_start(w_raw[:, :, :], A["w_qkv"][ds(h, 1)].rearrange("o p k c -> (o p) k c")
                                 ).then_inc(w_in, 16)

                def load_g(h):
                    sp.dma_start(g_raw[:, :, :], A["w_glu"][ds(h, 1)].rearrange("o p k c -> (o p) k c")
                                 ).then_inc(g_in, 16)

                def load_bias(h):
                    sp.dma_start(b_head[:, :], A["b_qkv"][ds(h, 1), :].to_broadcast([P, 3 * P])).then_inc(b_in, 16)

                load_g(0)
                load_w(0)
                load_bias(0)
                for dst, src in ((cos_t[:, :, :], A["rope_cos"]), (sin_t[:, :, :], A["rope_sin"]),
                                 (glu_b[:, :, :], A["chan"][:, 0:2, :]), (taps_b[:, :], A["chan"][:, 4, :]),
                                 (taps_w[:, :, :], A["taps"]),
                                 (lamv[:, 0, :], row(A["lambda_q1"])), (lamv[:, 1, :], row(A["lambda_k1"])),
                                 (lamv[:, 2, :], row(A["lambda_q2"])), (lamv[:, 3, :], row(A["lambda_k2"]))):
                    sp.dma_start(dst, src).then_inc(tab_in, 16)
                sp.wait_ge(gl, 1)
                load_g(1)
                sp.wait_ge(wl, 1)
                load_w(1)
                with sp.Fori(0, HEADS - 2) as h:
                    sp.wait_ge(pj_ev, h * NP + NP)
                    load_bias(h + 1)
                    sp.wait_ge(gl, h + 2)
                    load_g(h + 2)
                    sp.wait_ge(wl, h + 2)
                    load_w(h + 2)
                sp.wait_ge(pj_ev, LAST * NP)
                load_bias(LAST)
                sp.wait_ge(gl, HEADS)
                load_g(LAST)

            @block.gpsimd
            def _(pool):
                with pool.Fori(0, HEADS) as h:
                    pool.wait_ge(y_done, h + 1)
                    pool.nop(nofuse=True)
                    pool.dma_start(y_dram[ds(h, 1)].rearrange("o p t -> (o p) t"), y_sum[:, :]).then_inc(y_out, 16)
                    pool.wait_ge(o_ev, h * TT + TT)
                    pool.nop(nofuse=True)
                    pool.dma_start(o_dram[ds(h, 1)].rearrange("o p t c -> (o p) (t c)"),
                                   o_head[:, :, :].rearrange("p t c -> p (t c)")).then_inc(o_out, 16)
                pool.wait_ge(y_out, 16 * HEADS)
                pool.wait_ge(o_out, 16 * HEADS)

            @block.tensor
            def _(pe):
                def glu_unit(g, k, first=False):
                    part, c0, n = GLU[k]
                    if first and k >= 2:
                        pe.wait_ge(cv_ev, k - 1)
                    elif not first and k:
                        pe.wait_ge(cv_ev, g * NG + k)
                    if k == 0:
                        pe.wait_ge(gl, g + 1)
                        if not first:
                            pe.wait_ge(pj_ev, g * NP)
                    matmul3(nc, unit_bank(k, first)[:, 0:n], [lambda k, x=x: x[:, k, part * P:part * P + P] for x in w_glu],
                            [lambda k, x=x: x[:, k, c0:c0 + n] for x in hT], KD).then_inc(cv, 1)

                def proj_unit(g, t, first=False):
                    if first and t >= 2:
                        pe.wait_ge(pj_ev, t - 1)
                    elif not first and t:
                        pe.wait_ge(pj_ev, g * NP + t)
                    if t == 0:
                        pe.wait_ge(wl, g + 1)
                        pe.wait_ge(cv_ev, g * NG + NG)
                    c0 = t * P + M if t < TT else 0
                    matmul3(nc, unit_bank(t, first)[:, 0:3 * P], [lambda k, x=x: x[:, k, c0:c0 + P] for x in hT],
                            [lambda k, x=x: x[:, k, :] for x in w_head], KD).then_inc(pj, 1)

                def scores(h, i):
                    nfr = (i + 1) * P
                    for mp in range(2):
                        r = slice(mp * HD, mp * HD + HD)
                        if i == 0:
                            pe.wait_ge(ex_done, h * 16)
                        elif i < TT - 1:
                            pe.wait_ge(ex_done, h * 16 + 2 * (i - 1) + mp + 1)
                        elif mp == 0:
                            pe.wait_ge(ex_done, h * 16 + 2 * i)
                        else:
                            pe.wait_ge(map0, h + 1)
                        for c, n in pieces(mp * L, nfr):
                            k0 = c - mp * L
                            nc.tensor.matmul(S[:, c:c + n], qT[r, i * P:i * P + P], kT[r, k0:k0 + n], start=True,
                                             stop=True)
                        c = mp * L + nfr
                        ins = nc.tensor.matmul(S[:, c:c + M], qT[r, i * P:i * P + P], kT[r, T:L], start=True,
                                               stop=True)
                        if i < TT - 1:
                            ins.then_inc(s_done, 1)
                        elif mp == 0:
                            ins.then_inc(map0, 1)
                        else:
                            ins.then_inc(s_done, 2)

                def attend(h, last):
                    g = h + 1
                    if not last:
                        glu_unit(g, 0)
                    pe.wait_ge(roped, h + 1)
                    pe.wait_ge(wt_ev, h * NB)
                    pe.wait_ge(o_ev, h * TT)
                    for b in range(5):
                        bank = OB if b % 2 else TB
                        if b >= 2:
                            pe.wait_ge(tq_ev, h * 5 + b - 1)
                        if b == 4:
                            pe.nop(nofuse=True)
                            ins = nc.tensor.transpose(bank[:, 0:M], qkv[0:M, TT, P:2 * P], identity[0:M, 0:M])
                        else:
                            for c in range(4):
                                ins = nc.tensor.transpose(bank[:, c * P:c * P + P],
                                                          qkv[:, b % 2 * 4 + c, b // 2 * P:b // 2 * P + P],
                                                          identity[:, :])
                        ins.then_inc(tq, 1)
                        if not last and b in (1, 3):
                            glu_unit(g, (b + 1) // 2)
                    pe.wait_ge(tq_ev, h * 5 + 5)
                    scores(h, 0)
                    if not last:
                        glu_unit(g, 3)
                    pe.wait_ge(v_kept, h + 1)
                    for i in range(TT):
                        if i + 1 < TT:
                            scores(h, i + 1)
                        pe.wait_ge(w_done, h * TT + i + 1)
                        seen = h * NB + before[i]
                        pe.wait_ge(wt_ev, seen)
                        pe.wait_ge(o_ev, h * TT + i)
                        for b in range(nbatch[i]):
                            if b:
                                pe.wait_ge(wt_ev, seen + 1)
                            for j in range(4 * b, min(4 * b + 4, i + 1)):
                                ins = nc.tensor.transpose(TB[:, j % 4 * P:j % 4 * P + P],
                                                          mixed[:, j * P:j * P + P], identity[:, :])
                            ins.then_inc(wt, 1)
                            if b == 0:
                                nc.tensor.transpose(OB[0:M, 3 * P:4 * P], mixed[:, (i + 1) * P:(i + 1) * P + M],
                                                    identity[:, :]).then_inc(wt, 1)
                                if not last and i == 0:
                                    glu_unit(g, 4)
                                elif not last:
                                    proj_unit(g, i if i == 1 else i + 1)
                        pe.wait_ge(wt_ev, seen + 2)
                        nc.tensor.matmul(OB[:, 0:P], mixTm[:, :], v_use[0:M, TT, :], start=True, stop=False)
                        for j in range(i + 1):
                            if j == 4:
                                pe.wait_ge(wt_ev, seen + 3)
                            ins = nc.tensor.matmul(OB[:, 0:P], mixT[:, j * P:j * P + P], v_use[:, j, :],
                                                   start=False, stop=(j == i))
                        ins.then_inc(o_done, 1)
                        if not last and i == 0:
                            glu_unit(g, 5)
                            proj_unit(g, 0)
                        elif not last and i == 1:
                            proj_unit(g, 2)

                for k in range(NG):
                    glu_unit(0, k, first=True)
                for t in range(NP):
                    proj_unit(0, t, first=True)
                with pe.Fori(0, LAST) as h:
                    attend(h, False)
                attend(LAST, True)

            @block.scalar
            def _(act):
                def high_w(n):
                    act.wait_ge(w_in, n * 16 + 16)
                    act.wait_ge(pj, n * NP)
                    nc.scalar.activation(w_head[0][:, :, :], w_raw[:, :, :], ACT.Copy).then_inc(wh, 1)

                def high_g(n):
                    act.wait_ge(g_in, n * 16 + 16)
                    act.wait_ge(cv, n * NG)
                    nc.scalar.activation(w_glu[0][:, :, :], g_raw[:, :, :], ACT.Copy).then_inc(gh, 1)

                def glu_out(g, k, first=False):
                    part, c0, n = GLU[k]
                    act.wait_ge(cv, g * NG + k + 1)
                    act.nop(nofuse=True)
                    if part:
                        nc.scalar.activation(glu_t[:, c0:c0 + n], unit_bank(k, first)[:, 0:n], ACT.Tanh,
                                             bias=glu_h[:, 1, ds(g, 1)], scale=0.5).then_inc(cv_ev, 1)
                    else:
                        nc.scalar.activation(glu_a[:, c0:c0 + n], unit_bank(k, first)[:, 0:n], ACT.Identity,
                                             bias=glu_h[:, 0, ds(g, 1)], scale=0.5).then_inc(cv_ev, 1)

                def exps(h, i):
                    n = (i + 1) * P + M
                    act.wait_ge(w_done, h * TT + max(i - 1, 0))
                    for mp in range(2):
                        c = i % 2 * 2 + mp
                        act.wait_ge(mx_done, h * 16 + 2 * i + (mp + 1 if i < TT - 1 else 2))
                        nc.scalar.activation(prob[:, i % 2, mp, 0:n], S[:, mp * L:mp * L + n], ACT.Exp,
                                             bias=negmax[:, c:c + 1],
                                             accum_out=sums[:, c:c + 1]).then_inc(ex_done, 1)

                def attend(h, last):
                    g = h + 1
                    if not last:
                        high_w(g)
                        act.wait_ge(u_done, h + 1)
                        glu_out(g, 0)
                    act.wait_ge(pj_ev, h * NP + NP)
                    act.wait_ge(o_done, h * TT)
                    nc.scalar.activation(v_use[:, :, :], qkv[:, :, 2 * P:3 * P], ACT.Copy).then_inc(v_kept, 1)
                    act.wait_ge(s_done, h * 16)
                    for b in range(5):
                        act.wait_ge(tq, h * 5 + b + 1)
                        bank = OB if b % 2 else TB
                        if b == 4:
                            nc.scalar.activation(kT[:, T:L], bank[:, 0:M], ACT.Copy).then_inc(tq_ev, 1)
                        else:
                            dst = (kT if b // 2 else qT)[:, b % 2 * BANK:b % 2 * BANK + BANK]
                            nc.scalar.activation(dst, bank[:, :], ACT.Copy,
                                                 scale=1.0 if b // 2 else HD ** -0.5).then_inc(tq_ev, 1)
                        if not last and b in (1, 3):
                            glu_out(g, (b + 1) // 2)
                    exps(h, 0)
                    if not last:
                        glu_out(g, 3)
                    act.wait_ge(o_out, h * 16)
                    for i in range(TT):
                        act.wait_ge(o_done, h * TT + i)
                        seen = h * NB + before[i]
                        act.wait_ge(wt, seen + 1)
                        n = min(4, i + 1) * P
                        nc.scalar.activation(mixT[:, 0:n], TB[:, 0:n], ACT.Copy).then_inc(wt_ev, 1)
                        act.wait_ge(wt, seen + 2)
                        nc.scalar.activation(mixTm[:, :], OB[0:M, 3 * P:4 * P], ACT.Copy).then_inc(wt_ev, 1)
                        if i + 1 < TT:
                            exps(h, i + 1)
                        if nbatch[i] == 2:
                            act.wait_ge(wt, seen + 3)
                            n = (i - 3) * P
                            nc.scalar.activation(mixT[:, BANK:BANK + n], TB[:, 0:n], ACT.Copy).then_inc(wt_ev, 1)
                        if not last and i == 0:
                            glu_out(g, 4)
                        act.wait_ge(o_done, h * TT + i + 1)
                        nc.scalar.activation(o_head[:, i, :], OB[:, 0:P], ACT.Copy).then_inc(o_ev, 1)
                        if not last and i == 0:
                            glu_out(g, 5)
                        if not last and i == 2:
                            high_g(g + 1)

                high_g(0)
                high_w(0)
                act.wait_ge(pre, 2)
                nc.scalar.activation(lam[:, 0:2], lam[:, 0:2], ACT.Exp).then_inc(lam_e, 1)
                act.wait_ge(pre, 3)
                for k in range(NG):
                    glu_out(0, k, first=True)
                high_g(1)
                with act.Fori(0, LAST) as h:
                    attend(h, False)
                attend(LAST, True)

            @block.vector
            def _(dve):
                def low_w(n):
                    dve.wait_ge(wh, n + 1)
                    nc.vector.tensor_tensor(w_head[1][:, :, :], w_raw[:, :, :], w_head[0][:, :, :].bitcast(F32),
                                            ALU.subtract).then_inc(wl, 1)

                def low_g(n):
                    dve.wait_ge(gh, n + 1)
                    nc.vector.tensor_tensor(w_glu[1][:, :, :], g_raw[:, :, :], w_glu[0][:, :, :].bitcast(F32),
                                            ALU.subtract).then_inc(gl, 1)

                def proj_out(g, t, first=False):
                    n = P if t < TT else M
                    dve.wait_ge(pj, g * NP + t + 1)
                    nc.vector.tensor_tensor(qkv[0:n, t, :], unit_bank(t, first)[0:n, 0:3 * P], b_head[0:n, :],
                                            ALU.add).then_inc(pj_ev, 1)

                def tap(c, h, k):
                    if k == 0:
                        dve.wait_ge(u_done, h + 1)
                        dve.wait_ge(y_out, h * 16)
                        c.then(nc.vector.tensor_scalar(y_sum[:, :], u_pad[:, M:M + T], taps_w[:, ds(h, 1), 0],
                                                       taps_b[:, ds(h, 1)], ALU.mult, ALU.add))
                        return
                    ins = nc.vector.scalar_tensor_tensor(y_sum[:, :], u_pad[:, M + k:M + k + T],
                                                         taps_w[:, ds(h, 1), k], y_sum[:, :], ALU.mult, ALU.add)
                    if k == TAPS - 1:
                        ins.then_inc(y_done, 1)
                    else:
                        c.then(ins)

                def maxes(c, h, i):
                    nfr = (i + 1) * P
                    for mp in range(2):
                        dve.wait_ge(s_done, h * 16 + 2 * i + mp + 1)
                        s = S[:, mp * L:mp * L + nfr + M]
                        c.then(nc.vector.memset(s[0:CHUNK, nfr - CHUNK:nfr], -1e30))
                        q = i % 2 * 2 + mp
                        nc.vector.tensor_reduce(negmax[:, q:q + 1], s, AX.X, ALU.max, negate=True).then_inc(mx_done, 1)

                def attend(h, last):
                    g = h + 1
                    c = Chain(dve, chain, h * DVE_PER)
                    dve.wait_ge(pj_ev, h * NP + NP)
                    qk = qkv[:, :, 0:2 * P].rearrange("p t (x d) -> p t x d", d=HD)
                    r1, r2 = qk[:, :, :, 0:ROT], qk[:, :, :, ROT:2 * ROT]
                    bc = [x[:, :, :].unsqueeze(2).to_broadcast([P, TT + 1, 4, ROT]) for x in (cos_t, sin_t)]
                    tmp = [rot[:, j, :].rearrange("p (t x d) -> p t x d", t=TT + 1, x=4) for j in range(4)]
                    for j, (a, b) in enumerate(((r1, bc[0]), (r2, bc[1]), (r2, bc[0]), (r1, bc[1]))):
                        ins = nc.vector.tensor_tensor(tmp[j], a, b, ALU.mult)
                    c.then(ins)
                    nc.vector.tensor_tensor(r1, tmp[0], tmp[1], ALU.subtract)
                    nc.vector.tensor_tensor(r2, tmp[2], tmp[3], ALU.add).then_inc(roped, 1)
                    dve.wait_ge(cv_ev, h * NG + NG)
                    dve.wait_ge(y_done, h)
                    nc.vector.scalar_tensor_tensor(u_pad[:, PAD:PAD + L], glu_t[:, :], 1.0, glu_a[:, :],
                                                   ALU.add, ALU.mult).then_inc(u_done, 1)
                    if not last:
                        low_w(g)
                    k = 7
                    for j in range(k):
                        tap(c, h, j)
                    maxes(c, h, 0)
                    for i in range(TT):
                        n = (i + 1) * P + M
                        q = i % 2 * 2
                        dve.wait_ge(w_done, h * TT + i)
                        dve.wait_ge(ex_done, h * 16 + 2 * i + 2)
                        c.then(nc.vector.reciprocal(rr[:, :], sums[:, q:q + 2]))
                        c.then(nc.vector.tensor_tensor(rr[:, 1:2], rr[:, 1:2], lam[:, 3:4], ALU.mult))
                        second = prob[:, i % 2, 1, 0:n]
                        c.then(nc.vector.tensor_scalar(second, second, rr[:, 1:2], None, ALU.mult))
                        dve.wait_ge(wt, h * NB + before[i])
                        nc.vector.scalar_tensor_tensor(mixed[:, 0:n], prob[:, i % 2, 0, 0:n], rr[:, 0:1],
                                                       second, ALU.mult, ALU.subtract).then_inc(w_done, 1)
                        if not last and i == 1:
                            dve.wait_ge(tq, h * 5 + 5)
                            dve.wait_ge(v_kept, h + 1)
                            dve.wait_ge(b_in, g * 16 + 16)
                            proj_out(g, 0)
                        if not last and i == 2:
                            proj_out(g, 2)
                        if i + 1 < TT:
                            maxes(c, h, i + 1)
                        more = (TAPS - k) // (TT - i)
                        for j in range(k, k + more):
                            tap(c, h, j)
                        k += more
                        if not last and i >= 1:
                            proj_out(g, i if i == 1 else i + 1)
                        if not last and i == 3:
                            low_g(g + 1)
                    assert k == TAPS and c.n == DVE_PER, (k, c.n)

                nc.vector.memset(qkv[:, TT, :], 0.0).then_inc(init, 1)
                nc.vector.memset(u_pad[:, :], 0.0).then_inc(init, 1)
                dve.wait_ge(init, 2)
                low_g(0)
                low_w(0)
                dve.wait_ge(tab_in, 9 * 16)
                c0 = Chain(dve, sem("mx_lam_chain"))
                c0.then(nc.vector.tensor_tensor(lamp[:, :, :], lamv[:, 0:4:2, :], lamv[:, 1:4:2, :], ALU.mult))
                nc.vector.tensor_reduce(lam[:, 0:2], lamp[:, :, :], AX.X, ALU.add).then_inc(pre, 2)
                nc.vector.tensor_scalar(glu_h[:, :, :], glu_b[:, :, :], 0.5, None, ALU.mult).then_inc(pre, 1)
                dve.wait_ge(lam_e, 1)
                c0.then(nc.vector.tensor_tensor(lam[:, 2:3], lam[:, 0:1], lam[:, 1:2], ALU.subtract))
                c0.then(nc.vector.tensor_scalar(lam[:, 3:4], lam[:, 2:3], LAM_INIT, None, ALU.add))
                dve.wait_ge(b_in, 16)
                for t in range(NP):
                    proj_out(0, t, first=True)
                low_g(1)
                with dve.Fori(0, LAST) as h:
                    attend(h, False)
                attend(LAST, True)


def branch(nc, sem, A, identity, hT, o_dram, y_dram, th_dram, yconv, oT, at):
    m = Map(nc, at)
    oall = m.take("oall", [P, HEADS, TT, P])
    sq = m.take("br_sq", [P, 2, TT, P])
    ms = m.take("br_ms", [P, 5, TT * HEADS])
    sub_g = m.take("br_g", [P, 2])
    chan = m.take("br_chan", [P, 2, HEADS])
    ones = m.take("br_ones", [P, P])
    sqc = sq[:, :, :, :].rearrange("p s t c -> p s (t c)")
    rstd = m.take("br_rstd", [P, T])
    eps = m.take("br_eps", [P, 1])
    g_raw = m.take("br_g_raw", [P, KD, 2 * P])
    wg = [[m.take(f"br_wg{x}{j}", [P, KD, P], F32R) for j in range(2)] for x in range(2)]
    th = m.take("br_th", [P, 2, T])
    bias = m.take("br_bias", [P, 2, HEADS])
    half = m.take("br_half", [P, 2, HEADS])
    with nc.psum_tensor("br_t", [P, 2, BANK], F32) as TB, nc.psum_tensor("br_mean", [P, T], F32) as MEAN, \
            nc.psum_tensor("br_var", [P, T], F32) as VAR, nc.psum_tensor("br_gate", [P, 2, BANK], F32) as GP:
        y_in = [sem(f"br_y_in{j}") for j in range(4)]
        o_in = [sem(f"br_o_in{j}") for j in range(HEADS)]
        eps_ready = sem("br_eps_ready")
        par_in = sem("br_par")
        ready = sem("br_ones_ready")
        chain = sem("br_chain")
        root = sem("br_root")
        rooted = sem("br_rooted")
        g8 = sem("br_g8")
        summed, small_sq = sem("br_summed"), sem("br_small_sq")
        o_norm = sem("br_o_norm")
        mean_done = sem("br_mean_s")
        cent = sem("br_cent")
        sq_done = sem("br_sq_done")
        var_done = sem("br_var_s")
        tr, tr_ev = sem("br_tr"), sem("br_tr_ev")
        z_done = sem("br_z")
        g_in, halved = sem("br_g_in"), sem("br_halved")
        gh, gl = sem("br_gh"), sem("br_gl")
        gate_pr, th_done = sem("br_gate_pr"), sem("br_th_done")
        th_out = [sem("br_th_out0"), sem("br_th_out1")]
        NH = TT * HEADS
        with nc.Block() as block:
            @block.sync
            def _(sp):
                def load_gate(t):
                    sp.dma_start(g_raw[:, :, :], A["w_gate"][ds(t, 1)].rearrange("o p k c -> (o p) k c")
                                 ).then_inc(g_in, 16)

                load_gate(0)
                sp.dma_start(bias[:, :, :], A["chan"][:, 2:4, :]).then_inc(par_in, 16)
                sp.dma_start(sub_g[:, 0:1], A["subln_col"]).then_inc(par_in, 16)
                sp.dma_start(chan[:, :, :], A["chan"][:, 5:7, :]).then_inc(par_in, 16)
                for h in range(HEADS):
                    sp.dma_start(oall[:, h, :, :], o_dram[h]).then_inc(o_in[h], 16)
                for h in range(HEADS):
                    sp.dma_start(yconv[:, h, :], y_dram[h]).then_inc(y_in[h % 4], 16)
                with sp.Fori(0, TT - 1) as t:
                    sp.wait_ge(gl, t * 2 + 2)
                    load_gate(t + 1)

            @block.vector
            def _(dve):
                def low(t, j):
                    dve.wait_ge(gh, t * 2 + j + 1)
                    nc.vector.tensor_tensor(wg[1][j][:, :, :], g_raw[:, :, j * P:j * P + P],
                                            wg[0][j][:, :, :].bitcast(F32), ALU.subtract).then_inc(gl, 1)

                c = Chain(dve, chain)
                low(0, 0)
                low(0, 1)
                nc.vector.memset(ones[:, :], 1.0 / D).then_inc(ready, 1)
                dve.wait_ge(par_in, 48)
                nc.vector.tensor_scalar(half[:, :, :], bias[:, :, :], 0.5, None, ALU.mult).then_inc(halved, 1)
                nc.vector.tensor_scalar(sub_g[:, 1:2], sub_g[:, 0:1], 1.0 - LAM_INIT, None, ALU.mult).then_inc(g8, 1)
                for h in range(HEADS):
                    o = slice(h * TT, h * TT + TT)
                    dve.wait_ge(o_in[h], 16)
                    c.then(nc.vector.tensor_scalar(sq[:, 0, :, :], oall[:, h, :, :], O_LIMIT, -O_LIMIT, ALU.min,
                                                   ALU.max))
                    c.then(nc.vector.tensor_tensor(sq[:, 0, :, :], sq[:, 0, :, :], sq[:, 0, :, :], ALU.mult))
                    c.then(nc.vector.tensor_reduce(ms[:, 0, o], sq[:, 0, :, :], AX.X, ALU.add))
                    dve.wait_ge(small_sq, h + 1)
                    nc.vector.tensor_reduce(ms[:, 3, o], sq[:, 1, :, :], AX.X, ALU.add).then_inc(summed, 1)
                    if h == 2:
                        low(1, 0)
                    if h == 5:
                        low(1, 1)
                dve.wait_ge(summed, HEADS)
                c.then(nc.vector.tensor_scalar(ms[:, 2, :], ms[:, 3, :], 2.0 ** -60, None, ALU.is_ge))
                nc.vector.tensor_scalar(ms[:, 0, :], ms[:, 0, :], 1.0 / P, LN_EPS, ALU.mult, ALU.add)
                c.then(nc.vector.tensor_scalar(ms[:, 4, :], ms[:, 2, :], -1.0, 1.0, ALU.mult, ALU.add))
                nc.vector.scalar_tensor_tensor(ms[:, 1, :], ms[:, 3, :], 1.0 / P, ms[:, 2, :], ALU.mult, ALU.mult)
                c.then(nc.vector.tensor_tensor(ms[:, 0, :], ms[:, 0, :], ms[:, 4, :], ALU.mult))
                nc.vector.tensor_tensor(ms[:, 1, :], ms[:, 1, :], ms[:, 0, :], ALU.add).then_inc(root, 1)
                c.then(nc.vector.scalar_tensor_tensor(ms[:, 4, :], ms[:, 2, :], 2.0 ** -70, ms[:, 4, :], ALU.mult,
                                                      ALU.add))
                c.then(nc.vector.scalar_tensor_tensor(ms[:, 4, :], ms[:, 3, :], 2.0 ** -12, ms[:, 4, :], ALU.is_lt,
                                                      ALU.mult))
                dve.wait_ge(mean_done, 1)
                for h in range(HEADS):
                    nc.vector.tensor_tensor(yconv[:, h, :], yconv[:, h, :], MEAN[:, :], ALU.subtract).then_inc(cent, 1)
                low(2, 0)
                dve.wait_ge(rooted, 1)
                c.then(nc.vector.reciprocal(ms[:, 2, :], ms[:, 1, :]))
                c.then(nc.vector.tensor_tensor(ms[:, 2, :], ms[:, 2, :], ms[:, 4, :], ALU.mult))
                o2 = oall[:, :, :, :].rearrange("p h t c -> p (h t) c")
                nc.vector.tensor_tensor(o2, o2, ms[:, 2, :].unsqueeze(2).to_broadcast([P, NH, P]),
                                        ALU.mult).then_inc(o_norm, 1)
                low(2, 1)
                dve.wait_ge(rooted, 2)
                c.then(nc.vector.reciprocal(rstd[:, :], rstd[:, :]))
                for h in range(HEADS):
                    nc.vector.tensor_tensor(yconv[:, h, :], yconv[:, h, :], rstd[:, :], ALU.mult).then_inc(z_done, 1)
                low(3, 0)
                low(3, 1)
                with dve.Fori(3, TT - 1) as t:
                    low(t + 1, 0)
                    low(t + 1, 1)

            @block.tensor
            def _(pe):
                def gate_tile(t, first=False):
                    for j in range(2):
                        pe.wait_ge(gl, t * 2 + j + 1)
                        for f in range(2):
                            if not (first and j == 0):
                                pe.wait_ge(th_done, t * 4 + 2 * j + f - 1)
                            matmul3(nc, GP[:, f, :], [lambda k, x=x: x[j][:, k, :] for x in wg],
                                    [lambda k, x=x: x[:, k, M + f * BANK:M + f * BANK + BANK] for x in hT],
                                    KD).then_inc(gate_pr, 1)

                gate_tile(0, first=True)
                pe.wait_ge(ready, 1)
                for q in y_in:
                    pe.wait_ge(q, 16 * HEADS // 4)
                for f in range(2):
                    for h in range(HEADS):
                        ins = nc.tensor.matmul(MEAN[:, f * BANK:f * BANK + BANK], ones[:, :],
                                               yconv[:, h, f * BANK:f * BANK + BANK], start=(h == 0),
                                               stop=(h == HEADS - 1))
                ins.then_inc(mean_done, 1)
                gate_tile(1)
                for h in range(HEADS):
                    pe.wait_ge(sq_done, h + 1)
                    for f in range(2):
                        ins = nc.tensor.matmul(VAR[:, f * BANK:f * BANK + BANK], ones[:, :],
                                               sqc[:, h % 2, f * BANK:f * BANK + BANK], start=(h == 0),
                                               stop=(h == HEADS - 1))
                    ins.then_inc(var_done, 1)
                gate_tile(2)
                pe.wait_ge(o_norm, 1)
                n = 0
                for h in range(HEADS):
                    for f in range(2):
                        if n >= 2:
                            pe.wait_ge(tr_ev, n - 1)
                        for t in range(4):
                            ins = nc.tensor.transpose(TB[:, n % 2, t * P:t * P + P], oall[:, h, 4 * f + t, :],
                                                      identity[:, :])
                        ins.then_inc(tr, 1)
                        n += 1
                with pe.Fori(3, TT) as t:
                    gate_tile(t)

            @block.scalar
            def _(act):
                def high(t, j):
                    act.wait_ge(g_in, t * 16 + 16)
                    act.wait_ge(gate_pr, t * 4 - 2 + 2 * j if not isinstance(t, int) or t else 0)
                    nc.scalar.activation(wg[0][j][:, :, :], g_raw[:, :, j * P:j * P + P], ACT.Copy).then_inc(gh, 1)

                def tanh(t, j, f):
                    act.wait_ge(th_out[j], t * 16)
                    act.wait_ge(gate_pr, t * 4 + 2 * j + f + 1)
                    act.nop(nofuse=True)
                    nc.scalar.activation(th[:, j, f * BANK:f * BANK + BANK], GP[:, f, :], ACT.Tanh,
                                         bias=half[:, j, ds(t, 1)], scale=0.5).then_inc(th_done, 1)

                def small_squares(h):
                    act.wait_ge(o_in[h], 16)
                    act.wait_ge(summed, h)
                    nc.scalar.activation(sq[:, 1, :, :], oall[:, h, :, :], ACT.Square,
                                         scale=2.0 ** -70).then_inc(small_sq, 1)

                high(0, 0)
                high(0, 1)
                act.wait_ge(halved, 1)
                small_squares(0)
                small_squares(1)
                for f in range(2):
                    tanh(0, 0, f)
                high(1, 0)
                for h in (2, 3, 4):
                    small_squares(h)
                for f in range(2):
                    tanh(0, 1, f)
                high(1, 1)
                for h in (5, 6, 7):
                    small_squares(h)
                act.wait_ge(root, 1)
                nc.scalar.activation(ms[:, 1, :], ms[:, 1, :], ACT.Sqrt).then_inc(rooted, 1)
                for f in range(2):
                    tanh(1, 0, f)
                high(2, 0)
                for h in range(HEADS):
                    act.wait_ge(cent, h + 1)
                    if h >= 2:
                        act.wait_ge(var_done, h - 1)
                    nc.scalar.activation(sqc[:, h % 2, :], yconv[:, h, :], ACT.Square).then_inc(sq_done, 1)
                for f in range(2):
                    tanh(1, 1, f)
                high(2, 1)
                act.wait_ge(var_done, HEADS)
                act.wait_ge(eps_ready, 1)
                nc.scalar.activation(rstd[:, :], VAR[:, :], ACT.Sqrt, bias=eps[:, :]).then_inc(rooted, 1)
                for j in range(2):
                    for f in range(2):
                        tanh(2, j, f)
                    high(3, j)
                act.wait_ge(g8, 1)
                n = 0
                for h in range(HEADS):
                    for f in range(2):
                        act.wait_ge(tr, n + 1)
                        nc.scalar.activation(oT[:, h, f * BANK:f * BANK + BANK], TB[:, n % 2, :], ACT.Copy,
                                             scale=sub_g[:, 1:2]).then_inc(tr_ev, 1)
                        n += 1
                for h in range(HEADS):
                    act.wait_ge(z_done, h + 1)
                    nc.scalar.activation(yconv[:, h, :], yconv[:, h, :], ACT.Silu, bias=chan[:, 1, h:h + 1],
                                         scale=chan[:, 0, h:h + 1])
                with act.Fori(3, TT - 1) as t:
                    for j in range(2):
                        for f in range(2):
                            tanh(t, j, f)
                        high(t + 1, j)
                for j in range(2):
                    for f in range(2):
                        tanh(TT - 1, j, f)

            @block.gpsimd
            def _(pool):
                nc.gpsimd.memset(eps[:, :], LN_EPS).then_inc(eps_ready, 1)
                with pool.Fori(0, TT) as t:
                    for j in range(2):
                        pool.wait_ge(th_done, t * 4 + 2 * j + 2)
                        pool.nop(nofuse=True)
                        pool.dma_start(th_dram[ds(t, 1), :, j, :].rearrange("o p c -> (o p) c"),
                                       th[:, j, :]).then_inc(th_out[j], 16)
                for j in range(2):
                    pool.wait_ge(th_out[j], 16 * TT)


def merge(nc, sem, A, src, src_hi, src_lo, th_dram, m_dram, at):
    m = Map(nc, at)
    w_raw = m.take("mg_w_raw", [P, 2, KD, P])
    wp = [m.take(f"mg_wp{x}", [P, 2, 2, KD, P], F32R) for x in range(2)]
    th = m.take("mg_th", [P, 2, 2, T])
    cd = m.take("mg_cd", [P, 2, BANK])
    part = m.take("mg_part", [P, 2, 2, BANK])
    done = m.take("mg_done", [P, 2, BANK])
    bias = m.take("mg_bias", [P, 2, HEADS])
    with nc.psum_tensor("mg_ps", [P, 2, 2, 2, BANK], F32) as PS:
        par_in, w_in = sem("mg_par"), sem("mg_w_in")
        th_in = [sem("mg_th_in0"), sem("mg_th_in1")]
        halved = sem("mg_halved")
        xh, xl = sem("mg_xh"), sem("mg_xl")
        wh, wl = sem("mg_wh"), sem("mg_wl")
        pr = sem("mg_pr")
        cd_done = sem("mg_cd_done")
        part_done = sem("mg_part_done")
        m_done = sem("mg_m_done")
        m_out = [sem("mg_m_out0"), sem("mg_m_out1")]
        with nc.Block() as block:
            @block.sync
            def _(sp):
                def load_w(t):
                    for j, name in enumerate(("w_attn", "w_conv")):
                        sp.dma_start(w_raw[:, j, :, :], A[name][ds(t, 1)].rearrange("o p k c -> (o p) k c")
                                     ).then_inc(w_in, 16)

                def load_th(t, u):
                    sp.wait_ge(m_done, t * 2 + 1)
                    sp.dma_start(th[:, u, :, :], th_dram[ds(t, 1)].rearrange("o p j c -> (o p) j c")
                                 ).then_inc(th_in[u], 16)

                load_w(0)
                sp.dma_start(bias[:, 0, :], A["chan"][:, 7, :]).then_inc(par_in, 16)
                load_th(0, 0)
                with sp.Fori(0, TT // 2 - 1) as i:
                    for u in range(2):
                        t = i * 2 + u
                        sp.wait_ge(wl, t + 1)
                        load_w(t + 1)
                        load_th(t + 1, 1 - u)
                sp.wait_ge(wl, TT - 1)
                load_w(TT - 1)
                load_th(TT - 1, 1)

            @block.tensor
            def _(pe):
                def tile(t, u, first=False):
                    pe.wait_ge(wl, t + 1)
                    pe.wait_ge(m_done, t * 2 + 1)
                    for j in range(2):
                        for f in range(2):
                            if first and f == 0:
                                for k in range(KD):
                                    pe.wait_ge(xl, j * KD + k + 1)
                                    for y, (w, x) in enumerate(((0, 0), (0, 1), (1, 0))):
                                        ins = nc.tensor.matmul(PS[:, u, f, j, :], wp[w][:, u, j, k, :],
                                                               (src_hi, src_lo)[x][:, j, k, f * BANK:f * BANK + BANK],
                                                               start=(k == 0 and y == 0),
                                                               stop=(k == KD - 1 and y == 2))
                            else:
                                ins = matmul3(nc, PS[:, u, f, j, :], [lambda k, w=w: w[:, u, j, k, :] for w in wp],
                                              [lambda k, x=x: x[:, j, k, f * BANK:f * BANK + BANK]
                                               for x in (src_hi, src_lo)], KD)
                            if j == 1:
                                ins.then_inc(pr, 1)

                tile(0, 0, first=True)
                tile(1, 1)
                with pe.Fori(1, TT // 2) as i:
                    for u in range(2):
                        tile(i * 2 + u, u)

            @block.scalar
            def _(act):
                def high(t, u, first=False):
                    act.wait_ge(w_in, t * 32 + 32)
                    if not first:
                        act.wait_ge(pr, t * 2 - 2)
                    nc.scalar.activation(wp[0][:, u, :, :, :], w_raw[:, :, :, :], ACT.Copy).then_inc(wh, 1)

                def tile(t, u, last=False):
                    if not last:
                        high(t + 1, 1 - u)
                    for f in range(2):
                        act.wait_ge(m_done, t * 2 + f + 2)
                        act.wait_ge(pr, t * 2 + f + 1)
                        act.nop(nofuse=True)
                        nc.scalar.activation(cd[:, f, :], PS[:, u, f, 1, :], ACT.Identity,
                                             bias=bias[:, 1, ds(t, 1)], scale=0.5).then_inc(cd_done, 1)

                high(0, 0, first=True)
                for j in range(2):
                    for k in range(KD):
                        nc.scalar.activation(src_hi[:, j, k, :], src[:, j, k, :], ACT.Copy).then_inc(xh, 1)
                act.wait_ge(halved, 1)
                with act.Fori(0, TT // 2 - 1) as i:
                    for u in range(2):
                        tile(i * 2 + u, u)
                tile(TT - 2, 0)
                tile(TT - 1, 1, last=True)

            @block.gpsimd
            def _(pool):
                with pool.Fori(0, TT) as t:
                    for f in range(2):
                        pool.wait_ge(m_done, t * 2 + f + 4)
                        pool.nop(nofuse=True)
                        pool.dma_start(m_dram[ds(t, 1), :, f * BANK:f * BANK + BANK].rearrange("o p t -> (o p) t"),
                                       done[:, f, :]).then_inc(m_out[f], 16)
                for f in range(2):
                    pool.wait_ge(m_out[f], 16 * TT)

            @block.vector
            def _(dve):
                def low(t, u):
                    dve.wait_ge(wh, t + 1)
                    nc.vector.tensor_tensor(wp[1][:, u, :, :, :], w_raw[:, :, :, :],
                                            wp[0][:, u, :, :, :].bitcast(F32), ALU.subtract).then_inc(wl, 1)

                def tile(t, u, i, last=False):
                    if not last:
                        low(t + 1, 1 - u)
                    dve.wait_ge(th_in[u], i * 16 + 16)
                    for f in range(2):
                        dve.wait_ge(cd_done, t * 2 + f + 1)
                        fr = slice(f * BANK, f * BANK + BANK)
                        nc.vector.scalar_tensor_tensor(part[:, f, 0, :], th[:, u, 0, fr], 1.0, PS[:, u, f, 0, :],
                                                       ALU.add, ALU.mult)
                        nc.vector.scalar_tensor_tensor(part[:, f, 1, :], th[:, u, 1, fr], 1.0, cd[:, f, :],
                                                       ALU.add, ALU.mult).then_inc(part_done, 1)
                        dve.wait_ge(m_out[f], t * 16)
                        dve.wait_ge(part_done, t * 2 + f + 1)
                        nc.vector.scalar_tensor_tensor(done[:, f, :], part[:, f, 0, :], 0.5, part[:, f, 1, :],
                                                       ALU.mult, ALU.add).then_inc(m_done, 1)

                nc.vector.memset(part[:, :, :, :], 0.0).then_inc(m_done, 3)
                dve.wait_ge(m_done, 3)
                low(0, 0)
                for j in range(2):
                    for k in range(KD):
                        dve.wait_ge(xh, j * KD + k + 1)
                        nc.vector.tensor_tensor(src_lo[:, j, k, :], src[:, j, k, :],
                                                src_hi[:, j, k, :].bitcast(F32), ALU.subtract).then_inc(xl, 1)
                dve.wait_ge(par_in, 16)
                nc.vector.tensor_scalar(bias[:, 1, :], bias[:, 0, :], 0.5, None, ALU.mult).then_inc(halved, 1)
                with dve.Fori(0, TT // 2 - 1) as i:
                    for u in range(2):
                        tile(i * 2 + u, u, i)
                tile(TT - 2, 0, TT // 2 - 1)
                tile(TT - 1, 1, TT // 2 - 1, last=True)


def layer_norm_tile(dve, c, nc, x, out, stats, mv, gamma, beta, root, rooted, n):
    nc.vector.bn_stats(stats[:, 0, :], x[:, 0:BANK])
    c.then(nc.vector.bn_stats(stats[:, 1, :], x[:, BANK:D]))
    c.then(nc.vector.bn_aggr(mv[:, 0:2], stats[:, :, :].rearrange("p a b -> p (a b)")))
    nc.vector.tensor_scalar(mv[:, 2:3], mv[:, 1:2], LN_EPS, None, ALU.add).then_inc(root, 1)
    dve.wait_ge(rooted, n + 1)
    c.then(nc.vector.reciprocal(mv[:, 3:4], mv[:, 3:4]))
    c.then(nc.vector.tensor_scalar(x, x, mv[:, 0:1], mv[:, 3:4], ALU.subtract, ALU.mult))
    c.then(nc.vector.tensor_tensor(x, x, gamma, ALU.mult))
    return nc.vector.tensor_tensor(out, x, beta, ALU.add)


def project(nc, sem, A, m_dram, identity, h_dram, h1T, acc_dram, at):
    m = Map(nc, at)
    mT = m.take("pj_m", [P, KD, T])
    wout = m.take("pj_w", [P, KD, D])
    bout = m.take("pj_bout", [P, D])
    gamma = m.take("pj_gamma", [P, D])
    beta = m.take("pj_beta", [P, D])
    h_in = m.take("pj_h", [P, 2, D])
    r = m.take("pj_r", [P, 2, D])
    scaled = m.take("pj_scaled", [P, 2, D])
    stats = m.take("pj_stats", [P, 2, 6])
    mv = m.take("pj_mv", [P, 4])
    with nc.psum_tensor("pj_y", [P, 2, D], F32) as Y, nc.psum_tensor("pj_t", [P, 4, BANK], F32) as TB:
        par_in, h_ld = sem("pj_par"), [sem("pj_h_in0"), sem("pj_h_in1")]
        mw_in = [sem(f"pj_mw_in{k}") for k in range(KD)]
        y_done, r_done = sem("pj_y_done"), sem("pj_r_done")
        chain, root, rooted = sem("pj_chain"), sem("pj_root"), sem("pj_rooted")
        h1_done, tr, ac = sem("pj_h1"), sem("pj_tr"), sem("pj_acc")
        hi_done, lo_done = sem("pj_hi"), sem("pj_lo")
        acc_out = [sem("pj_acc_out0"), sem("pj_acc_out1")]

        def half(t, f):
            fr = slice(t * P, t * P + P)
            return (TB[:, t % 2 * 2 + f, :].rearrange("p (k c) -> p k c", k=4),
                    h1T[0][:, 4 * f:4 * f + 4, fr], h1T[1][:, 4 * f:4 * f + 4, fr])

        with nc.Block() as block:
            @block.sync
            def _(sp):
                for k in range(KD):
                    sp.dma_start(mT[:, k, :], m_dram[k]).then_inc(mw_in[k], 16)
                    sp.dma_start(wout[:, k, :], A["w_out"][:, k, :]).then_inc(mw_in[k], 16)
                for dst, name in ((bout, "b_out"), (gamma, "ln1_g"), (beta, "ln1_b")):
                    sp.dma_start(dst[:, :], row(A[name])).then_inc(par_in, 16)
                for t in range(TT):
                    if t >= 2:
                        sp.wait_ge(r_done, t - 1)
                    sp.dma_start(h_in[:, t % 2, :], h_dram[t]).then_inc(h_ld[t % 2], 16)

            @block.gpsimd
            def _(pool):
                for t in range(TT):
                    pool.wait_ge(ac, t + 1)
                    pool.dma_start(acc_dram[t], scaled[:, t % 2, :]).then_inc(acc_out[t % 2], 16)
                for q in acc_out:
                    pool.wait_ge(q, 16 * TT // 2)

            @block.tensor
            def _(pe):
                def turn(t):
                    pe.wait_ge(h1_done, t + 1)
                    for f in range(2):
                        if t >= 2:
                            pe.wait_ge(lo_done, 2 * (t - 2) + f + 1)
                        for k in range(4):
                            ins = nc.tensor.transpose(TB[:, t % 2 * 2 + f, k * P:k * P + P],
                                                      r[:, t % 2, (4 * f + k) * P:(4 * f + k + 1) * P], identity[:, :])
                        ins.then_inc(tr, 1)

                for t in range(TT):
                    if t >= 2:
                        pe.wait_ge(r_done, t - 1)
                    for f in range(2):
                        for k in range(KD):
                            if t == 0 and f == 0:
                                pe.wait_ge(mw_in[k], 32)
                            ins = nc.tensor.matmul(Y[:, t % 2, f * BANK:f * BANK + BANK], mT[:, k, t * P:t * P + P],
                                                   wout[:, k, f * BANK:f * BANK + BANK], start=(k == 0),
                                                   stop=(k == KD - 1))
                    ins.then_inc(y_done, 1)
                    if t:
                        turn(t - 1)
                turn(TT - 1)

            @block.vector
            def _(dve):
                c = Chain(dve, chain)
                dve.wait_ge(par_in, 48)

                def low(t):
                    for f in range(2):
                        ps, hi, lo = half(t, f)
                        dve.wait_ge(hi_done, 2 * t + f + 1)
                        nc.vector.tensor_tensor(lo, ps, hi.bitcast(F32), ALU.subtract).then_inc(lo_done, 1)

                for t in range(TT):
                    u = t % 2
                    dve.wait_ge(y_done, t + 1)
                    if t >= 2:
                        dve.wait_ge(ac, t - 1)
                    c.then(nc.vector.tensor_tensor(r[:, u, :], Y[:, u, :], bout[:, :], ALU.add))
                    dve.wait_ge(h_ld[u], 16 * (t // 2 + 1))
                    nc.vector.scalar_tensor_tensor(r[:, u, :], h_in[:, u, :], ALPHA, r[:, u, :], ALU.mult,
                                                   ALU.add).then_inc(r_done, 1)
                    dve.wait_ge(r_done, t + 1)
                    layer_norm_tile(dve, c, nc, r[:, u, :], r[:, u, :], stats, mv, gamma[:, :], beta[:, :], root,
                                    rooted, t).then_inc(h1_done, 1)
                    if t:
                        low(t - 1)
                low(TT - 1)

            @block.scalar
            def _(act):
                def store(t):
                    act.wait_ge(h1_done, t + 1)
                    if t >= 2:
                        act.wait_ge(acc_out[t % 2], 16 * (t // 2))
                    nc.scalar.activation(scaled[:, t % 2, :], r[:, t % 2, :], ACT.Copy, scale=ALPHA).then_inc(ac, 1)
                    for f in range(2):
                        ps, hi, _ = half(t, f)
                        act.wait_ge(tr, 2 * t + f + 1)
                        nc.scalar.activation(hi, ps, ACT.Copy).then_inc(hi_done, 1)

                for t in range(TT):
                    act.wait_ge(root, t + 1)
                    nc.scalar.activation(mv[:, 3:4], mv[:, 2:3], ACT.Sqrt).then_inc(rooted, 1)
                    if t:
                        store(t - 1)
                store(TT - 1)


class Ahead:

    def __init__(self, nc, sem, name, m, banks, h1T, slots):
        self.nc, self.banks, self.h1T, self.slots = nc, banks, h1T, slots
        self.raw = m.take(name + "_u_raw", [P, 2, KD, E2 * P])
        self.parts = [m.take(name + f"_u{j}", [P, 2, KD, E2 * P], F32R) for j in range(2)]
        self.coef = m.take(name + "_coef", [P, slots, E2, T])
        self.u_in = [sem(name + "_u_in0"), sem(name + "_u_in1")]
        self.high_made = sem(name + "_u_high")
        self.low_made = sem(name + "_u_low")
        self.up_done = sem(name + "_up")
        self.gelu_done = sem(name + "_gelu")
        self.stored = [sem(name + "_a_out0"), sem(name + "_a_out1")]

    def credits(self, dve):
        for q, n in ((self.low_made, 1), (self.up_done, 2), (self.gelu_done, 2)):
            self.nc.vector.memset(self.coef[:, 0, 0, 0:8], 0.0).then_inc(q, n)
            dve.wait_ge(q, n)

    def load(self, sp, A, first, n, slot):
        sp.wait_ge(self.low_made, n)
        sp.dma_start(self.raw[:, slot, :, :], A["u_t"][ds(n + first, 1)].rearrange("o p k e -> (o p) k e")
                     ).then_inc(self.u_in[slot], 16)

    def high(self, act, n, slot, i):
        act.wait_ge(self.u_in[slot], i * 16 + 16)
        act.wait_ge(self.up_done, n * E2)
        self.nc.scalar.activation(self.parts[0][:, slot, :, :], self.raw[:, slot, :, :],
                                  ACT.Copy).then_inc(self.high_made, 1)

    def low(self, dve, n, slot):
        dve.wait_ge(self.high_made, n + 1)
        self.nc.vector.tensor_tensor(self.parts[1][:, slot, :, :], self.raw[:, slot, :, :],
                                     self.parts[0][:, slot, :, :].bitcast(F32),
                                     ALU.subtract).then_inc(self.low_made, 1)

    def up(self, pe, n, slot, first=0, last=E2 * 2 * KD):
        if first == 0:
            pe.wait_ge(self.low_made, n + 2)
        for c in range(first, last):
            j, f, k = c // (2 * KD), c // KD % 2, c % KD
            if f == 0 and k == 0:
                pe.wait_ge(self.gelu_done, n * E2 + j + 1)
            fr = slice(f * BANK, f * BANK + BANK)
            for y, (w, h) in enumerate(((0, 0), (0, 1), (1, 0))):
                ins = self.nc.tensor.matmul(self.banks[:, j, fr], self.parts[w][:, slot, k, j * P:j * P + P],
                                            self.h1T[h][:, k, fr], start=(k == 0 and y == 0),
                                            stop=(k == KD - 1 and y == 2))
            if f == 1 and k == KD - 1:
                ins.then_inc(self.up_done, 1)

    def gelu(self, act, n, slot, i, j):
        if self.slots == 2:
            act.wait_ge(self.stored[slot], i * 16)
        else:
            act.wait_ge(self.stored[1 - slot], (i + slot) * 16)
        act.wait_ge(self.up_done, n * E2 + j + 1 + 2)
        self.nc.scalar.activation(self.coef[:, slot % self.slots, j, :], self.banks[:, j, :], ACT.Gelu).then_inc(self.gelu_done, 1)

    def store(self, pool, a_dram, first, n, slot):
        pool.wait_ge(self.gelu_done, n * E2 + E2 + 2)
        pool.nop(nofuse=True)
        pool.dma_start(a_dram[ds(n + first, 1)].rearrange("o p j t -> (o p) (j t)"),
                       self.coef[:, slot % self.slots, :, :].rearrange("p j t -> p (j t)")).then_inc(self.stored[slot], 16)


def search(nc, sem, A, h1T, a_dram, identity, picks, at):
    m = Map(nc, at)
    PER = 20
    SEARCHED = 2
    with nc.psum_tensor("se_a", [P, E2, T], F32) as PA, nc.psum_tensor("se_q", [P, 2, BANK], F32) as Q, \
            nc.psum_tensor("se_s", [P, TT, KEYS], F32) as S:
        ahead = Ahead(nc, sem, "se", m, PA, h1T, 2)
        raw = m.take("se_raw", [P, 2, KD, P])
        wq = [m.take(f"se_w{j}", [P, 2, KD, P], F32R) for j in range(2)]
        sub = m.take("se_sub", [P, 2, KEYS])
        qt = m.take("se_qt", [P, 2, T])
        sv = m.take("se_sv", [P, 2 * TT, K])
        si = m.take("se_si", [P, 2 * TT, K], U32)
        sf = m.take("se_sf", [P, 2 * TT, K])
        cv = m.take("se_cv", [P, TT, K])
        ci = m.take("se_ci", [P, TT, K], U32)
        cab = m.take("se_cab", [P, 2, TT, K], U32)
        cf = m.take("se_cf", [P, 2, TT, K])
        iota = m.take("se_iota", [P, K])
        gs = m.take("se_gs", [P, 2, TT])
        pick = m.take("se_pick", [P, 3, TT, K])
        pick_all = m.take("se_pick_all", [P, 3 * TT, HEADS, K])
        s = m.take("se_s", [P, 2 * TT, KEYS])
        cand_mem, left_mem = m.take("se_cand", [P, TT * K * K]), m.take("se_left", [P, 2 * TT * KEYS])
        cand = cand_mem[:, :].rearrange("p (t c) -> p t c", t=TT)
        eq = cand_mem[:, :].rearrange("p (x a) -> p x a", a=K)
        s_left = left_mem[:, :].rearrange("p (x n) -> p x n", n=KEYS)
        cand_left = left_mem[:, :].rearrange("p (t c) -> p t c", t=TT)
        par_in = sem("se_par")
        w_in = [sem("se_w_in0"), sem("se_w_in1")]
        wh, wl = sem("se_wh"), sem("se_wl")
        q_done, q_ev, s_done, s_ev = (sem("se_" + x) for x in ("q_done", "q_ev", "s_done", "s_ev"))
        chain = sem("se_chain")
        ex, exd = sem("se_ex"), sem("se_exd")
        picked, kept = sem("se_picked"), sem("se_kept")
        tr, tr_ev = sem("se_tr"), sem("se_tr_ev")
        with nc.Block() as block:
            @block.sync
            def _(sp):
                def load(x, u):
                    sp.dma_start(raw[:, u, :, :], A["w_query"][ds(x, 1)].rearrange("o p k c -> (o p) k c")
                                 ).then_inc(w_in[u], 16)
                    sp.dma_start(sub[:, u, :], A["subkeys"][ds(x, 1)].rearrange("o p c -> (o p) c")
                                 ).then_inc(w_in[u], 16)

                sp.dma_start(iota[:, :], A["iota"][:, 0:K]).then_inc(par_in, 16)
                load(0, 0)
                load(1, 1)
                with sp.Fori(0, HEADS - 1) as h:
                    for u in range(2):
                        ahead.load(sp, A, 0, h * 2 + u, u)
                    for u in range(2):
                        sp.wait_ge(wl, h * 2 + u + 1)
                        sp.wait_ge(s_done, h * 2 + u + 1)
                        load(h * 2 + 2 + u, u)
                for u in range(2):
                    ahead.load(sp, A, 0, (HEADS - 1) * 2 + u, u)

            @block.gpsimd
            def _(pool):
                with pool.Fori(0, HEADS) as h:
                    for u in range(2):
                        ahead.store(pool, a_dram, 0, h * 2 + u, u)
                for q in ahead.stored:
                    pool.wait_ge(q, 16 * HEADS)

            @block.tensor
            def _(pe):
                def queries(x, u):
                    pe.wait_ge(wl, x + 1)
                    pe.wait_ge(q_ev, x)
                    for f in range(2):
                        ins = matmul3(nc, Q[:, f, :], [lambda k, w=w: w[:, u, k, :] for w in wq],
                                      [lambda k, y=y: y[:, k, f * BANK:f * BANK + BANK] for y in h1T], KD)
                    ins.then_inc(q_done, 1)

                def score(x, u):
                    pe.wait_ge(q_ev, x + 1)
                    pe.wait_ge(s_ev, x)
                    for t in range(TT):
                        ins = nc.tensor.matmul(S[:, t, :], qt[:, u, t * P:t * P + P], sub[:, u, :], start=True,
                                               stop=True)
                    ins.then_inc(s_done, 1)

                half = 2 * KD
                queries(0, 0)
                queries(1, 1)
                score(0, 0)
                score(1, 1)
                with pe.Fori(0, HEADS - 1) as h:
                    ahead.up(pe, h * 2, 0)
                    queries(h * 2 + 2, 0)
                    ahead.up(pe, h * 2 + 1, 1, 0, half)
                    score(h * 2 + 2, 0)
                    queries(h * 2 + 3, 1)
                    ahead.up(pe, h * 2 + 1, 1, half, 2 * half)
                    score(h * 2 + 3, 1)
                for u in range(2):
                    ahead.up(pe, (HEADS - 1) * 2 + u, u)
                pe.wait_ge(kept, HEADS)
                for t in range(TT):
                    if t >= 2:
                        pe.wait_ge(tr_ev, t - 1)
                    for j in range(3):
                        ins = nc.tensor.transpose(Q[:, t % 2, j * P:j * P + P],
                                                  pick_all[:, j * TT + t, :, :].rearrange("p h k -> p (h k)"),
                                                  identity[:, :])
                    ins.then_inc(tr, 1)

            @block.scalar
            def _(act):
                def high(h, u):
                    act.wait_ge(w_in[u], h * 32 + 32)
                    nc.scalar.activation(wq[0][:, u, :, :], raw[:, u, :, :], ACT.Copy).then_inc(wh, 1)

                def query_out(x, u):
                    act.wait_ge(q_done, x + 1)
                    nc.scalar.activation(qt[:, u, :], Q[:, :, :].rearrange("p f c -> p (f c)"),
                                         ACT.Copy).then_inc(q_ev, 1)

                def score_out(x, u):
                    act.wait_ge(s_done, x + 1)
                    nc.scalar.activation(s[:, u * TT:u * TT + TT, :], S[:, :, :], ACT.Copy).then_inc(s_ev, 1)

                def exps(h):
                    act.wait_ge(ex, h + 1)
                    nc.scalar.activation(pick[:, 2, :, :], pick[:, 2, :, :], ACT.Exp).then_inc(exd, 1)

                def keep(h):
                    act.wait_ge(picked, h + 1)
                    act.nop(nofuse=True)
                    nc.scalar.activation(pick_all[:, :, ds(h, 1), :].rearrange("p j o k -> p j (o k)"),
                                         pick[:, :, :, :].rearrange("p j t k -> p (j t) k"),
                                         ACT.Copy).then_inc(kept, 1)

                for u in range(2):
                    high(0, u)
                ahead.high(act, 0, 0, 0)
                for u in range(2):
                    query_out(u, u)
                for u in range(2):
                    score_out(u, u)
                with act.Fori(0, HEADS - 1) as h:
                    for u in range(2):
                        act.wait_ge(q_done, h * 2 + u + 1)
                        high(h + 1, u)
                    ahead.high(act, h * 2 + 1, 1, h)
                    for j in range(E2):
                        ahead.gelu(act, h * 2, 0, h, j)
                    act.wait_ge(s_done, h * 2 + 1)
                    query_out(h * 2 + 2, 0)
                    ahead.high(act, h * 2 + 2, 0, h + 1)
                    ahead.gelu(act, h * 2 + 1, 1, h, 0)
                    act.wait_ge(chain, h * PER + SEARCHED)
                    score_out(h * 2 + 2, 0)
                    act.wait_ge(s_done, h * 2 + 2)
                    query_out(h * 2 + 3, 1)
                    exps(h)
                    ahead.gelu(act, h * 2 + 1, 1, h, 1)
                    score_out(h * 2 + 3, 1)
                    keep(h)
                ahead.high(act, (HEADS - 1) * 2 + 1, 1, HEADS - 1)
                for j in range(E2):
                    ahead.gelu(act, (HEADS - 1) * 2, 0, HEADS - 1, j)
                exps(HEADS - 1)
                for j in range(E2):
                    ahead.gelu(act, (HEADS - 1) * 2 + 1, 1, HEADS - 1, j)
                keep(HEADS - 1)
                for t in range(TT):
                    act.wait_ge(tr, t + 1)
                    nc.scalar.activation(picks[:, :, t * P:t * P + P],
                                         Q[:, t % 2, 0:3 * P].rearrange("p (j c) -> p j c", j=3),
                                         ACT.Copy).then_inc(tr_ev, 1)

            @block.vector
            def _(dve):
                def low(x, u):
                    dve.wait_ge(wh, x + 1)
                    nc.vector.tensor_tensor(wq[1][:, u, :, :], raw[:, u, :, :], wq[0][:, u, :, :].bitcast(F32),
                                            ALU.subtract).then_inc(wl, 1)

                def search_head(h, c, last):
                    def top16(vals, idx, src, left, n):
                        for x in range(n):
                            ins = nc.vector.max(vals[:, x, 0:8], src[:, x, :])
                        c.then(ins, apart=True)
                        for x in range(n):
                            nc.vector.max_index(idx[:, x, 0:8], vals[:, x, 0:8], src[:, x, :])
                            ins = nc.vector.match_replace(left[:, x, :], vals[:, x, 0:8], src[:, x, :], LOWEST)
                        c.then(ins, apart=True)
                        for x in range(n):
                            ins = nc.vector.max(vals[:, x, 8:16], left[:, x, :])
                        c.then(ins, apart=True)
                        for x in range(n):
                            ins = nc.vector.max_index(idx[:, x, 8:16], vals[:, x, 8:16], left[:, x, :])
                        c.then(ins, apart=True)

                    dve.wait_ge(s_ev, h * 2 + 2)
                    dve.nop(nofuse=True)
                    if not last:
                        for u in range(2):
                            low(h * 2 + 2 + u, u)
                    ahead.low(dve, h * 2 + 1, 1)
                    dve.nop(nofuse=True)
                    top16(sv, si, s, s_left, 2 * TT)
                    c.then(nc.vector.tensor_copy(sf[:, :, :], si[:, :, :]))
                    c.then(nc.vector.tensor_tensor(cand.rearrange("p t (a b) -> p t a b", a=K),
                                                   sv[:, 0:TT, :].unsqueeze(3).to_broadcast([P, TT, K, K]),
                                                   sv[:, TT:2 * TT, :].unsqueeze(2).to_broadcast([P, TT, K, K]),
                                                   ALU.add), apart=True)
                    if not last:
                        ahead.low(dve, h * 2 + 2, 0)
                        dve.nop(nofuse=True)
                    top16(cv, ci, cand, cand_left, TT)
                    dve.wait_ge(kept, h)
                    nc.vector.tensor_tensor(pick[:, 2, :, :], cv[:, :, :],
                                            cv[:, :, 0:1].to_broadcast([P, TT, K]), ALU.subtract).then_inc(ex, 1)
                    nc.vector.tensor_scalar(cab[:, 0, :, :], ci[:, :, :], 4, None, ALU.logical_shift_right)
                    c.then(nc.vector.tensor_scalar(cab[:, 1, :, :], ci[:, :, :], K - 1, None, ALU.bitwise_and))
                    c.then(nc.vector.tensor_copy(cf[:, :, :, :], cab[:, :, :, :]))
                    e4 = eq.rearrange("p (t k) a -> p t k a", t=TT)
                    for j in range(2):
                        c.then(nc.vector.tensor_tensor(
                            eq, cf[:, j, :, :].rearrange("p t k -> p (t k)").unsqueeze(2)
                            .to_broadcast([P, TT * K, K]),
                            iota[:, :].unsqueeze(1).to_broadcast([P, TT * K, K]), ALU.is_equal))
                        c.then(nc.vector.tensor_tensor(e4, e4, sf[:, j * TT:j * TT + TT, :].unsqueeze(2)
                                                       .to_broadcast([P, TT, K, K]), ALU.mult))
                        c.then(nc.vector.tensor_reduce(pick[:, j, :, :].rearrange("p t k -> p (t k)"), eq,
                                                       AX.X, ALU.add))
                    dve.wait_ge(exd, h + 1)
                    c.then(nc.vector.tensor_reduce(gs[:, 0, :], pick[:, 2, :, :], AX.X, ALU.add))
                    c.then(nc.vector.reciprocal(gs[:, 1, :], gs[:, 0, :]))
                    nc.vector.tensor_tensor(pick[:, 2, :, :], pick[:, 2, :, :],
                                            gs[:, 1, :].unsqueeze(2).to_broadcast([P, TT, K]),
                                            ALU.mult).then_inc(picked, 1)
                    assert c.n == PER, c.n

                ahead.credits(dve)
                dve.wait_ge(par_in, 16)
                for u in range(2):
                    low(u, u)
                ahead.low(dve, 0, 0)
                with dve.Fori(0, HEADS - 1) as h:
                    search_head(h, Chain(dve, chain, h * PER), False)
                search_head(HEADS - 1, Chain(dve, chain, (HEADS - 1) * PER), True)


def gates(nc, sem, A, h1T, picks, g_dram, a_dram, at):
    QUADS = GT // 4
    UP = E2 * 2 * KD // QUADS
    m = Map(nc, at)
    with nc.psum_tensor("gt_a", [P, E2, T], F32) as PA, nc.psum_tensor("gt_ps", [P, 4, BANK], F32) as PS:
        ahead = Ahead(nc, sem, "gt", m, PA, h1T, 1)
        hot1 = m.take("gt_hot1", [P, 2, 4, KEYS])
        hot2 = m.take("gt_hot2", [P, 2, 4, KEYS])
        stage = [m.take(f"gt_stage{j}", [P, KEYS, GT]) for j in range(2)]
        iota = m.take("gt_iota", [P, KEYS])
        part = m.take("gt_part", [P, 3, GT])
        par_in, chain = sem("gt_par"), sem("gt_chain")
        hot_ready = sem("gt_hot")
        mm_done = sem("gt_mm")
        ev_done = sem("gt_ev")
        g_out = [sem("gt_out0"), sem("gt_out1")]
        with nc.Block() as block:
            @block.sync
            def _(sp):
                sp.dma_start(iota[:, :], A["iota"]).then_inc(par_in, 16)
                with sp.Fori(0, GROUPS // 2) as i:
                    for u in range(2):
                        ahead.load(sp, A, 2 * HEADS, i * 2 + u, u)
                ahead.load(sp, A, 2 * HEADS, GROUPS, 0)

            @block.gpsimd
            def _(pool):
                with pool.Fori(0, GROUPS // 2) as i:
                    for u in range(2):
                        pool.wait_ge(ev_done, (i * 2 + u + 1) * QUADS + 3)
                        pool.nop(nofuse=True)
                        pool.dma_start(g_dram[:, ds(i * 2 + u, 1), :, :].rearrange("p o a t -> p (o a) t"),
                                       stage[u][:, :, :]).then_inc(g_out[u], 16)
                        ahead.store(pool, a_dram, 2 * HEADS, i * 2 + u, u)
                for u in range(2):
                    pool.wait_ge(g_out[u], 16 * GROUPS // 2)
                    pool.wait_ge(ahead.stored[u], 16 * GROUPS // 2)

            @block.vector
            def _(dve):
                dve.wait_ge(par_in, 16)
                ahead.credits(dve)
                nc.vector.memset(part[:, 0, :], 0.0).then_inc(mm_done, 1)
                dve.wait_ge(mm_done, 1)
                nc.vector.memset(part[:, 1, :], 0.0).then_inc(ev_done, 3)
                dve.wait_ge(ev_done, 3)
                ahead.low(dve, 0, 0)
                with dve.Fori(0, GROUPS // 2) as i:
                    for u in range(2):
                        g = i * 2 + u
                        dve.wait_ge(hot_ready, g * QUADS)
                        nc.vector.tensor_copy(part[:, :, :], picks[:, :, ds(g * GT, GT)]).then_inc(chain, 1)
                        dve.wait_ge(chain, g + 1)
                        for q in range(QUADS):
                            if q == 8:
                                ahead.low(dve, g + 1, 1 - u)
                            dve.wait_ge(mm_done, g * QUADS + q)
                            for x in range(4):
                                t = 4 * q + x
                                nc.vector.tensor_scalar(hot1[:, q % 2, x, :], iota[:, :], part[:, 0, t:t + 1], None,
                                                        ALU.is_equal)
                                ins = nc.vector.tensor_scalar(hot2[:, q % 2, x, :], iota[:, :], part[:, 1, t:t + 1],
                                                              part[:, 2, t:t + 1], ALU.is_equal, ALU.mult)
                            ins.then_inc(hot_ready, 1)

            @block.tensor
            def _(pe):
                with pe.Fori(0, GROUPS // 2) as i:
                    for u in range(2):
                        for q in range(QUADS):
                            x0 = (i * 2 + u) * QUADS + q
                            pe.wait_ge(hot_ready, x0 + 1)
                            pe.wait_ge(ev_done, x0)
                            for x in range(4):
                                ins = nc.tensor.matmul(PS[:, q % 4, x * P:x * P + P], hot2[:, q % 2, x, :],
                                                       hot1[:, q % 2, x, :], start=True, stop=True)
                            ins.then_inc(mm_done, 1)
                            ahead.up(pe, i * 2 + u, u, q * UP, q * UP + UP)

            @block.scalar
            def _(act):
                ahead.high(act, 0, 0, 0)
                with act.Fori(0, GROUPS // 2) as i:
                    for u in range(2):
                        g = i * 2 + u
                        act.wait_ge(g_out[u], i * 16)
                        for q in range(QUADS):
                            act.wait_ge(mm_done, g * QUADS + q + 2)
                            nc.scalar.activation(stage[u][:, :, 4 * q:4 * q + 4],
                                                 PS[:, q % 4, :].rearrange("p (t a) -> p a t", t=4),
                                                 ACT.Copy).then_inc(ev_done, 1)
                            if q == 4:
                                ahead.high(act, g + 1, 1 - u, i + u)
                            if q == 8:
                                ahead.gelu(act, g, u, i, 0)
                        ahead.gelu(act, g, u, i, 1)


def experts_ahead(nc, sem, A, acc, g_dram, a_dram, acc_dram, at):
    m = Map(nc, at)
    v_raw = m.take("ea_v_raw", [P, E2, D])
    v = [m.take(f"ea_v{j}", [P, 2, E2, D], F32R) for j in range(2)]
    gate = m.take("ea_gate", [P, 2, GROUPS, E2, GT])
    coef = m.take("ea_coef", [P, 2, E2, T])
    c = [m.take(f"ea_c{j}", [P, 2, E2, T], F32R) for j in range(2)]
    with nc.psum_tensor("ea_f", [P, 4, D], F32) as PF:
        acc_in = [sem(f"ea_acc_in{t}") for t in range(TT)]
        v_in = sem("ea_v_in")
        g_in = [sem("ea_g_in0"), sem("ea_g_in1")]
        a_in = [sem("ea_a_in0"), sem("ea_a_in1")]
        vh, vl, gated, ch, cl = (sem("ea_" + x) for x in ("vh", "vl", "gated", "ch", "cl"))
        down = sem("ea_down")
        added = sem("ea_added")
        with nc.Block() as block:
            @block.sync
            def _(sp):
                with sp.Fori(0, AHEAD // 2) as i:
                    for u in range(2):
                        s = i * 2 + u
                        sp.wait_ge(vl, s)
                        sp.dma_start(v_raw[:, :, :], A["v"][ds(s, 1)].rearrange("o j p d -> p (o j) d")
                                     ).then_inc(v_in, 16)
                        sp.wait_ge(cl, s)
                        sp.dma_start(coef[:, u, :, :], a_dram[ds(s, 1)].rearrange("o p j t -> (o p) j t")
                                     ).then_inc(a_in[u], 16)
                        sp.dma_start(gate[:, u, :, :, :].rearrange("p g j t -> p g (j t)"),
                                     g_dram[:, :, ds(s * E2, E2), :].rearrange("p g j t -> p g (j t)")
                                     ).then_inc(g_in[u], 16)

            @block.gpsimd
            def _(pool):
                pool.wait_ge(g_in[0], 16)
                for t in range(TT):
                    pool.dma_start(acc[:, t, :], acc_dram[t]).then_inc(acc_in[t], 16)

            @block.tensor
            def _(pe):
                with pe.Fori(0, AHEAD // 2) as i:
                    for u in range(2):
                        s = i * 2 + u
                        pe.wait_ge(cl, s + 2)
                        pe.wait_ge(vl, s + 1)
                        for t in range(TT):
                            pe.wait_ge(added, s * TT + t)
                            for f in range(2):
                                ins = matmul3(nc, PF[:, t % 4, f * BANK:f * BANK + BANK],
                                              [lambda j, x=x: x[:, u, j, t * P:t * P + P] for x in c],
                                              [lambda j, x=x: x[:, u, j, f * BANK:f * BANK + BANK] for x in v], E2)
                            ins.then_inc(down, 1)

            @block.scalar
            def _(act):
                with act.Fori(0, AHEAD // 2) as i:
                    for u in range(2):
                        s = i * 2 + u
                        act.wait_ge(v_in, s * 16 + 16)
                        act.wait_ge(down, s * TT)
                        nc.scalar.activation(v[0][:, u, :, :], v_raw[:, :, :], ACT.Copy).then_inc(vh, 1)
                        act.wait_ge(gated, s + 1)
                        nc.scalar.activation(c[0][:, u, :, :], coef[:, u, :, :], ACT.Copy).then_inc(ch, 1)

            @block.vector
            def _(dve):
                for q, n in ((cl, 1), (down, TT), (added, 3)):
                    nc.vector.memset(c[1][:, 0, 0, 0:8].bitcast(F32), 0.0).then_inc(q, n)
                    dve.wait_ge(q, n)

                def prepare(s, u, i, x):
                    if x == 0:
                        dve.wait_ge(g_in[u], i * 16 + 16)
                        dve.wait_ge(a_in[u], i * 16 + 16)
                        c4 = coef[:, u, :, :].rearrange("p j (g t) -> p j g t", t=GT)
                        nc.vector.tensor_tensor(c4, c4, gate[:, u, :, :, :].rearrange("p g j t -> p j g t"),
                                                ALU.mult).then_inc(gated, 1)
                    elif x == 1:
                        dve.wait_ge(vh, s + 1)
                        nc.vector.tensor_tensor(v[1][:, u, :, :], v_raw[:, :, :], v[0][:, u, :, :].bitcast(F32),
                                                ALU.subtract).then_inc(vl, 1)
                    else:
                        dve.wait_ge(ch, s + 1)
                        nc.vector.tensor_tensor(c[1][:, u, :, :], coef[:, u, :, :], c[0][:, u, :, :].bitcast(F32),
                                                ALU.subtract).then_inc(cl, 1)

                def add(s, t):
                    dve.wait_ge(acc_in[t], 16)
                    dve.wait_ge(down, s * TT + t + 1 + TT)
                    nc.vector.tensor_tensor(acc[:, t, :], acc[:, t, :], PF[:, t % 4, :], ALU.add).then_inc(added, 1)

                def step(s, u, i):
                    for x in range(3):
                        prepare(s, u, i, x)
                        add(s - 1, 2 * x)
                        add(s - 1, 2 * x + 1)
                    add(s - 1, TT - 2)
                    add(s - 1, TT - 1)

                for x in (1, 0, 2):
                    prepare(0, 0, 0, x)
                with dve.Fori(0, AHEAD // 2 - 1) as i:
                    step(i * 2 + 1, 1, i)
                    step(i * 2 + 2, 0, i + 1)
                step(AHEAD - 1, 1, AHEAD // 2 - 1)
                for t in range(TT):
                    add(AHEAD - 1, t)


def experts(nc, sem, A, h1T, acc, g_dram, at):
    STEPS = KEYS // E2 - AHEAD
    m = Map(nc, at)
    u_raw = m.take("ex_u_raw", [P, 2, KD, E2 * P])
    v_raw = m.take("ex_v_raw", [P, 2, E2, D])
    u_hi = m.take("ex_u_hi", [P, KD, E2 * P], F32R)
    u_lo = m.take("ex_u_lo", [P, KD, E2 * P], F32R)
    v_hi = m.take("ex_v_hi", [P, E2, D], F32R)
    v_lo = m.take("ex_v_lo", [P, E2, D], F32R)
    gate = m.take("ex_gate", [P, 2, GROUPS, E2, GT])
    c_hi = m.take("ex_c_hi", [P, E2, T], F32R)
    c_lo = m.take("ex_c_lo", [P, E2, T], F32R)
    coef = m.take("ex_coef", [P, E2, T])
    with nc.psum_tensor("ex_a", [P, E2, T], F32) as PA, nc.psum_tensor("ex_f", [P, 2, D], F32) as PF:
        u_in = [sem("ex_u_in0"), sem("ex_u_in1")]
        v_in = [sem("ex_v_in0"), sem("ex_v_in1")]
        g_in = [sem("ex_g_in0"), sem("ex_g_in1")]
        uh, ul = sem("ex_uh"), sem("ex_ul")
        vh, vl = sem("ex_vh"), sem("ex_vl")
        up = sem("ex_up")
        ge = sem("ex_ge")
        gated = sem("ex_gated")
        ch, cl = sem("ex_ch"), sem("ex_cl")
        down = sem("ex_down")
        added = sem("ex_added")
        with nc.Block() as block:
            @block.sync
            def _(sp):
                with sp.Fori(0, STEPS // 2) as i:
                    for u in range(2):
                        s = i * 2 + u
                        sp.wait_ge(ul, s)
                        sp.dma_start(u_raw[:, u, :, :], A["u_t"][ds(s + AHEAD, 1)].rearrange("o p k e -> (o p) k e")
                                     ).then_inc(u_in[u], 16)
                        sp.wait_ge(gated, s)
                        sp.dma_start(gate[:, u, :, :, :].rearrange("p g j t -> p g (j t)"),
                                     g_dram[:, :, ds((s + AHEAD) * E2, E2), :].rearrange("p g j t -> p g (j t)")
                                     ).then_inc(g_in[u], 16)
                        sp.wait_ge(vl, s)
                        sp.dma_start(v_raw[:, u, :, :], A["v"][ds(s + AHEAD, 1)].rearrange("o j p d -> p (o j) d")
                                     ).then_inc(v_in[u], 16)

            @block.tensor
            def _(pe):
                def upward(s, first=False):
                    pe.wait_ge(ul, s + 2)
                    for j in range(E2):
                        if not first:
                            pe.wait_ge(ge, (s - 1) * E2 + j + 1)
                        for f in range(2):
                            ins = matmul3(nc, PA[:, j, f * BANK:f * BANK + BANK],
                                          [lambda k, x=x: x[:, k, j * P:j * P + P] for x in (u_hi, u_lo)],
                                          [lambda k, x=x: x[:, k, f * BANK:f * BANK + BANK] for x in h1T], KD)
                        ins.then_inc(up, 1)

                def downward(s):
                    pe.wait_ge(cl, s + 1)
                    pe.wait_ge(vl, s + 2)
                    for t in range(TT):
                        pe.wait_ge(added, s * TT + t)
                        for f in range(2):
                            ins = matmul3(nc, PF[:, t % 2, f * BANK:f * BANK + BANK],
                                          [lambda j, x=x: x[:, j, t * P:t * P + P] for x in (c_hi, c_lo)],
                                          [lambda j, x=x: x[:, j, f * BANK:f * BANK + BANK] for x in (v_hi, v_lo)],
                                          E2)
                        ins.then_inc(down, 1)

                upward(0, first=True)
                with pe.Fori(0, STEPS - 1) as i:
                    upward(i + 1)
                    downward(i)
                downward(STEPS - 1)

            @block.scalar
            def _(act):
                def split_u(s, u, i):
                    act.wait_ge(u_in[u], i * 16 + 16)
                    act.wait_ge(up, s * E2)
                    nc.scalar.activation(u_hi[:, :, :], u_raw[:, u, :, :], ACT.Copy).then_inc(uh, 1)

                def rest(s, u, i):
                    act.wait_ge(cl, s)
                    for j in range(E2):
                        act.wait_ge(up, s * E2 + j + 1)
                        nc.scalar.activation(coef[:, j, :], PA[:, j, :], ACT.Gelu).then_inc(ge, 1)
                    act.wait_ge(down, s * TT)
                    act.wait_ge(v_in[u], i * 16 + 16)
                    nc.scalar.activation(v_hi[:, :, :], v_raw[:, u, :, :], ACT.Copy).then_inc(vh, 1)
                    act.wait_ge(gated, s + 2)
                    nc.scalar.activation(c_hi[:, :, :], coef[:, :, :], ACT.Copy).then_inc(ch, 1)

                split_u(0, 0, 0)
                with act.Fori(0, STEPS // 2 - 1) as i:
                    split_u(i * 2 + 1, 1, i)
                    rest(i * 2, 0, i)
                    split_u(i * 2 + 2, 0, i + 1)
                    rest(i * 2 + 1, 1, i)
                split_u(STEPS - 1, 1, STEPS // 2 - 1)
                rest(STEPS - 2, 0, STEPS // 2 - 1)
                rest(STEPS - 1, 1, STEPS // 2 - 1)

            @block.vector
            def _(dve):
                for x, q in enumerate((ul, vl, gated, added)):
                    nc.vector.memset(coef[:, x % 2, 0:8], 0.0).then_inc(q, 1)
                    dve.wait_ge(q, 1)

                def split_u(s, u):
                    dve.wait_ge(uh, s + 1)
                    nc.vector.tensor_tensor(u_lo[:, :, :], u_raw[:, u, :, :], u_hi[:, :, :].bitcast(F32),
                                            ALU.subtract).then_inc(ul, 1)

                def add(s):
                    for t in range(TT):
                        dve.wait_ge(down, s * TT + t + 1)
                        nc.vector.tensor_tensor(acc[:, t, :], acc[:, t, :], PF[:, t % 2, :], ALU.add).then_inc(added, 1)

                def rest(s, u, i):
                    dve.wait_ge(ge, s * E2 + E2)
                    dve.wait_ge(g_in[u], i * 16 + 16)
                    c4 = coef[:, :, :].rearrange("p j (g t) -> p j g t", t=GT)
                    nc.vector.tensor_tensor(c4, c4, gate[:, u, :, :, :].rearrange("p g j t -> p j g t"),
                                            ALU.mult).then_inc(gated, 1)
                    dve.wait_ge(vh, s + 1)
                    nc.vector.tensor_tensor(v_lo[:, :, :], v_raw[:, u, :, :], v_hi[:, :, :].bitcast(F32),
                                            ALU.subtract).then_inc(vl, 1)
                    dve.wait_ge(ch, s + 1)
                    nc.vector.tensor_tensor(c_lo[:, :, :], coef[:, :, :], c_hi[:, :, :].bitcast(F32),
                                            ALU.subtract).then_inc(cl, 1)

                split_u(0, 0)
                split_u(1, 1)
                rest(0, 0, 0)
                with dve.Fori(0, STEPS // 2 - 1) as i:
                    split_u(i * 2 + 2, 0)
                    add(i * 2)
                    rest(i * 2 + 1, 1, i)
                    split_u(i * 2 + 3, 1)
                    add(i * 2 + 1)
                    rest(i * 2 + 2, 0, i + 1)
                add(STEPS - 2)
                rest(STEPS - 1, 1, STEPS // 2 - 1)
                add(STEPS - 1)


def norm_out(nc, sem, A, acc, out, at):
    m = Map(nc, at)
    gamma = m.take("no_gamma", [P, D])
    beta = m.take("no_beta", [P, D])
    stats = m.take("no_stats", [P, 2, 2, 6])
    mv = m.take("no_mv", [P, 2, 4])
    par_in, chain = sem("no_par"), sem("no_chain")
    root, rooted, ready = sem("no_root"), sem("no_rooted"), sem("no_ready")
    y_out = sem("no_out")
    with nc.Block() as block:
        @block.sync
        def _(sp):
            sp.dma_start(gamma[:, :], row(A["ln2_g"])).then_inc(par_in, 16)
            sp.dma_start(beta[:, :], row(A["ln2_b"])).then_inc(par_in, 16)
            o = out.rearrange("b (t p) d -> (b t) p d", p=P)
            for t in range(TT):
                sp.wait_ge(ready, t + 1)
                sp.dma_start(o[t], acc[:, t, :]).then_inc(y_out, 16)
            sp.wait_ge(y_out, 16 * TT)

        @block.vector
        def _(dve):
            c = Chain(dve, chain)

            def statistics(t):
                u = t % 2
                nc.vector.bn_stats(stats[:, u, 0, :], acc[:, t, 0:BANK])
                c.then(nc.vector.bn_stats(stats[:, u, 1, :], acc[:, t, BANK:D]))
                c.then(nc.vector.bn_aggr(mv[:, u, 0:2], stats[:, u, :, :].rearrange("p a b -> p (a b)")))
                nc.vector.tensor_scalar(mv[:, u, 2:3], mv[:, u, 1:2], LN_EPS, None, ALU.add).then_inc(root, 1)

            statistics(0)
            dve.wait_ge(par_in, 32)
            for t in range(TT):
                if t + 1 < TT:
                    statistics(t + 1)
                u, x = t % 2, acc[:, t, :]
                dve.wait_ge(rooted, t + 1)
                c.then(nc.vector.reciprocal(mv[:, u, 3:4], mv[:, u, 3:4]))
                c.then(nc.vector.tensor_scalar(x, x, mv[:, u, 0:1], mv[:, u, 3:4], ALU.subtract, ALU.mult))
                c.then(nc.vector.tensor_tensor(x, x, gamma[:, :], ALU.mult))
                nc.vector.tensor_tensor(x, x, beta[:, :], ALU.add).then_inc(ready, 1)

        @block.scalar
        def _(act):
            for t in range(TT):
                act.wait_ge(root, t + 1)
                nc.scalar.activation(mv[:, t % 2, 3:4], mv[:, t % 2, 2:3], ACT.Sqrt).then_inc(rooted, 1)


def encoder_block(nc, A, out):
    def sem(name):
        return nc.alloc_semaphore(name=name)

    def dram(name, shape):
        return nc.dram_tensor(name, shape, F32, kind="Internal").ap()

    h_dram = dram("h_dram", [TT, P, D])
    y_dram = dram("y_dram", [HEADS, P, T])
    o_dram = dram("o_dram", [HEADS, P, TT, P])
    th_dram = dram("th_dram", [TT, P, 2, T])
    m_dram = dram("m_dram", [KD, P, T])
    acc_dram = dram("acc_dram", [TT, P, D])
    a_dram = dram("a_dram", [AHEAD, P, E2, T])
    g_dram = dram("g_dram", [P, GROUPS, KEYS, GT])
    W = KD * T * 4
    WL = KD * L * 4
    ident_at, top = 16512, 229344
    at = ident_at + P * 4
    identity = Map(nc, ident_at).take("identity", [P, P])
    hT = [Map(nc, at + j * WL).take(f"hT{j}", [P, KD, L], F32R) for j in range(2)]
    a1 = at + 2 * WL
    both = Map(nc, a1).take("both", [P, 2, HEADS, T])
    both_hi = Map(nc, at).take("both_hi", [P, 2, HEADS, T], F32R)
    both_lo = Map(nc, a1).take("both_lo", [P, 2, HEADS, T], F32R)
    h1T = [Map(nc, at + j * W).take(f"h1T{j}", [P, KD, T], F32R) for j in range(2)]
    a2 = at + 2 * W
    acc = Map(nc, a2).take("acc", [P, TT, D])
    picks = Map(nc, top - 3 * T * 4).take("picks", [P, 3, T])

    with nc.cleanup_on_exit():
        norm_in(nc, sem, A, hT, h_dram, identity, a1)
        mix(nc, sem, A, hT, identity, o_dram, y_dram, a1)
    with nc.cleanup_on_exit():
        branch(nc, sem, A, identity, hT, o_dram, y_dram, th_dram, both[:, 1, :, :], both[:, 0, :, :], a1 + 2 * W)
        merge(nc, sem, A, both, both_hi, both_lo, th_dram, m_dram, a1 + 2 * W)
        project(nc, sem, A, m_dram, identity, h_dram, h1T, acc_dram, a2)
    with nc.cleanup_on_exit():
        search(nc, sem, A, h1T, a_dram, identity, picks, a2)
        gates(nc, sem, A, h1T, picks, g_dram, a_dram, a2)
    with nc.cleanup_on_exit():
        experts_ahead(nc, sem, A, acc, g_dram, a_dram, acc_dram, a2 + W)
        experts(nc, sem, A, h1T, acc, g_dram, a2 + W)
        norm_out(nc, sem, A, acc, out, a2 + W)


def _layout(inputs):
    import numpy as np

    def f(name):
        a = np.asarray(inputs[name])
        return a if name in ("x", "meta", "ln_in_g", "ln_in_b") else a[0]

    def tiles(w, parts):
        n = w.shape[1] // (parts * P)
        return w.reshape(w.shape[0] // P, P, parts, n, P).transpose(3, 1, 0, 2, 4).reshape(n, P, w.shape[0] // P,
                                                                                          parts * P)

    def col(v):
        return v.reshape(-1, P).T

    w, b = f("w_in"), f("b_in")
    q3, c2 = 3 * HEADS * P, 3 * HEADS * P + 2 * D
    pos = np.arange(L, dtype=np.float32)
    inv = np.float32(500000.0) ** (-np.arange(0, 2 * ROT, 2, dtype=np.float32) / np.float32(2 * ROT))
    ang = (pos[:, None] * inv[None, :]).astype(np.float32)
    order = np.concatenate([np.arange(M, L), np.arange(M), np.zeros(P - M, np.int64)])

    def rope(fn):
        return fn(ang).astype(np.float32)[order].reshape(TT + 1, P, ROT).transpose(1, 0, 2)

    return {
        "x": f("x"), "meta": f("meta"), "ln_in_g": f("ln_in_g"), "ln_in_b": f("ln_in_b"),
        "w_qkv": tiles(w[:, :q3], 3), "w_glu": tiles(w[:, q3:c2], 2), "w_gate": tiles(w[:, c2:], 2),
        "b_qkv": b[:q3].reshape(3, HEADS, P).transpose(1, 0, 2).reshape(HEADS, 3 * P),
        "chan": np.stack([col(v) for v in (b[q3:q3 + D], b[q3 + D:c2], b[c2:c2 + D], b[c2 + D:], f("dw_bias"),
                                           f("conv_ln_g"), f("conv_ln_b"), f("b_conv_proj"))], axis=1),
        "taps": f("dw_kernel").reshape(TAPS, HEADS, P).transpose(2, 1, 0),
        "lambda_q1": f("lambda_q1"), "lambda_k1": f("lambda_k1"), "lambda_q2": f("lambda_q2"),
        "lambda_k2": f("lambda_k2"), "subln_col": f("subln_g").reshape(P, 1),
        "w_attn": tiles(f("w_attn_proj"), 1), "w_conv": tiles(f("w_conv_proj"), 1),
        "w_out": f("w_out").reshape(KD, P, D).transpose(1, 0, 2),
        "b_out": f("b_out"), "ln1_g": f("ln1_g"), "ln1_b": f("ln1_b"), "ln2_g": f("ln2_g"), "ln2_b": f("ln2_b"),
        "w_query": f("peer_wq").reshape(KD, P, 2 * HEADS, P).transpose(2, 1, 0, 3),
        "subkeys": f("peer_subkeys").reshape(2 * HEADS, KEYS, P).transpose(0, 2, 1),
        "u_t": f("peer_u").reshape(STEPS, E2, KEYS, KD, P).transpose(0, 4, 3, 1, 2).reshape(STEPS, P, KD, E2 * P),
        "v": f("peer_v").reshape(STEPS, E2, P, D),
        "rope_cos": rope(np.cos), "rope_sin": rope(np.sin),
        "identity": np.eye(P, dtype=np.float32),
        "iota": np.broadcast_to(np.arange(KEYS, dtype=np.float32), (P, KEYS)),
    }


def kernel(**inputs):
    import numpy as np
    import concourse.bacc as bacc
    from concourse.bass_utils import run_bass_kernel_spmd

    nc = bacc.Bacc("TRN2", target_bir_lowering=False, num_devices=1)
    arrays, args = {}, {}
    for name, a in _layout(inputs).items():
        a = np.ascontiguousarray(a)
        arrays[f"in_{name}"] = a
        args[name] = nc.dram_tensor(f"in_{name}", a.shape, mybir.dt.from_np(a.dtype), kind="ExternalInput").ap()
    out = nc.dram_tensor("out", (1, T, D), F32, kind="ExternalOutput").ap()
    encoder_block(nc, args, out)
    r = run_bass_kernel_spmd(nc, [arrays], core_ids=[0])
    return r.results[0]["out"]
```
